# Optimizing a Trainium2 kernel written in Bass

```python
import math
import jax, jax.numpy as jnp
from jax import lax
import numpy as np

D_MODEL = 1024
BATCH = 1
SEQ = 256
DEPTH = 1

CHUNK = 64
Q_BLOCK = 128
DA_HEADS = 8
DA_HEAD_DIM = 64
SB_HEADS = 16
SB_HEAD_DIM = 64
DA_QK = DA_HEADS * DA_HEAD_DIM
DA_V = DA_HEADS * 2 * DA_HEAD_DIM
SB_W = SB_HEADS * SB_HEAD_DIM
IN_SIZES = (DA_QK, DA_QK, DA_QK, DA_QK, DA_V, SB_W, SB_W, SB_W, D_MODEL, D_MODEL)
IN_COLS = sum(IN_SIZES)
N_EXPERTS = 32
TOP_K = 4
D_EXPERT = D_MODEL
SWIGLU_LIMIT = 7.0
SWIGLU_ALPHA = 1.702
EXPERT_BLOCK = 256
EPS = 1e-6

kernel_name = "hybrid_diffattn_stickbreak_moe_adaln"

def rms_norm(x, g):
    x32 = x.astype(jnp.float32)
    y = x32 * lax.rsqrt(jnp.mean(x32 * x32, axis=-1, keepdims=True) + EPS)
    return (y * g.astype(jnp.float32)).astype(x.dtype)

def alibi_slopes(n_heads):
    return jnp.asarray([2.0 ** (-8.0 * (i + 1) / n_heads) for i in range(n_heads)], jnp.float32)

def to_qblocks(a):
    b, s, h, d = a.shape
    return a.reshape(b, s // Q_BLOCK, Q_BLOCK, h, d).transpose(1, 0, 3, 2, 4)

def from_qblocks(a):
    nb, b, h, qb, d = a.shape
    return a.transpose(1, 0, 3, 2, 4).reshape(b, nb * qb, h, d)

def differential_attention(q1, q2, k1, k2, v, lam):
    s_len = q1.shape[1]
    scale = 1.0 / math.sqrt(DA_HEAD_DIM)
    k1t = k1.astype(jnp.float32).transpose(0, 2, 1, 3)
    k2t = k2.astype(jnp.float32).transpose(0, 2, 1, 3)
    vt = v.astype(jnp.float32).transpose(0, 2, 1, 3)
    slopes = alibi_slopes(DA_HEADS)
    kpos = jnp.arange(s_len)

    def step(args):
        qa, qb, bi = args
        qpos = bi * Q_BLOCK + jnp.arange(Q_BLOCK)
        allowed = (kpos[None, :] // CHUNK) <= (qpos[:, None] // CHUNK)
        dist = jnp.abs(qpos[:, None] - kpos[None, :]).astype(jnp.float32)
        bias = -slopes[:, None, None] * dist[None]
        s1 = jnp.einsum('bhqd,bhkd->bhqk', qa, k1t) * scale + bias
        s2 = jnp.einsum('bhqd,bhkd->bhqk', qb, k2t) * scale + bias
        s1 = jnp.where(allowed, s1, -jnp.inf)
        s2 = jnp.where(allowed, s2, -jnp.inf)
        w = jax.nn.softmax(s1, axis=-1) - lam * jax.nn.softmax(s2, axis=-1)
        return jnp.einsum('bhqk,bhkd->bhqd', w, vt)

    nb = s_len // Q_BLOCK
    out = lax.map(step, (to_qblocks(q1.astype(jnp.float32)), to_qblocks(q2.astype(jnp.float32)),
                         jnp.arange(nb)))
    return from_qblocks(out)

def stick_breaking_attention(q, k, v):
    s_len = q.shape[1]
    scale = 1.0 / math.sqrt(SB_HEAD_DIM)
    kt = k.astype(jnp.float32).transpose(0, 2, 1, 3)
    vt = v.astype(jnp.float32).transpose(0, 2, 1, 3)
    kpos = jnp.arange(s_len)

    def step(args):
        qb, bi = args
        qpos = bi * Q_BLOCK + jnp.arange(Q_BLOCK)
        strict = kpos[None, :] < qpos[:, None]
        z = jnp.einsum('bhqd,bhkd->bhqk', qb, kt) * scale
        log1m = jnp.where(strict, -jax.nn.softplus(z), 0.0)
        suffix = lax.cumsum(log1m, axis=3, reverse=True) - log1m
        a = jnp.where(strict, jnp.exp(jax.nn.log_sigmoid(z) + suffix), 0.0)
        return jnp.einsum('bhqk,bhkd->bhqd', a, vt)

    nb = s_len // Q_BLOCK
    out = lax.map(step, (to_qblocks(q.astype(jnp.float32)), jnp.arange(nb)))
    return from_qblocks(out)

def token_mixer(h, layer, w_in, lam_q1, lam_k1, lam_q2, lam_k2, subln_g, w_pa, w_pb, w_o):
    b, s, _ = h.shape
    proj = h @ w_in
    offs = np.cumsum(IN_SIZES)[:-1].tolist()
    q1, q2, k1, k2, va, qs, ks, vs, ga, gb = jnp.split(proj, offs, axis=-1)
    hd = (b, s, DA_HEADS, DA_HEAD_DIM)
    lam_init = 0.8 - 0.6 * math.exp(-0.3 * layer)
    lam = (jnp.exp(jnp.sum(lam_q1.astype(jnp.float32) * lam_k1.astype(jnp.float32)))
           - jnp.exp(jnp.sum(lam_q2.astype(jnp.float32) * lam_k2.astype(jnp.float32))) + lam_init)
    oa = differential_attention(q1.reshape(hd), q2.reshape(hd), k1.reshape(hd), k2.reshape(hd),
                                va.reshape(b, s, DA_HEADS, 2 * DA_HEAD_DIM), lam)
    oa = rms_norm(oa, subln_g) * (1.0 - lam_init)
    oa = oa.reshape(b, s, DA_V).astype(h.dtype)
    sd = (b, s, SB_HEADS, SB_HEAD_DIM)
    ob = stick_breaking_attention(qs.reshape(sd), ks.reshape(sd), vs.reshape(sd))
    ob = ob.reshape(b, s, SB_W).astype(h.dtype)
    merged = jax.nn.sigmoid(ga) * (oa @ w_pa) + jax.nn.sigmoid(gb) * (ob @ w_pb)
    return merged @ w_o

def moe_ffn(h, router_w, router_b, w_gu, b_gu, w_down, b_down):
    b, s, d = h.shape
    n = b * s
    t = h.reshape(n, d)
    logits = (t @ router_w + router_b).astype(jnp.float32)
    top_val, top_idx = lax.top_k(logits, TOP_K)
    gates = jax.nn.softmax(top_val, axis=-1)
    m = n * TOP_K
    e = top_idx.reshape(m)
    tok = jnp.arange(m) // TOP_K
    wts = gates.reshape(m)
    order = jnp.argsort(e, stable=True)
    e_s = e[order]
    counts = jnp.bincount(e, length=N_EXPERTS)
    padded = ((counts + EXPERT_BLOCK - 1) // EXPERT_BLOCK) * EXPERT_BLOCK
    pad_end = jnp.cumsum(padded)
    pad_start = pad_end - padded
    grp_start = jnp.cumsum(counts) - counts
    dest = pad_start[e_s] + (jnp.arange(m) - grp_start[e_s])
    n_blocks = -(-m // EXPERT_BLOCK) + N_EXPERTS
    n_slots = n_blocks * EXPERT_BLOCK
    slot_tok = jnp.full((n_slots,), n, jnp.int32).at[dest].set(tok[order].astype(jnp.int32))
    slot_w = jnp.zeros((n_slots,), jnp.float32).at[dest].set(wts[order])
    blk_exp = jnp.minimum(jnp.searchsorted(pad_end, jnp.arange(n_blocks) * EXPERT_BLOCK, side='right'),
                          N_EXPERTS - 1)
    t_pad = jnp.concatenate([t, jnp.zeros((1, d), t.dtype)], axis=0)
    xb = t_pad[slot_tok].reshape(n_blocks, EXPERT_BLOCK, d)

    def expert_block(args):
        xe, eid = args
        gu = xe @ w_gu[eid] + b_gu[eid]
        g, u = jnp.split(gu, 2, axis=-1)
        g = jnp.minimum(g, SWIGLU_LIMIT)
        u = jnp.clip(u, -SWIGLU_LIMIT, SWIGLU_LIMIT)
        act = (u + 1.0) * (g * jax.nn.sigmoid(SWIGLU_ALPHA * g))
        return act @ w_down[eid] + b_down[eid]

    yb = lax.map(expert_block, (xb, blk_exp))
    y = (yb.reshape(n_slots, d).astype(jnp.float32) * slot_w[:, None]).astype(t.dtype)
    out = jax.ops.segment_sum(y, slot_tok, num_segments=n + 1)[:n]
    return out.reshape(b, s, d)

def setup_inputs(seed: int = 0) -> dict:
    key = jax.random.key(seed)
    ks = jax.random.split(key, 24)
    f32 = jnp.float32
    D, E, F = D_MODEL, N_EXPERTS, D_EXPERT
    nrm = lambda k, shape, s: jax.random.normal(k, shape, f32) * s
    return {
        "x": nrm(ks[0], (BATCH, SEQ, D), 1.0),
        "c": nrm(ks[1], (BATCH, D), 1.0),
        "w_ada": nrm(ks[2], (DEPTH, D, 6 * D), 0.5 * D ** -0.5),
        "b_ada": nrm(ks[3], (DEPTH, 6 * D), 0.02),
        "norm1_g": 1.0 + nrm(ks[4], (DEPTH, D), 0.02),
        "w_in": nrm(ks[5], (DEPTH, D, IN_COLS), D ** -0.5),
        "lam_q1": nrm(ks[6], (DEPTH, DA_HEAD_DIM), 0.1),
        "lam_k1": nrm(ks[7], (DEPTH, DA_HEAD_DIM), 0.1),
        "lam_q2": nrm(ks[8], (DEPTH, DA_HEAD_DIM), 0.1),
        "lam_k2": nrm(ks[9], (DEPTH, DA_HEAD_DIM), 0.1),
        "subln_g": 1.0 + nrm(ks[10], (DEPTH, 2 * DA_HEAD_DIM), 0.02),
        "w_pa": nrm(ks[11], (DEPTH, DA_V, D), DA_V ** -0.5),
        "w_pb": nrm(ks[12], (DEPTH, SB_W, D), SB_W ** -0.5),
        "w_o": nrm(ks[13], (DEPTH, D, D), D ** -0.5),
        "norm2_g": 1.0 + nrm(ks[14], (DEPTH, D), 0.02),
        "router_w": nrm(ks[15], (DEPTH, D, E), D ** -0.5),
        "router_b": nrm(ks[16], (DEPTH, E), 0.01),
        "w_gu": nrm(ks[17], (DEPTH, E, D, 2 * F), D ** -0.5),
        "b_gu": nrm(ks[18], (DEPTH, E, 2 * F), 0.02),
        "w_down": nrm(ks[19], (DEPTH, E, F, D), F ** -0.5),
        "b_down": nrm(ks[20], (DEPTH, E, D), 0.02),
        "final_g": 1.0 + nrm(ks[21], (D,), 0.02),
    }

def reference(x, c, w_ada, b_ada, norm1_g, w_in, lam_q1, lam_k1, lam_q2, lam_k2, subln_g,
              w_pa, w_pb, w_o, norm2_g, router_w, router_b, w_gu, b_gu, w_down, b_down, final_g):
    for l in range(DEPTH):
        mod = (c @ w_ada[l] + b_ada[l])[:, None, :]
        sh1, sc1, g1, sh2, sc2, g2 = jnp.split(mod, 6, axis=-1)
        h = rms_norm(x, norm1_g[l]) * (1.0 + sc1) + sh1
        x = x + g1 * token_mixer(h, l, w_in[l], lam_q1[l], lam_k1[l], lam_q2[l], lam_k2[l],
                                 subln_g[l], w_pa[l], w_pb[l], w_o[l])
        h = rms_norm(x, norm2_g[l]) * (1.0 + sc2) + sh2
        x = x + g2 * moe_ffn(h, router_w[l], router_b[l], w_gu[l], b_gu[l], w_down[l], b_down[l])
    return rms_norm(x, final_g)


_drawn_inputs = setup_inputs


def setup_inputs(seed=0):
    import zlib

    import numpy as np

    out = dict(_drawn_inputs(seed))
    spreads = {}
    factors = {'norm1_g': 3.512,
     'lam_q1': 4.032,
     'lam_k2': 8.0,
     'subln_g': 10.862,
     'b_gu': 8.0,
     'b_down': 34.804,
     'final_g': 20.578,
     'norm2_g': 3.26,
     'router_b': 4.493}
    for name, (base, spread) in spreads.items():
        noise = np.random.default_rng([zlib.crc32(name.encode()), seed]).standard_normal(out[name].shape)
        drawn = base * np.exp(spread * noise) if base else spread * noise
        out[name] = __import__('jax').numpy.asarray(drawn.astype(out[name].dtype))
    for name, factor in factors.items():
        out[name] = (out[name] * factor).astype(out[name].dtype)
    return out
```

```python
import math
from contextlib import ExitStack

import concourse.bass as bass
import numpy as np
from concourse import mybir

F32 = mybir.dt.float32
I32 = mybir.dt.int32
ALU = mybir.AluOpType
ACT = mybir.ActivationFunctionType
AX = mybir.AxisListType

P = 128
D = 1024
T = 256
KT = D // P
TT = T // P
DH = 64
DAH, SBH = 8, 16
CHUNKMASK = 64
NE, TOPK = 32, 4
EPS = 1e-6
LAM_INIT = 0.8 - 0.6 * math.exp(-0.3 * 0)
FAR = 1e30
LIMIT, ALPHA = 7.0, 1.702

CW = 512
GROUPS_ADA1 = 4
GROUPS_IN = 16
GROUPS_ADA2 = 8
CAP = 72
PASSES = -(-T // CAP)
PAIRS = NE // 2
G_BRANCH = GROUPS_ADA1 + GROUPS_IN + GROUPS_ADA2
HB = KT // 2 * CAP

R_C, R_N1, R_N2, R_ADA, R_SUB, R_LQ, R_LK, R_END = 0, 8, 16, 24, 72, 73, 74, 75
M_SH1, M_SC1, M_G1, M_SH2, M_SC2, M_G2 = (8 * n for n in range(6))


class Order:

    def __init__(self, engine, sem):
        self.engine, self.sem, self.base, self.steps = engine, sem, 0, 0

    def then(self, instruction):
        instruction.then_inc(self.sem, 1)
        self.steps += 1
        self.engine.wait_ge(self.sem, self.base + self.steps)

    def start_at(self, base):
        self.base, self.steps = base, 0


def build(nc, x, c, w_ada, b_ada, norm1_g, w_in, lam_q1, lam_k1, lam_q2, lam_k2, subln_g, w_pa, w_pb, w_o,
          norm2_g, router_w, router_b, w_gu, b_gu, w_down, b_down, final_g, out):
    ctx = ExitStack()
    with ctx:
        def sb(name, shape, dt=F32):
            return ctx.enter_context(nc.sbuf_tensor(name, shape, dt))

        def sem(name):
            return ctx.enter_context(nc.semaphore(name))

        gu_ring = sb("gu_ring", [P, 16, 2048])
        down_ring = sb("down_ring", [P, 4, 2048])
        qkT = down_ring[:, :, :].rearrange("p s n -> p (s n)").rearrange("p (i b t) -> p i b t", i=2, b=16)
        v_sb = gu_ring[:, 8:10, :].rearrange("p i (t n) -> p i t n", t=TT)
        hT = gu_ring[:, 10, :].rearrange("p (k t) -> p k t", k=KT)
        g1b = gu_ring[:, 10, 0:D]
        g1diag = gu_ring[:, 10, D:2 * D].rearrange("p (k n) -> p k n", k=KT)
        gateT = gu_ring[:, 11:13, :].rearrange("p i (k t) -> p i k t", k=KT)
        oaT = gu_ring[:, 13, :].rearrange("p (k t) -> p k t", k=KT)
        obT = gu_ring[:, 14, :].rearrange("p (k t) -> p k t", k=KT)
        da_w = gu_ring[:, 14, 0:768].rearrange("p (b n) -> p b n", b=2)
        da_wT = gu_ring[:, 14, 768:1536].rearrange("p (b n) -> p b n", b=2)
        mergedT = gu_ring[:, 15, :].rearrange("p (k t) -> p k t", k=KT)
        oa = gu_ring[:, 15, :].rearrange("p (t n) -> p t n", t=TT)

        xres = sb("xres", [P, TT, D])
        xn = sb("xn", [P, TT, D])
        scratch = sb("scratch", [P, 5024])
        at = [0]

        def part(n):
            at[0] += n
            assert at[0] <= 5024
            return scratch[:, at[0] - n:at[0]]

        da_s = part(4 * 384).rearrange("p (b m n) -> p b m n", b=2, m=2)
        sb_t = part(2 * 384).rearrange("p (b n) -> p b n", b=2)
        sb_l = part(3 * 384).rearrange("p (b n) -> p b n", b=3)
        sb_a = part(3 * 384).rearrange("p (b n) -> p b n", b=3)
        dist = part(384)
        h2T = scratch[:, 0:2048].rearrange("p (k t) -> p k t", k=KT)
        tmp = scratch[:, 2048:3072].rearrange("p (b n) -> p b n", b=2)
        at[0] = 0
        xT = part(KT * CAP).rearrange("p (k s) -> p k s", k=KT)
        g_sb = part(KT * CAP).rearrange("p (k s) -> p k s", k=KT)
        sig = part(KT * CAP).rearrange("p (k s) -> p k s", k=KT)
        u_sb = part(KT * CAP).rearrange("p (k s) -> p k s", k=KT)
        act_sb = part(KT * CAP).rearrange("p (k s) -> p k s", k=KT)
        yT = part(KT * CAP).rearrange("p (k s) -> p k s", k=KT)
        y_sb = part(D)
        onehot = part(TT * CAP).rearrange("p (t s) -> p t s", t=TT)
        gated = part(TT * CAP).rearrange("p (t s) -> p t s", t=TT)
        backT = part(T)
        y_rows = y_sb[0:NE, :]
        lg, r_a, r_b = (scratch[:, 2304 + 64 * n:2368 + 64 * n].rearrange("p (t e) -> p t e", t=TT)
                        for n in range(3))

        ident = sb("ident", [P, P])
        ones = sb("ones", [P, P])
        neg_ones = sb("neg_ones", [P, P])
        neg_tri = sb("neg_tri", [P, P])
        before = sb("before", [P, P])
        iota = sb("iota", [P, CAP])
        vec = sb("vec", [P, R_END])
        bgu = sb("bgu", [P, NE, 16])
        mod = sb("mod", [P, 48])
        a1 = sb("a1", [P, KT])
        a2 = sb("a2", [P, KT])
        lam = sb("lam", [P, 4])
        nsub = sb("nsub", [P, 1])
        stat = sb("stat", [P, 8])
        smax = sb("smax", [P, 2, 4])
        ssum = sb("ssum", [P, 2, 4])
        srec = sb("srec", [P, 2, 4])
        osq = sb("osq", [P, 16])
        rw_sb = sb("rw_sb", [P, KT, NE])
        rb_sb = sb("rb_sb", [1, NE])
        top8 = sb("top8", [P, TT, 8])
        r1 = sb("r1", [P, TT, NE + 1])
        sel = sb("sel", [P, TT, NE])
        gates = sb("gates", [P, TT, NE])
        small = sb("small", [P, 8])
        fgb = sb("fgb", [P, D])
        most = sb("most", [P, 1], I32)
        vt = xn[0:R_END, 0, 0:P]
        bgu_rows = xn[:, 1, 0:512].rearrange("p (a f) -> p a f", a=4)

        bank = [ctx.enter_context(nc.psum_tensor(f"bank{n}", [P, 512], F32)) for n in range(8)]

        slot_in = [sem(f"slot_in{n}") for n in range(16)]
        down_in = [sem(f"down_in{n}") for n in range(4)]
        small_in = sem("small_in")
        bgu_in = sem("bgu_in")
        x_in = sem("x_in")
        router_in = sem("router_in")
        bdown_in = sem("bdown_in")
        fg_in = sem("fg_in")
        out_done = sem("out_done")
        groups_used = sem("groups_used")
        gu_used = sem("gu_used")
        down_used = sem("down_used")
        consts = sem("consts")
        pool_own = sem("pool_own")
        dist_abs = sem("dist_abs")
        vecT_done = sem("vecT_done")
        vec_ready = sem("vec_ready")
        lam_done = sem("lam_done")
        lam_exp = sem("lam_exp")
        sq_done = sem("sq_done")
        ms_ready = sem("ms_ready")
        root_ready = sem("root_ready")
        xn_ready = sem("xn_ready")
        xT_done = sem("xT_done")
        mod_ready = sem("mod_ready")
        emptied = sem("emptied")
        proj_done = sem("proj_done")
        scores_done = sem("scores_done")
        scores_ready = sem("scores_ready")
        max_ready = sem("max_ready")
        exp_ready = sem("exp_ready")
        w_ready = sem("w_ready")
        wT_done = sem("wT_done")
        wT_ready = sem("wT_ready")
        pv_done = sem("pv_done")
        pv_read = sem("pv_read")
        oa_ready = sem("oa_ready")
        oaT_done = sem("oaT_done")
        oaT_ready = sem("oaT_ready")
        diag_ready = sem("diag_ready")
        g1b_done = sem("g1b_done")
        g1b_ready = sem("g1b_ready")
        z_done = sem("z_done")
        absz_ready = sem("absz_ready")
        ln_ready = sem("ln_ready")
        splus_ready = sem("splus_ready")
        splus_masked = sem("splus_masked")
        logw_done = sem("logw_done")
        sbw_ready = sem("sbw_ready")
        sbw_masked = sem("sbw_masked")
        sbpv_done = sem("sbpv_done")
        obT_ready = sem("obT_ready")
        branch_done = sem("branch_done")
        merged_ready = sem("merged_ready")
        mixed_done = sem("mixed_done")
        x1_ready = sem("x1_ready")
        h2T_even = sem("h2T_even")
        h2T_odd = sem("h2T_odd")
        logits_done = sem("logits_done")
        top_ready = sem("top_ready")
        gexp_ready = sem("gexp_ready")
        sel_ready = sem("sel_ready")
        rank_done = sem("rank_done")
        most_ready = sem("most_ready")
        gates_ready = sem("gates_ready")
        bgu_done = sem("bgu_done")
        seed_done = sem("seed_done")
        onehot_ready = sem("onehot_ready")
        gated_ready = sem("gated_ready")
        taken_done = sem("taken_done")
        xTe_ready = sem("xTe_ready")
        g_done = sem("g_done")
        gu_read = sem("gu_read")
        gmin_ready = sem("gmin_ready")
        sig_ready = sem("sig_ready")
        act_ready = sem("act_ready")
        back_done = sem("back_done")
        back_ready = sem("back_ready")
        yT_ready = sem("yT_ready")
        y_done = sem("y_done")
        y_ready = sem("y_ready")
        given_done = sem("given_done")
        given_added = sem("given_added")
        out_ready = sem("out_ready")
        sum_ready = sem("sum_ready")
        act_own, dve_own = sem("act_own"), sem("dve_own")

        def group_slots(group):
            s = (2 * group + 4) % 8
            return s, s + 1

        def group_chunk(group, h):
            return gu_ring[:, group_slots(group)[h], :].rearrange("p (k n) -> p k n", n=CW)

        def wait_group(eng, group, h, loops=0):
            chunk = 2 * group + h
            eng.wait_ge(slot_in[group_slots(group)[h]], (loops + chunk // 8 + 1) * 16)

        USES = [8] * 4 + [9] * 4 + [0] * 8

        block = ctx.enter_context(nc.Block())

        @block.sync
        def _(sp):
            def load_group(w, col, group, wait=None, loops=0):
                if wait is not None:
                    sp.wait_ge(groups_used, wait)
                for h in range(2):
                    src = w[0, h * 512:(h + 1) * 512, bass.ds(col, CW)].rearrange("(k p) n -> p k n", p=P)
                    sp.dma_start(group_chunk(group, h), src).then_inc(slot_in[group_slots(group)[h]], 16)

            for g in range(GROUPS_ADA1):
                load_group(w_ada, g * CW, g)
            with sp.Fori(0, 2) as it:
                for g in range(8):
                    col = it * 3072 + g * CW if g < 6 else it * 1024 + 6144 + (g - 6) * CW
                    load_group(w_in, col, GROUPS_ADA1 + g, wait=it * 8 + (g + 1))
            g0 = GROUPS_ADA1 + GROUPS_IN
            for g in range(GROUPS_ADA2):
                load_group(w_ada, (GROUPS_ADA1 + g) * CW, g0 + g, wait=g0 + g - 3)
            g0 += GROUPS_ADA2
            for n, (w, half) in enumerate([(w_pa, 0), (w_pb, 0), (w_pa, 1), (w_pb, 1), (w_o, 0), (w_o, 1)]):
                load_group(w, half * CW, g0 + n, wait=g0 + n - 3)

            def load_gu(e, expert, half, kt):
                sp.dma_start(gu_ring[:, 8 * half + kt, :],
                             w_gu[0, bass.ds(expert, 1), kt * P:(kt + 1) * P, :].rearrange("a p n -> p (a n)")
                             ).then_inc(slot_in[8 * half + kt], 16)

            def load_down(expert, j):
                sp.dma_start(down_ring[:, j, :].rearrange("p (k n) -> p k n", k=2),
                             w_down[0, bass.ds(expert, 1), j * 2 * P:(j + 1) * 2 * P, :]
                             .rearrange("a (k p) n -> p (a k) n", p=P)).then_inc(down_in[j], 16)

            for kt in range(KT):
                if kt % 2 == 0:
                    sp.wait_ge(groups_used, 31 + kt // 2)
                load_gu(0, 0, 0, kt)
            sp.wait_ge(sbpv_done, SBH)
            sp.dma_start(y_rows, b_down[0, :, :]).then_inc(bdown_in, 16)
            for j in range(4):
                load_down(0, j)
            for kt in range(KT):
                if kt == 2:
                    sp.wait_ge(x1_ready, 4)
                load_gu(1, 1, 1, kt)
            for j in range(4):
                sp.wait_ge(down_used, j + 1)
                load_down(1, j)

            def pair(first, n):
                for half in range(2):
                    for kt in range(KT):
                        sp.wait_ge(gu_used, first * 8 + (8 * half + kt - 15))
                        load_gu(None, n * 2 + half, half, kt)
                    for j in range(4):
                        sp.wait_ge(down_used, first * 4 + (4 * half + j - 3))
                        load_down(n * 2 + half, j)

            with sp.Fori(1, PAIRS) as n:
                pair(n * 2, n)
            sp.wait_ge(most_ready, 1)
            count = sp.value_load(most[0:1, 0:1], min_val=0, max_val=T)
            with sp.Fori(1, PASSES) as p:
                with sp.If(count > p * CAP):
                    with sp.Fori(0, PAIRS) as n:
                        pair(p * NE + n * 2, n)
            for tt in range(TT):
                sp.wait_ge(out_ready, tt + 1)
                sp.dma_start(out[0, tt * P:(tt + 1) * P, :], xn[:, tt, :]).then_inc(out_done, 16)
            sp.wait_ge(out_done, 16 * TT)

        @block.gpsimd
        def _(pool):
            own = Order(pool, pool_own)

            def tri(m, fill, keep_when, base, step, channel):
                return nc.gpsimd.affine_select(out=m, in_=m, compare_op=keep_when, fill=fill, base=base,
                                               pattern=[[step, P]], channel_multiplier=channel)

            nc.gpsimd.memset(ones[:], 1.0).then_inc(consts, 1)
            own.then(nc.gpsimd.memset(ident[:], 0.0))
            tri(ident[:], 1.0, ALU.not_equal, 0, -1, 1).then_inc(consts, 1)
            nc.gpsimd.iota(dist[:, 0:128], pattern=[[-1, 128]], base=0, channel_multiplier=1,
                           allow_small_or_imprecise_dtypes=True).then_inc(consts, 1)
            nc.gpsimd.iota(dist[:, 128:384], pattern=[[-1, 256]], base=P, channel_multiplier=1,
                           allow_small_or_imprecise_dtypes=True).then_inc(consts, 1)
            nc.gpsimd.iota(iota[:], pattern=[[1, CAP]], base=1, channel_multiplier=0,
                           allow_small_or_imprecise_dtypes=True).then_inc(consts, 1)
            nc.gpsimd.memset(neg_ones[:], -1.0).then_inc(consts, 1)
            own.then(nc.gpsimd.memset(neg_tri[:], -1.0))
            tri(neg_tri[:], 0.0, ALU.is_ge, 0, -1, 1).then_inc(consts, 1)
            own.then(nc.gpsimd.memset(before[:], 1.0))
            tri(before[:], 0.0, ALU.is_gt, 0, 1, -1).then_inc(consts, 1)

            def causal(m):
                v = m.rearrange("p (a n) -> p a n", a=3)[:, 0:3:2, :]
                return nc.gpsimd.affine_select(out=v, in_=v, compare_op=ALU.is_gt, fill=0.0, base=0,
                                               pattern=[[0, 2], [1, P]], channel_multiplier=-1)

            for s in range(SBH + 2):
                if s < SBH:
                    pool.wait_ge(splus_ready, s + 1)
                    causal(sb_l[:, s % 3, :]).then_inc(splus_masked, 1)
                if s >= 2:
                    pool.wait_ge(sbw_ready, s - 1)
                    causal(sb_a[:, (s - 2) % 3, :]).then_inc(sbw_masked, 1)

        @block.scalar
        def _(act):
            own = Order(act, act_own)
            A = nc.scalar.activation
            for rows, src in ((slice(R_C, R_N1), c[0, :].rearrange("(r f) -> r f", f=P)),
                              (slice(R_N1, R_N2), norm1_g[0, :].rearrange("(r f) -> r f", f=P)),
                              (slice(R_N2, R_ADA), norm2_g[0, :].rearrange("(r f) -> r f", f=P)),
                              (slice(R_ADA, R_SUB), b_ada[0, :].rearrange("(r f) -> r f", f=P)),
                              (slice(R_SUB, R_LQ), subln_g[0:1, :])):
                act.dma_start(xn[rows, 0, 0:P], src).then_inc(small_in, 16)
            for row, a, b in ((R_LQ, lam_q1, lam_q2), (R_LK, lam_k1, lam_k2)):
                act.dma_start(xn[row:row + 1, 0, 0:DH], a[0:1, :]).then_inc(small_in, 16)
                act.dma_start(xn[row:row + 1, 0, DH:P], b[0:1, :]).then_inc(small_in, 16)
            act.dma_start(xres[:, :, :], x[0, :, :].rearrange("(t p) n -> p t n", p=P)).then_inc(x_in, 16)
            act.dma_start(bgu_rows, b_gu[0, :, :].rearrange("e (r f) -> (e r) f", f=P)
                          .rearrange("(a p) f -> p a f", p=P)).then_inc(bgu_in, 16)
            act.dma_start(rw_sb[:], router_w[0, :, :].rearrange("(k p) e -> p k e", p=P)).then_inc(router_in, 16)
            act.dma_start(rb_sb[:], router_b[0:1, :]).then_inc(router_in, 16)
            act.dma_start(fgb[:], final_g.partition_broadcast(P)).then_inc(fg_in, 16)

            act.wait_ge(x_in, 16)
            for tt in range(TT):
                A(hT[:, 4 * tt:4 * tt + 4, :], xres[:, tt, :].rearrange("p (k t) -> p k t", k=4), ACT.Square,
                  accum_out=stat[:, tt:tt + 1]).then_inc(sq_done, 1)
            act.wait_ge(ms_ready, 1)
            A(stat[:, 4:6], stat[:, 2:4], ACT.Sqrt).then_inc(root_ready, 1)
            act.wait_ge(lam_done, 1)
            for n in range(2):
                A(lam[:, n:n + 1], bank[(7, 4)[n]][:, 256:257], ACT.Exp).then_inc(lam_exp, 1)
            act.wait_ge(xT_done, 4)
            act.wait_ge(mod_ready, 1)
            for kt in range(KT):
                A(hT[:, kt, :], bank[kt // 2][:, (kt % 2) * T:(kt % 2 + 1) * T], ACT.Identity,
                  scale=a1[:, kt:kt + 1], bias=mod[:, M_SH1 + kt:M_SH1 + kt + 1]).then_inc(emptied, 1)
            with act.Fori(0, 2) as it:
                for g in range(8):
                    for h in range(2):
                        if h == 0:
                            act.wait_ge(proj_done, it * 8 + (g + 1))
                        else:
                            act.wait_ge(groups_used, it * 8 + (GROUPS_ADA1 + g + 1))
                        src = bank[2 * (g % 2) + h][:, :]
                        if g < 4:
                            dst = qkT[:, bass.ds(it, 1), 4 * g + 2 * h:4 * g + 2 * h + 2, :]
                            A(dst.rearrange("p i b t -> p (i b t)"), src, ACT.Copy,
                              scale=DH ** -0.5 if g < 2 else 1.0).then_inc(emptied, 1)
                        elif g < 6:
                            dst = v_sb[:, bass.ds(it, 1), h, (g - 4) * CW:(g - 3) * CW]
                            A(dst.rearrange("p i n -> p (i n)"), src, ACT.Copy).then_inc(emptied, 1)
                        else:
                            b = 4 * (g - 6) + 2 * h
                            dst = gateT[:, bass.ds(it, 1), b:b + 2, :]
                            A(dst.rearrange("p i k t -> p (i k t)"), src, ACT.Sigmoid).then_inc(emptied, 1)

            for s in range(DAH + 1):
                if s < DAH:
                    for m in range(2):
                        for t in range(TT):
                            act.wait_ge(max_ready, 4 * s + 2 * m + t + 1)
                            span = slice(0, 128) if t == 0 else slice(128, 384)
                            A(da_s[:, s % 2, m, span], da_s[:, s % 2, m, span], ACT.Exp,
                              bias=smax[:, s % 2, 2 * m + t:2 * m + t + 1],
                              accum_out=ssum[:, s % 2, 2 * m + t:2 * m + t + 1]).then_inc(exp_ready, 1)
                if s >= 1:
                    act.wait_ge(wT_done, s)
                    if s >= 3:
                        act.wait_ge(pv_done, s - 2)
                    A(da_wT[:, (s - 1) % 2, :], bank[4][:, 0:384], ACT.Copy).then_inc(wT_ready, 1)
            act.wait_ge(ms_ready, 2)
            A(osq[:], osq[:], ACT.Sqrt).then_inc(root_ready, 1)

            for s in range(SBH + 2):
                if s < SBH:
                    act.wait_ge(absz_ready, s + 1)
                    own.then(A(sb_t[:, s % 2, :], sb_t[:, s % 2, :], ACT.Exp))
                    A(sb_t[:, s % 2, :], sb_t[:, s % 2, :], ACT.Ln, bias=1.0).then_inc(ln_ready, 1)
                if s >= 2:
                    h = s - 2
                    act.wait_ge(logw_done, h + 1)
                    if h >= 3:
                        act.wait_ge(sbpv_done, h - 2)
                    A(sb_a[:, h % 3, :], bank[(0, 1, 2, 5)[h % 4]][:, 0:384], ACT.Exp).then_inc(sbw_ready, 1)
                if 4 <= s < 8:
                    n = s - 4
                    act.wait_ge(oaT_done, n + 1)
                    A(oaT[:, 2 * n:2 * n + 2, :].rearrange("p k t -> p (k t)"), bank[3 + n % 2][:, :], ACT.Copy,
                      scale=nsub[:, 0:1]).then_inc(oaT_ready, 1)
                if s in (8, 9):
                    n = s - 8
                    act.wait_ge(g1b_done, n + 1)
                    A(g1b[:, n * 512:(n + 1) * 512], bank[3 + n][:, :], ACT.Copy).then_inc(g1b_ready, 1)

            for tt in range(TT):
                act.wait_ge(x1_ready, tt + 3)
                A(xn[:, tt, :], xres[:, tt, :], ACT.Square, accum_out=stat[:, tt:tt + 1]).then_inc(sq_done, 1)
            act.wait_ge(ms_ready, 3)
            A(stat[:, 4:6], stat[:, 2:4], ACT.Sqrt).then_inc(root_ready, 1)
            for kt in range(0, KT, 2):
                act.wait_ge(xT_done, 5 + kt // 2)
                A(h2T[:, kt, :], bank[4 + kt // 2][:, 0:T], ACT.Identity,
                  scale=a2[:, kt:kt + 1], bias=mod[:, M_SH2 + kt:M_SH2 + kt + 1]).then_inc(h2T_even, 1)
            act.wait_ge(top_ready, 1)
            for tt in range(TT):
                A(r_b[:, tt, :], lg[:, tt, :], ACT.Exp, bias=small[:, tt:tt + 1]).then_inc(gexp_ready, 1)
            act.wait_ge(yT_ready, 1)
            act.wait_ge(seed_done, 2)
            A(backT[0:NE, :], bank[2][0:NE, 0:T], ACT.Copy).then_inc(back_ready, 1)

            def copy_y(given):
                for h in range(2):
                    act.wait_ge(y_done, given * 2 + (h + 1))
                    A(y_sb[0:CAP, h * 512:(h + 1) * 512], bank[6 + h][0:CAP, :], ACT.Copy).then_inc(y_ready, 1)

            def expert(e, given):
                copy_y(given)
                act.wait_ge(gmin_ready, e + 1)
                A(sig, g_sb, ACT.Sigmoid, scale=ALPHA).then_inc(sig_ready, 1)
                act.wait_ge(back_done, e + 1)
                A(backT[0:CAP, :], bank[4][0:CAP, 0:T], ACT.Copy).then_inc(back_ready, 1)

            with act.Fori(0, PAIRS) as n:
                for half in range(2):
                    expert(n * 2 + half, n * 2 + half)
            copy_y(NE)
            act.wait_ge(most_ready, 1)
            count = act.value_load(most[0:1, 0:1], min_val=0, max_val=T)
            with act.Fori(1, PASSES) as p:
                with act.If(count > p * CAP):
                    with act.Fori(0, PAIRS) as n:
                        for half in range(2):
                            expert(p * NE + n * 2 + half, p * (NE + 1) + n * 2 + half)
                    copy_y(p * (NE + 1) + NE)

            act.wait_ge(sum_ready, 1)
            for tt in range(TT):
                A(xn[:, tt, :], xres[:, tt, :], ACT.Square, accum_out=stat[:, tt:tt + 1]).then_inc(sq_done, 1)
            act.wait_ge(ms_ready, 4)
            A(stat[:, 4:6], stat[:, 2:4], ACT.Sqrt).then_inc(root_ready, 1)

        @block.vector
        def _(dve):
            own = Order(dve, dve_own)
            V = nc.vector

            def root_mean(n, tiles_done):
                dve.wait_ge(sq_done, 2 * tiles_done)
                V.tensor_scalar(stat[:, 2:4], stat[:, 0:2], 1.0 / D, EPS, ALU.mult, ALU.add).then_inc(ms_ready, 1)
                dve.wait_ge(root_ready, n)
                own.then(V.reciprocal(stat[:, 6:8], stat[:, 4:6]))

            dve.wait_ge(vecT_done, 1)
            V.tensor_copy(vec[:], bank[7][:, 0:R_END]).then_inc(vec_ready, 1)
            dve.wait_ge(vec_ready, 1)
            V.tensor_tensor(lam[:, 3:4], vec[:, R_LQ:R_LQ + 1], vec[:, R_LK:R_LK + 1], ALU.mult).then_inc(vec_ready, 1)
            V.tensor_scalar(nsub[:], vec[:, R_SUB:R_SUB + 1], 1.0 - LAM_INIT, None, ALU.mult).then_inc(vec_ready, 1)
            dve.wait_ge(bgu_done, 1)
            V.tensor_copy(bgu[:].rearrange("p e r -> p (e r)"), bank[6][:, :]).then_inc(vec_ready, 1)
            root_mean(1, 1)
            dve.wait_ge(bgu_done, 1)
            for tt in range(TT):
                V.tensor_scalar(xn[:, tt, :], xres[:, tt, :], stat[:, 6 + tt:7 + tt], None, ALU.mult
                                ).then_inc(xn_ready, 1)
            dve.wait_ge(lam_exp, 2)
            own.then(V.tensor_tensor(lam[:, 2:3], lam[:, 1:2], lam[:, 0:1], ALU.subtract))
            own.then(V.tensor_scalar(lam[:, 2:3], lam[:, 2:3], -LAM_INIT, None, ALU.add))
            dve.wait_ge(consts, 4)
            own.then(V.scalar_tensor_tensor(dist[:], dist[:], -1.0, dist[:], op0=ALU.mult, op1=ALU.max))
            V.memset(dist[0:64, 64:128], FAR)
            own.then(V.memset(dist[0:64, 128 + 192:384], FAR))
            dve.wait_ge(groups_used, GROUPS_ADA1)
            own.then(V.tensor_tensor(mod[:, 0:16], bank[5][:, 0:16], vec[:, R_ADA:R_ADA + 16], ALU.add))
            V.scalar_tensor_tensor(a1[:], mod[:, M_SC1:M_SC1 + 8], 1.0, vec[:, R_N1:R_N1 + 8],
                                   op0=ALU.add, op1=ALU.mult).then_inc(mod_ready, 1)

            SPAN = [slice(0, 128), slice(128, 384)]
            for s in range(DAH + 2):
                if s < DAH:
                    b = s % 2
                    for m in range(2):
                        dve.wait_ge(scores_done, 2 * s + m + 1)
                        if s >= 2 and m == 0:
                            dve.wait_ge(w_ready, s - 1)
                        V.scalar_tensor_tensor(da_s[:, b, m, :], dist[:], -(2.0 ** (-8.0 * (s + 1) / DAH)),
                                               bank[2 * b + m][:, 0:384], op0=ALU.mult, op1=ALU.add
                                               ).then_inc(scores_ready, 1)
                        dve.wait_ge(scores_ready, 2 * s + m + 1)
                        for t in range(TT):
                            V.tensor_reduce(smax[:, b, 2 * m + t:2 * m + t + 1], da_s[:, b, m, SPAN[t]], AX.X,
                                            ALU.max, negate=True).then_inc(max_ready, 1)
                if 1 <= s <= DAH:
                    h, b = s - 1, (s - 1) % 2
                    dve.wait_ge(exp_ready, 4 * h + 4)
                    own.then(V.reciprocal(srec[:, b, :], ssum[:, b, :]))
                    own.then(V.tensor_scalar(srec[:, b, 2:4], srec[:, b, 2:4], lam[:, 2:3], None, ALU.mult))
                    for t in range(TT):
                        V.tensor_scalar(da_s[:, b, 0, SPAN[t]], da_s[:, b, 0, SPAN[t]], srec[:, b, t:t + 1], None,
                                        ALU.mult).then_inc(dve_own, 1)
                        own.steps += 1
                    dve.wait_ge(dve_own, own.base + own.steps)
                    if h >= 2:
                        dve.wait_ge(wT_done, h - 1)
                    for t in range(TT):
                        last = V.scalar_tensor_tensor(da_w[:, b, SPAN[t]], da_s[:, b, 1, SPAN[t]],
                                                      srec[:, b, 2 + t:3 + t], da_s[:, b, 0, SPAN[t]],
                                                      op0=ALU.mult, op1=ALU.add)
                        if t == 0:
                            last.then_inc(dve_own, 1)
                            own.steps += 1
                    last.then_inc(w_ready, 1)
                if s >= 2:
                    h = s - 2
                    dve.wait_ge(pv_done, h + 1)
                    V.tensor_copy(oa[:, :, h * P:(h + 1) * P],
                                  bank[6 + h % 2][:, 0:256].rearrange("p (t n) -> p t n", t=TT)).then_inc(pv_read, 1)
            dve.wait_ge(pv_read, DAH)
            oav = oa.rearrange("p t (h n) -> p (t h) n", n=P)
            sqv = xn[:, :, :].rearrange("p t (h n) -> p (t h) n", n=P)
            dve.wait_ge(xT_done, 4)
            own.then(V.tensor_tensor(sqv, oav, oav, ALU.mult))
            own.then(V.tensor_reduce(osq[:], sqv, AX.X, ALU.add))
            V.tensor_scalar(osq[:], osq[:], 1.0 / (2 * DH), EPS, ALU.mult, ALU.add).then_inc(ms_ready, 1)

            def minus_abs(h):
                z, l = bank[(0, 1, 2, 5)[h % 4]][:, 0:384], sb_l[:, h % 3, :]
                dve.wait_ge(z_done, h + 1)
                if h >= 3:
                    dve.wait_ge(logw_done, h - 2)
                own.then(V.tensor_scalar(l, z, 0.0, None, ALU.max))
                V.scalar_tensor_tensor(sb_t[:, h % 2, :], l, -2.0, z, op0=ALU.mult, op1=ALU.add
                                       ).then_inc(absz_ready, 1)

            def softplus(h):
                dve.wait_ge(ln_ready, h + 1)
                V.tensor_tensor(sb_l[:, h % 3, :], sb_l[:, h % 3, :], sb_t[:, h % 2, :], ALU.add
                                ).then_inc(splus_ready, 1)

            dve.wait_ge(groups_used, GROUPS_ADA1 + GROUPS_IN + GROUPS_ADA2)
            own.then(V.tensor_tensor(mod[:, 16:48], bank[5][:, 16:48], vec[:, R_ADA + 16:R_ADA + 48], ALU.add))
            V.scalar_tensor_tensor(a2[:], mod[:, M_SC2:M_SC2 + 8], 1.0, vec[:, R_N2:R_N2 + 8],
                                   op0=ALU.add, op1=ALU.mult).then_inc(mod_ready, 1)
            minus_abs(0)
            dve.wait_ge(root_ready, 2)
            own.then(V.reciprocal(osq[:], osq[:]))
            V.tensor_tensor(oav, oav, osq[:].unsqueeze(2).to_broadcast([P, 16, P]), ALU.mult).then_inc(oa_ready, 1)
            for kt in range(KT):
                V.tensor_scalar(g1diag[:, kt, :], ident[:], mod[:, M_G1 + kt:M_G1 + kt + 1], None, ALU.mult
                                ).then_inc(diag_ready, 1)
            for s in range(1, SBH + 5):
                if s < SBH:
                    if s >= 2:
                        dve.wait_ge(splus_ready, s - 1)
                    minus_abs(s)
                if s - 1 < SBH:
                    softplus(s - 1)
                if s >= 5 and (s - 5) % 2 == 0 and (s - 5) // 2 < SBH // 2:
                    pair = (s - 5) // 2
                    dve.wait_ge(sbpv_done, 2 * pair + 2)
                    V.tensor_copy(obT[:, pair, :], bank[6 + pair % 2][:, 0:T]).then_inc(obT_ready, 1)

            def wait_bank(first_done, firsts, second, groups):
                if second:
                    dve.wait_ge(groups_used, groups)
                else:
                    dve.wait_ge(first_done, firsts)

            for half in range(2):
                for n in range(2):
                    blk = slice(4 * half + 2 * n, 4 * half + 2 * n + 2)
                    dst = mergedT[:, blk, :].rearrange("p k t -> p (k t)")
                    wait_bank(branch_done, 2 * half + 1, n, G_BRANCH + 2 * half + 1)
                    own.then(V.tensor_tensor(dst, bank[4 * half + n][:, :],
                                             gateT[:, 0, blk, :].rearrange("p k t -> p (k t)"), ALU.mult))
                for n in range(2):
                    blk = slice(4 * half + 2 * n, 4 * half + 2 * n + 2)
                    dst = mergedT[:, blk, :].rearrange("p k t -> p (k t)")
                    wait_bank(branch_done, 2 * half + 2, n, G_BRANCH + 2 * half + 2)
                    own.then(V.tensor_tensor(tmp[:, n, :], bank[4 * half + 2 + n][:, :],
                                             gateT[:, 1, blk, :].rearrange("p k t -> p (k t)"), ALU.mult))
                    V.tensor_tensor(dst, dst, tmp[:, n, :], ALU.add).then_inc(merged_ready, 1)
            dve.wait_ge(g1b_ready, 2)
            dve.wait_ge(merged_ready, 4)
            for half in range(2):
                for tt in range(TT):
                    n = 2 * half + tt
                    cols = slice(half * 512, (half + 1) * 512)
                    wait_bank(mixed_done, half + 1, tt, G_BRANCH + 4 + half + 1)
                    if n >= 2:
                        dve.wait_ge(x1_ready, n - 1)
                    own.then(V.tensor_tensor(tmp[:, n % 2, :], bank[n][:, :], g1b[:, cols], ALU.mult))
                    V.tensor_tensor(xres[:, tt, cols], xres[:, tt, cols], tmp[:, n % 2, :], ALU.add
                                    ).then_inc(x1_ready, 1)
            dve.wait_ge(sq_done, 4)
            V.tensor_scalar(stat[:, 2:4], stat[:, 0:2], 1.0 / D, EPS, ALU.mult, ALU.add).then_inc(ms_ready, 1)
            dve.wait_ge(root_ready, 3)
            own.then(V.reciprocal(stat[:, 6:8], stat[:, 4:6]))
            for tt in range(TT):
                V.tensor_scalar(xn[:, tt, :], xres[:, tt, :], stat[:, 6 + tt:7 + tt], None, ALU.mult
                                ).then_inc(xn_ready, 1)
            for kt in range(1, KT, 2):
                dve.wait_ge(xT_done, 5 + kt // 2)
                dve.wait_ge(h2T_even, kt // 2 + 1)
                V.tensor_scalar(h2T[:, kt, :], bank[4 + kt // 2][:, T:2 * T], a2[:, kt:kt + 1],
                                mod[:, M_SH2 + kt:M_SH2 + kt + 1], ALU.mult, ALU.add).then_inc(h2T_odd, 1)

            dve.wait_ge(logits_done, 1)
            own.then(V.tensor_copy(lg[:], bank[0][:, 0:TT * NE].rearrange("p (t e) -> p t e", t=TT)))
            for tt in range(TT):
                own.then(V.max(top8[:, tt, :], lg[:, tt, :]))
            V.tensor_scalar(small[:, 0:2], top8[:, :, 0], -1.0, None, ALU.mult).then_inc(top_ready, 1)
            for tt in range(TT):
                fourth = top8[:, tt, TOPK - 1:TOPK]
                own.then(V.tensor_scalar(sel[:, tt, :], lg[:, tt, :], fourth, None, ALU.is_gt))
                own.then(V.tensor_reduce(small[:, 2 + tt:3 + tt], sel[:, tt, :], AX.X, ALU.add))
                own.then(V.tensor_scalar(r_a[:, tt, :], lg[:, tt, :], fourth, None, ALU.is_equal))
                own.then(V.tensor_tensor_scan(r1[:, tt, 0:NE], r_a[:, tt, :], ones[:, 0:NE],
                                              small[:, 2 + tt:3 + tt], op0=ALU.add, op1=ALU.mult))
                own.then(V.scalar_tensor_tensor(r_a[:, tt, :], r1[:, tt, 0:NE], TOPK + 0.5, r_a[:, tt, :],
                                                op0=ALU.is_lt, op1=ALU.mult))
                V.tensor_tensor(sel[:, tt, :], sel[:, tt, :], r_a[:, tt, :], ALU.add).then_inc(sel_ready, 1)
            dve.wait_ge(sel_ready, 2)
            dve.wait_ge(gexp_ready, 2)
            own.then(V.tensor_tensor(r_b[:], r_b[:], sel[:], ALU.mult))
            own.then(V.tensor_reduce(small[:, 4:6], r_b[:], AX.X, ALU.add))
            own.then(V.reciprocal(small[:, 6:8], small[:, 4:6]))
            V.tensor_tensor(gates[:], r_b[:], small[:, 6:8].unsqueeze(2).to_broadcast([P, TT, NE]), ALU.mult
                            ).then_inc(gates_ready, 1)
            dve.wait_ge(rank_done, 1)
            own.then(V.memset(r1[:, :, NE:NE + 1], 0.0))
            own.then(V.scalar_tensor_tensor(r1[:, :, 0:NE], bank[1][:, 0:TT * NE].rearrange("p (t e) -> p t e", t=TT),
                                            1.0, sel[:], op0=ALU.add, op1=ALU.mult))
            dve.wait_ge(gates_ready, 1)

            def pick(expert):
                for tt in range(TT):
                    last = V.tensor_scalar(onehot[:, tt, :], iota[:], r1[:, tt, bass.ds(expert, 1)], None, ALU.is_equal)
                    if tt == 0:
                        own.then(last)
                last.then_inc(onehot_ready, 1)

            dve.wait_ge(logits_done, 1)
            pick(0)
            own.then(V.tensor_reduce(small[:, 0:1], bank[1][:, 64:64 + NE], AX.X, ALU.max))
            V.tensor_copy(most[:], small[:, 0:1]).then_inc(most_ready, 1)
            V.memset(yT[:], 0.0)
            own.then(V.memset(backT[:], 0.0))
            dve.wait_ge(seed_done, 1)
            own.then(V.tensor_tensor(yT[:, :, 0:NE], bank[3][:, 0:KT * NE].rearrange("p (k e) -> p k e", k=KT),
                                     mod[:, M_G2:M_G2 + 8].unsqueeze(2).to_broadcast([P, KT, NE]), ALU.mult))
            V.tensor_copy(small[:, 1:2], small[:, 0:1]).then_inc(yT_ready, 1)

            def split(b0):
                return [bank[b0 + h][:, 0:HB].rearrange("p (k s) -> p k s", k=4) for h in range(2)]

            def halves(t):
                return [t[:, 4 * h:4 * h + 4, :] for h in range(2)]

            def wide(t):
                return t.unsqueeze(2).to_broadcast([P, 4, CAP])

            def take(taken):
                dve.wait_ge(taken_done, taken)
                for h, (src, dst) in enumerate(zip(split(6), halves(xT))):
                    own.then(V.tensor_tensor(dst, src, wide(a2[:, 4 * h:4 * h + 4]), ALU.mult))
                    last = V.tensor_tensor(dst, dst, wide(mod[:, M_SH2 + 4 * h:M_SH2 + 4 * h + 4]), ALU.add)
                    if h == 0:
                        own.then(last)
                last.then_inc(xTe_ready, 1)

            def add_given(given):
                for n in range(4):
                    tt, half = n // 2, n % 2
                    cols = slice(half * 512, (half + 1) * 512)
                    dve.wait_ge(given_done, given * 4 + (n + 1))
                    V.tensor_tensor(xres[:, tt, cols], xres[:, tt, cols], bank[(6, 7, 4, 5)[n]][:, :], ALU.add
                                    ).then_inc(given_added, 1)

            def expert(e, given, n):
                dve.wait_ge(back_ready, e + 1)
                for tt in range(TT):
                    last = V.tensor_scalar(gated[:, tt, :], iota[:], r1[:, tt, bass.ds(n, 1)],
                                           gates[:, tt, bass.ds(n, 1)], ALU.is_equal, ALU.mult)
                    if tt == 0:
                        own.then(last)
                last.then_inc(gated_ready, 1)
                pick(n + 1)
                add_given(given)
                dve.wait_ge(g_done, e + 1)
                for h, (src, dst) in enumerate(zip(split(0), halves(g_sb))):
                    own.then(V.tensor_tensor(dst, src, wide(bgu[:, bass.ds(n, 1), 4 * h:4 * h + 4]
                                                            .rearrange("p a r -> p (a r)")), ALU.add))
                V.tensor_scalar(g_sb, g_sb, LIMIT, None, ALU.min).then_inc(gmin_ready, 1)
                dve.wait_ge(gu_used, e * 8 + 8)
                for h, (src, dst) in enumerate(zip(split(2), halves(u_sb))):
                    last = V.tensor_tensor(dst, src, wide(bgu[:, bass.ds(n, 1), 8 + 4 * h:12 + 4 * h]
                                                          .rearrange("p a r -> p (a r)")), ALU.add)
                    if h == 0:
                        own.then(last)
                last.then_inc(gu_read, 1)
                dve.wait_ge(gu_read, e + 2)
                own.then(V.tensor_scalar(u_sb, u_sb, LIMIT, -LIMIT, ALU.min, ALU.max))
                dve.wait_ge(gmin_ready, e + 1)
                own.then(V.scalar_tensor_tensor(u_sb, u_sb, 1.0, g_sb, op0=ALU.add, op1=ALU.mult))
                dve.wait_ge(sig_ready, e + 1)
                V.tensor_tensor(act_sb, u_sb, sig, ALU.mult).then_inc(act_ready, 1)
                take(given + 2)
                dve.wait_ge(down_used, e * 4 + 4)
                for h, (src, dst) in enumerate(zip(split(4), halves(yT))):
                    last = V.tensor_tensor(dst, src, wide(mod[:, M_G2 + 4 * h:M_G2 + 4 * h + 4]), ALU.mult)
                    if h == 0:
                        own.then(last)
                last.then_inc(yT_ready, 1)

            PER = 1 + 1 + 2 + 1 + 1 + 1 + 3 + 1
            take(1)
            dve.wait_ge(back_ready, 1)
            V.tensor_copy(small[:, 2:3], small[:, 0:1]).then_inc(gu_read, 1)
            start = own.steps
            with dve.Fori(0, PAIRS) as n:
                for half in range(2):
                    own.start_at(n * (2 * PER) + (start + PER * half))
                    expert(n * 2 + half, n * 2 + half, n * 2 + half)
                    assert own.steps == PER
            own.start_at(start + NE * PER)
            add_given(NE)
            dve.wait_ge(most_ready, 1)
            count = dve.value_load(most[0:1, 0:1], min_val=0, max_val=T)
            AGAIN = 3 + 1 + 3
            ROUND = AGAIN + NE * PER
            start = own.base
            with dve.Fori(1, PASSES) as p:
                with dve.If(count > p * CAP):
                    own.start_at(p * ROUND + (start - ROUND))
                    own.then(V.tensor_scalar(r1[:], r1[:], -float(CAP), None, ALU.add))
                    own.then(V.memset(yT[:], 0.0))
                    dve.wait_ge(taken_done, p * (NE + 1))
                    pick(0)
                    own.then(V.tensor_copy(small[:, 2:3], small[:, 0:1]))
                    V.tensor_copy(small[:, 1:2], small[:, 0:1]).then_inc(yT_ready, 1)
                    take(p * (NE + 1) + 1)
                    assert own.steps == AGAIN
                    with dve.Fori(0, PAIRS) as n:
                        for half in range(2):
                            own.start_at(p * ROUND + n * (2 * PER) + (start - ROUND + AGAIN + PER * half))
                            expert(p * NE + n * 2 + half, p * (NE + 1) + n * 2 + half, n * 2 + half)
                    add_given(p * (NE + 1) + NE)

            dve.drain().then_inc(sum_ready, 1)
            dve.wait_ge(sq_done, 6)
            V.tensor_scalar(stat[:, 2:4], stat[:, 0:2], 1.0 / D, EPS, ALU.mult, ALU.add).then_inc(ms_ready, 1)
            dve.wait_ge(root_ready, 4)
            V.reciprocal(stat[:, 6:8], stat[:, 4:6]).then_inc(ms_ready, 1)
            dve.wait_ge(ms_ready, 5)
            dve.wait_ge(fg_in, 16)
            for tt in range(TT):
                V.scalar_tensor_tensor(xn[:, tt, :], xres[:, tt, :], stat[:, 6 + tt:7 + tt], fgb[:],
                                       op0=ALU.mult, op1=ALU.mult).then_inc(out_ready, 1)

        @block.tensor
        def _(pe):
            M = nc.tensor.matmul

            pe.wait_ge(consts, 2)
            pe.wait_ge(small_in, 9 * 16)
            nc.tensor.transpose(bank[7][:, 0:R_END], vt, ident[0:R_END, 0:R_END]).then_inc(vecT_done, 1)
            pe.wait_ge(bgu_in, 16)
            for a in range(4):
                last = nc.tensor.transpose(bank[6][:, a * P:(a + 1) * P], bgu_rows[:, a, :], ident[:])
            last.then_inc(bgu_done, 1)
            pe.wait_ge(vec_ready, 2)
            for n in range(2):
                last = M(bank[(7, 4)[n]][:, 256:257], ones[64 * n:64 * n + 64, :], lam[64 * n:64 * n + 64, 3:4],
                         start=True, stop=True)
            last.then_inc(lam_done, 1)

            def transpose_rows(b0):
                for kt in range(KT):
                    for tt in range(TT):
                        last = nc.tensor.transpose(bank[b0 + kt // 2][:, (kt % 2) * T + tt * P:(kt % 2) * T + (tt + 1) * P],
                                                   xn[:, tt, kt * P:(kt + 1) * P], ident[:])
                    if kt % 2:
                        last.then_inc(xT_done, 1)

            pe.wait_ge(xn_ready, 2)
            transpose_rows(0)

            def ada_group(g, group):
                for h in range(2):
                    wait_group(pe, group, h)
                for blk in range(4):
                    for kt in range(KT):
                        last = M(bank[5][:, 4 * g + blk:4 * g + blk + 1],
                                 group_chunk(group, kt // 4)[:, kt % 4, blk * P:(blk + 1) * P],
                                 vec[:, R_C + kt:R_C + kt + 1], start=kt == 0, stop=kt == KT - 1)
                last.then_inc(groups_used, 1)
                return last

            for g in range(GROUPS_ADA1):
                ada_group(g, g)

            with pe.Fori(0, 2) as it:
                for g in range(8):
                    group = GROUPS_ADA1 + g
                    for h in range(2):
                        wait_group(pe, group, h, loops=it * 2)
                    for h in range(2):
                        pe.wait_ge(emptied, it * 16 + (2 * g + h + 5))
                        if g == 0 and h == 0:
                            pe.wait_ge(emptied, 8)
                        dst = bank[2 * (g % 2) + h]
                        if g in (4, 5):
                            for kt in range(KT):
                                last = M(dst[:, :], hT[:, kt, h * P:(h + 1) * P], group_chunk(group, kt // 4)[:, kt % 4, :],
                                         start=kt == 0, stop=kt == KT - 1)
                        else:
                            for b in range(2):
                                cols = slice((2 * h + b) * P, (2 * h + b + 1) * P)
                                for kt in range(KT):
                                    last = M(dst[:, b * T:(b + 1) * T], group_chunk(group, kt // 4)[:, kt % 4, cols],
                                             hT[:, kt, :], start=kt == 0, stop=kt == KT - 1)
                        last.then_inc(groups_used if h else proj_done, 1)

            pe.wait_ge(emptied, 8 + 32)
            for s in range(DAH + 2):
                if s < DAH:
                    part, blk = slice(64 * (s % 2), 64 * (s % 2) + 64), s // 2
                    if s >= 2:
                        pe.wait_ge(scores_ready, 2 * (s - 1))
                    for m in range(2):
                        q = qkT[part, 0, 4 * m + blk, :]
                        k = qkT[part, 0, 8 + 4 * m + blk, :]
                        dst = bank[2 * (s % 2) + m]
                        M(dst[:, 0:128], q[:, 0:P], k[:, 0:P], start=True, stop=True)
                        M(dst[:, 128:384], q[:, P:T], k, start=True, stop=True).then_inc(scores_done, 1)
                    ada_group(GROUPS_ADA1 + s, GROUPS_ADA1 + GROUPS_IN + s)
                if 1 <= s <= DAH:
                    h = s - 1
                    pe.wait_ge(w_ready, h + 1)
                    if h >= 1:
                        pe.wait_ge(wT_ready, h)
                    for n in range(3):
                        last = nc.tensor.transpose(bank[4][:, n * P:(n + 1) * P], da_w[:, h % 2, n * P:(n + 1) * P], ident[:])
                    last.then_inc(wT_done, 1)
                if s >= 2:
                    h = s - 2
                    pe.wait_ge(wT_ready, h + 1)
                    if h >= 2:
                        pe.wait_ge(pv_read, h - 1)
                    dst, wt = bank[6 + h % 2], da_wT[:, h % 2, :]
                    cols = slice(h * P, (h + 1) * P)
                    M(dst[:, 0:128], wt[:, 0:P], v_sb[:, 0, 0, cols], start=True, stop=True)
                    M(dst[:, 128:256], wt[:, P:2 * P], v_sb[:, 0, 0, cols], start=True, stop=False)
                    M(dst[:, 128:256], wt[:, 2 * P:3 * P], v_sb[:, 0, 1, cols], start=False, stop=True).then_inc(pv_done, 1)

            pe.wait_ge(scores_ready, 2 * DAH)
            pe.wait_ge(pv_read, DAH)
            for s in range(SBH + 4):
                if s < SBH:
                    part, blk = slice(64 * (s % 2), 64 * (s % 2) + 64), s // 2
                    if s == 3:
                        pe.wait_ge(mod_ready, 2)
                    if s >= 4:
                        pe.wait_ge(sbw_ready, s - 3)
                    q, k = qkT[part, 1, blk, :], qkT[part, 1, 8 + blk, :]
                    z = bank[(0, 1, 2, 5)[s % 4]]
                    M(z[:, 0:256], k[:, 0:P], q, start=True, stop=False, skip_group_check=True)
                    M(z[:, 256:384], k[:, P:T], q[:, P:T], start=False, stop=False, skip_group_check=True
                      ).then_inc(z_done, 1)
                if 2 <= s < SBH + 2:
                    h = s - 2
                    z, l = bank[(0, 1, 2, 5)[h % 4]], sb_l[:, h % 3, :]
                    pe.wait_ge(splus_masked, h + 1)
                    M(z[:, 0:256], neg_tri[:], l[:, 0:256], start=False, stop=False, skip_group_check=True)
                    M(z[:, 128:256], neg_ones[:], l[:, 256:384], start=False, stop=False, skip_group_check=True)
                    M(z[:, 256:384], neg_tri[:], l[:, 256:384], start=False, stop=True, skip_group_check=True
                      ).then_inc(logw_done, 1)
                if 4 <= s:
                    h = s - 4
                    pe.wait_ge(sbw_masked, h + 1)
                    if h >= 4 and h % 2 == 0:
                        pe.wait_ge(obT_ready, h // 2 - 1)
                    dst = bank[6 + (h // 2) % 2][64 * (h % 2):64 * (h % 2) + 64, :]
                    a, cols = sb_a[:, h % 3, :], slice(h * DH, (h + 1) * DH)
                    M(dst[:, 0:256], v_sb[:, 1, 0, cols], a[:, 0:256], start=True, stop=False, skip_group_check=True)
                    M(dst[:, 128:256], v_sb[:, 1, 1, cols], a[:, 256:384], start=False, stop=True, skip_group_check=True
                      ).then_inc(sbpv_done, 1)
                if 3 <= s < 7:
                    n = s - 3
                    if n == 0:
                        pe.wait_ge(oa_ready, 1)
                        pe.wait_ge(wT_ready, DAH)
                    if n >= 2:
                        pe.wait_ge(oaT_ready, n - 1)
                    for j in range(4):
                        kt, tt = 2 * n + j // 2, j % 2
                        last = nc.tensor.transpose(bank[3 + n % 2][:, j * P:(j + 1) * P], oa[:, tt, kt * P:(kt + 1) * P], ident[:])
                    last.then_inc(oaT_done, 1)
                if s in (7, 8):
                    n = s - 7
                    pe.wait_ge(oaT_ready, 3 + n)
                    pe.wait_ge(diag_ready, 4 * n + 4)
                    for j in range(4):
                        last = M(bank[3 + n][:, j * P:(j + 1) * P], ones[:], g1diag[:, 4 * n + j, :], start=True, stop=True)
                    last.then_inc(g1b_done, 1)

            g0 = GROUPS_ADA1 + GROUPS_IN + GROUPS_ADA2
            pe.wait_ge(sbw_ready, SBH)
            pe.wait_ge(g1b_ready, 2)
            for n in range(4):
                src = oaT if n % 2 == 0 else obT
                if n == 1:
                    pe.wait_ge(obT_ready, SBH // 2)
                for h in range(2):
                    wait_group(pe, g0 + n, h)
                for blk in range(4):
                    for kt in range(KT):
                        last = M(bank[2 * n + blk // 2][:, (blk % 2) * T:(blk % 2 + 1) * T],
                                 group_chunk(g0 + n, kt // 4)[:, kt % 4, blk * P:(blk + 1) * P], src[:, kt, :],
                                 start=kt == 0, stop=kt == KT - 1)
                    if blk % 2 == 1:
                        last.then_inc(groups_used if blk == 3 else branch_done, 1)
            pe.wait_ge(merged_ready, 4)
            for half in range(2):
                for h in range(2):
                    wait_group(pe, g0 + 4 + half, h)
                for tt in range(TT):
                    for kt in range(KT):
                        last = M(bank[2 * half + tt][:, :], mergedT[:, kt, tt * P:(tt + 1) * P],
                                 group_chunk(g0 + 4 + half, kt // 4)[:, kt % 4, :], start=kt == 0, stop=kt == KT - 1)
                    last.then_inc(groups_used if tt else mixed_done, 1)

            pe.wait_ge(xn_ready, 4)
            transpose_rows(4)
            pe.wait_ge(h2T_even, KT // 2)
            pe.wait_ge(h2T_odd, KT // 2)
            pe.wait_ge(router_in, 32)
            pe.wait_ge(x1_ready, 4)
            for tt in range(TT):
                dst = bank[0][:, tt * NE:(tt + 1) * NE]
                for kt in range(KT):
                    M(dst, h2T[:, kt, tt * P:(tt + 1) * P], rw_sb[:, kt, :], start=kt == 0, stop=False)
                last = M(dst, ones[0:1, :], rb_sb[:], start=False, stop=True)
            last.then_inc(logits_done, 1)
            pe.wait_ge(bdown_in, 16)
            for kt in range(KT):
                last = nc.tensor.transpose(bank[3][:, kt * NE:(kt + 1) * NE], y_rows[:, kt * P:(kt + 1) * P],
                                           ident[0:NE, 0:NE])
            last.then_inc(seed_done, 1)
            pe.wait_ge(sel_ready, 2)
            M(bank[1][:, 0:NE], before[:], sel[:, 0, :], start=True, stop=True)
            M(bank[1][:, NE:2 * NE], ones[:], sel[:, 0, :], start=True, stop=False)
            M(bank[1][:, NE:2 * NE], before[:], sel[:, 1, :], start=False, stop=True)
            M(bank[1][:, 2 * NE:3 * NE], ones[:], sel[:, 0, :], start=True, stop=False)
            M(bank[1][:, 2 * NE:3 * NE], ones[:], sel[:, 1, :], start=False, stop=True).then_inc(rank_done, 1)
            pe.wait_ge(gates_ready, 1)
            for tt in range(TT):
                last = nc.tensor.transpose(bank[2][0:NE, tt * P:(tt + 1) * P], gates[:, tt, :], ident[:])
            last.then_inc(seed_done, 1)

            def take(picked):
                pe.wait_ge(onehot_ready, picked)
                for kt in range(KT):
                    dst = bank[6 + kt // 4][:, (kt % 4) * CAP:(kt % 4 + 1) * CAP]
                    for tt in range(TT):
                        last = M(dst, xn[:, tt, kt * P:(kt + 1) * P], onehot[:, tt, :], start=tt == 0, stop=tt == TT - 1)
                last.then_inc(taken_done, 1)

            def y_back(given):
                pe.wait_ge(yT_ready, given + 1)
                for kt in range(KT):
                    last = nc.tensor.transpose(bank[6 + kt // 4][0:CAP, (kt % 4) * P:(kt % 4 + 1) * P], yT[:, kt, :], ident[:])
                    if kt % 4 == 3:
                        last.then_inc(y_done, 1)

            def give(given, back):
                pe.wait_ge(y_ready, given * 2 + 2)
                pe.wait_ge(back_ready, back)
                for n in range(4):
                    tt, half = n // 2, n % 2
                    M(bank[(6, 7, 4, 5)[n]][:, :], backT[0:CAP, tt * P:(tt + 1) * P],
                      y_sb[0:CAP, half * 512:(half + 1) * 512], start=True, stop=True).then_inc(given_done, 1)

            def expert(e, given, half, fills):
                pe.wait_ge(xTe_ready, given + 1)
                pe.wait_ge(gu_read, e + 1)
                for kt in range(KT):
                    pe.wait_ge(slot_in[8 * half + kt], fills * 16 + 16 * USES[8 * half + kt])
                    for f in range(16):
                        last = M(bank[f // 4][:, (f % 4) * CAP:(f % 4 + 1) * CAP],
                                 gu_ring[:, 8 * half + kt, f * P:(f + 1) * P], xT[:, kt, :],
                                 start=kt == 0 and f % 4 == 0, stop=kt == KT - 1, skip_group_check=True)
                        if kt == KT - 1 and f == 7:
                            last.then_inc(g_done, 1)
                    last.then_inc(gu_used, 1)
                    if kt == 1:
                        y_back(given)
                    if kt == 4:
                        give(given, e + 1)
                pe.wait_ge(given_added, given * 4 + 4)
                take(given + 2)
                pe.wait_ge(gated_ready, e + 1)
                for tt in range(TT):
                    last = nc.tensor.transpose(bank[4][0:CAP, tt * P:(tt + 1) * P], gated[:, tt, :], ident[:])
                last.then_inc(back_done, 1)
                pe.wait_ge(act_ready, e + 1)
                pe.wait_ge(back_ready, e + 2)
                for kt in range(KT):
                    if kt % 2 == 0:
                        pe.wait_ge(down_in[kt // 2], e * 16 + 16)
                    for f in range(KT):
                        last = M(bank[4 + f // 4][:, (f % 4) * CAP:(f % 4 + 1) * CAP],
                                 down_ring[:, kt // 2, (kt % 2) * D + f * P:(kt % 2) * D + (f + 1) * P], act_sb[:, kt, :],
                                 start=kt == 0 and f % 4 == 0, stop=kt == KT - 1, skip_group_check=True)
                    if kt % 2 == 1:
                        last.then_inc(down_used, 1)

            take(1)
            with pe.Fori(0, PAIRS) as n:
                for half in range(2):
                    expert(n * 2 + half, n * 2 + half, half, n + 1)
            y_back(NE)
            give(NE, NE + 1)
            pe.wait_ge(most_ready, 1)
            count = pe.value_load(most[0:1, 0:1], min_val=0, max_val=T)
            with pe.Fori(1, PASSES) as p:
                with pe.If(count > p * CAP):
                    pe.wait_ge(given_added, p * (4 * (NE + 1)))
                    take(p * (NE + 1) + 1)
                    with pe.Fori(0, PAIRS) as n:
                        for half in range(2):
                            expert(p * NE + n * 2 + half, p * (NE + 1) + n * 2 + half, half, p * PAIRS + n + 1)
                    y_back(p * (NE + 1) + NE)
                    give(p * (NE + 1) + NE, p * NE + NE + 1)


_INS = ["x", "c", "w_ada", "b_ada", "norm1_g", "w_in", "lam_q1", "lam_k1", "lam_q2", "lam_k2", "subln_g", "w_pa", "w_pb",
        "w_o", "norm2_g", "router_w", "router_b", "w_gu", "b_gu", "w_down", "b_down", "final_g"]


def kernel(**inputs):
    import concourse.bacc as bacc
    from concourse.bass_utils import run_bass_kernel_spmd

    nc = bacc.Bacc("TRN2", target_bir_lowering=False, num_devices=1)
    arrays, args = {}, []
    for name in _INS:
        a = np.ascontiguousarray(inputs[name])
        arrays[f"in_{name}"] = a
        args.append(nc.dram_tensor(f"in_{name}", a.shape, mybir.dt.from_np(a.dtype), kind="ExternalInput").ap())
    args.append(nc.dram_tensor("out", (1, T, D), F32, kind="ExternalOutput").ap())
    build(nc, *args)
    return run_bass_kernel_spmd(nc, [arrays], core_ids=[0]).results[0]["out"]
```

```python
import math
from contextlib import ExitStack

import concourse.bass as bass
import numpy as np
from concourse import mybir

F32 = mybir.dt.float32
I32 = mybir.dt.int32
ALU = mybir.AluOpType
ACT = mybir.ActivationFunctionType
AX = mybir.AxisListType

P = 128
D = 1024
T = 256
KT = D // P
TT = T // P
DH = 64
DAH, SBH = 8, 16
CHUNKMASK = 64
NE, TOPK = 32, 4
EPS = 1e-6
LAM_INIT = 0.8 - 0.6 * math.exp(-0.3 * 0)
FAR = 1e30
LIMIT, ALPHA = 7.0, 1.702

CW = 512
GROUPS_ADA1 = 4
GROUPS_IN = 16
GROUPS_ADA2 = 8
CAP = 64
BLOCKS = T // CAP
EXTRA = 16
ITEMS = NE + EXTRA
PAIRS = NE // 2
G_BRANCH = GROUPS_ADA1 + GROUPS_IN + GROUPS_ADA2

R_C, R_N1, R_N2, R_ADA, R_SUB, R_LQ, R_LK, R_END = 0, 8, 16, 24, 72, 73, 74, 75
M_SH1, M_SC1, M_G1, M_SH2, M_SC2, M_G2 = (8 * n for n in range(6))


class Order:

    def __init__(self, engine, sem):
        self.engine, self.sem, self.base, self.steps = engine, sem, 0, 0

    def then(self, instruction):
        instruction.then_inc(self.sem, 1)
        self.steps += 1
        self.engine.wait_ge(self.sem, self.base + self.steps)

    def start_at(self, base):
        self.base, self.steps = base, 0


def build(nc, x, c, w_ada, b_ada, norm1_g, w_in, lam_q1, lam_k1, lam_q2, lam_k2, subln_g, w_pa, w_pb, w_o,
          norm2_g, router_w, router_b, w_gu, b_gu, w_down, b_down, final_g, out):
    ctx = ExitStack()
    with ctx:
        def sb(name, shape, dt=F32):
            return ctx.enter_context(nc.sbuf_tensor(name, shape, dt))

        def sem(name):
            return ctx.enter_context(nc.semaphore(name))

        gu_ring = sb("gu_ring", [P, 16, 2048])
        down_ring = sb("down_ring", [P, 4, 2048])
        qkT = down_ring[:, :, :].rearrange("p s n -> p (s n)").rearrange("p (i b t) -> p i b t", i=2, b=16)
        v_sb = gu_ring[:, 8:10, :].rearrange("p i (t n) -> p i t n", t=TT)
        hT = gu_ring[:, 10, :].rearrange("p (k t) -> p k t", k=KT)
        g1b = gu_ring[:, 10, 0:D]
        g1diag = gu_ring[:, 10, D:2 * D].rearrange("p (k n) -> p k n", k=KT)
        gateT = gu_ring[:, 11:13, :].rearrange("p i (k t) -> p i k t", k=KT)
        oaT = gu_ring[:, 13, :].rearrange("p (k t) -> p k t", k=KT)
        obT = gu_ring[:, 14, :].rearrange("p (k t) -> p k t", k=KT)
        da_w = gu_ring[:, 14, 0:768].rearrange("p (b n) -> p b n", b=2)
        da_wT = gu_ring[:, 14, 768:1536].rearrange("p (b n) -> p b n", b=2)
        mergedT = gu_ring[:, 15, :].rearrange("p (k t) -> p k t", k=KT)
        oa = gu_ring[:, 15, :].rearrange("p (t n) -> p t n", t=TT)

        xres = sb("xres", [P, TT, D])
        xn = sb("xn", [P, TT, D])
        scratch = sb("scratch", [P, 5120])
        at = [0]

        def part(n):
            at[0] += n
            assert at[0] <= 5120
            return scratch[:, at[0] - n:at[0]]

        da_s = part(4 * 384).rearrange("p (b m n) -> p b m n", b=2, m=2)
        sb_t = part(2 * 384).rearrange("p (b n) -> p b n", b=2)
        sb_l = part(3 * 384).rearrange("p (b n) -> p b n", b=3)
        sb_a = part(3 * 384).rearrange("p (b n) -> p b n", b=3)
        dist = part(384)
        h2T = scratch[:, 0:2048].rearrange("p (k t) -> p k t", k=KT)
        tmp = scratch[:, 2048:3072].rearrange("p (b n) -> p b n", b=2)
        at[0] = 0
        xT = part(512).rearrange("p (j a s) -> p j a s", j=4, a=2)
        g_sb = part(512).rearrange("p (j a s) -> p j a s", j=4, a=2)
        sig = part(512).rearrange("p (j a s) -> p j a s", j=4, a=2)
        u_sb = part(512).rearrange("p (j a s) -> p j a s", j=4, a=2)
        act_sb = part(512).rearrange("p (j a s) -> p j a s", j=4, a=2)
        x_raw, g_raw, u_raw, y_sb, g2b = part(512), part(512), part(512), part(512), part(512)
        lg, r_a, r_b = (scratch[:, 3072 + 64 * n:3136 + 64 * n].rearrange("p (t e) -> p t e", t=TT)
                        for n in range(3))
        tables = u_raw[0:NE, :].rearrange("p (a t) -> p a t", a=2)

        ident = sb("ident", [P, P])
        ones = sb("ones", [P, P])
        neg_ones = sb("neg_ones", [P, P])
        neg_tri = sb("neg_tri", [P, P])
        before = sb("before", [P, P])
        iota = sb("iota", [P, CAP])
        number = sb("number", [P, 1])
        onehot = sb("onehot", [P, TT, CAP])
        gated = sb("gated", [P, TT, 2, CAP])
        back = sb("back", [P, T])
        vec = sb("vec", [P, R_END])
        bgu = sb("bgu", [P, NE, 16])
        mod = sb("mod", [P, 48])
        a1 = sb("a1", [P, KT])
        a2 = sb("a2", [P, KT])
        lam = sb("lam", [P, 4])
        nsub = sb("nsub", [P, 1])
        stat = sb("stat", [P, 8])
        smax = sb("smax", [P, 2, 4])
        ssum = sb("ssum", [P, 2, 4])
        srec = sb("srec", [P, 2, 4])
        osq = sb("osq", [P, 16])
        rw_sb = sb("rw_sb", [P, KT, NE])
        rb_sb = sb("rb_sb", [1, NE])
        top8 = sb("top8", [P, TT, 8])
        r1 = sb("r1", [P, TT, ITEMS + 1])
        sel = sb("sel", [P, TT, NE])
        gates = sb("gates", [P, TT, ITEMS])
        over = sb("over", [NE, 4])
        place = sb("place", [NE, 4])
        item_of = sb("item_of", [NE, 5, EXTRA])
        ids_f = sb("ids_f", [1, EXTRA + 1])
        ids = sb("ids", [1, EXTRA + 1], I32)
        small = sb("small", [P, 8])
        vt = xn[0:R_END, 0, 0:P]
        fgb = xn[:, 0, :]
        bgu_rows = xn[:, 1, 0:512].rearrange("p (a f) -> p a f", a=4)

        bank = [ctx.enter_context(nc.psum_tensor(f"bank{n}", [P, 512], F32)) for n in range(8)]

        slot_in = [sem(f"slot_in{n}") for n in range(16)]
        down_in = [sem(f"down_in{n}") for n in range(4)]
        small_in = sem("small_in")
        bgu_in = sem("bgu_in")
        x_in = sem("x_in")
        router_in = sem("router_in")
        bdown_in = sem("bdown_in")
        fg_in = sem("fg_in")
        out_done = sem("out_done")
        groups_used = sem("groups_used")
        gu_used = sem("gu_used")
        down_used = sem("down_used")
        consts = sem("consts")
        pool_own = sem("pool_own")
        dist_abs = sem("dist_abs")
        vecT_done = sem("vecT_done")
        vec_ready = sem("vec_ready")
        lam_done = sem("lam_done")
        lam_exp = sem("lam_exp")
        sq_done = sem("sq_done")
        ms_ready = sem("ms_ready")
        root_ready = sem("root_ready")
        xn_ready = sem("xn_ready")
        xT_done = sem("xT_done")
        mod_ready = sem("mod_ready")
        emptied = sem("emptied")
        proj_done = sem("proj_done")
        scores_done = sem("scores_done")
        scores_ready = sem("scores_ready")
        max_ready = sem("max_ready")
        exp_ready = sem("exp_ready")
        w_ready = sem("w_ready")
        wT_done = sem("wT_done")
        wT_ready = sem("wT_ready")
        pv_done = sem("pv_done")
        pv_read = sem("pv_read")
        oa_ready = sem("oa_ready")
        oaT_done = sem("oaT_done")
        oaT_ready = sem("oaT_ready")
        diag_ready = sem("diag_ready")
        g1b_done = sem("g1b_done")
        g1b_ready = sem("g1b_ready")
        z_done = sem("z_done")
        absz_ready = sem("absz_ready")
        ln_ready = sem("ln_ready")
        splus_ready = sem("splus_ready")
        splus_masked = sem("splus_masked")
        logw_done = sem("logw_done")
        sbw_ready = sem("sbw_ready")
        sbw_masked = sem("sbw_masked")
        sbpv_done = sem("sbpv_done")
        obT_ready = sem("obT_ready")
        branch_done = sem("branch_done")
        merged_ready = sem("merged_ready")
        mixed_done = sem("mixed_done")
        x1_ready = sem("x1_ready")
        h2T_even = sem("h2T_even")
        h2T_odd = sem("h2T_odd")
        logits_done = sem("logits_done")
        top_ready = sem("top_ready")
        gexp_ready = sem("gexp_ready")
        sel_ready = sem("sel_ready")
        rank_done = sem("rank_done")
        counts_done = sem("counts_done")
        over_ready = sem("over_ready")
        place_done = sem("place_done")
        tablesT_done = sem("tablesT_done")
        tables_ready = sem("tables_ready")
        itemsel_ready = sem("itemsel_ready")
        items_done = sem("items_done")
        items_ready = sem("items_ready")
        gates_ready = sem("gates_ready")
        g2b_done = sem("g2b_done")
        g2b_ready = sem("g2b_ready")
        bgu_done = sem("bgu_done")
        onehot_ready = sem("onehot_ready")
        gated_ready = sem("gated_ready")
        taken_done = sem("taken_done")
        xraw_ready = sem("xraw_ready")
        takenT_done = sem("takenT_done")
        xTe_ready = sem("xTe_ready")
        g_done = sem("g_done")
        raw_ready = sem("raw_ready")
        gT_done = sem("gT_done")
        uT_done = sem("uT_done")
        gmin_ready = sem("gmin_ready")
        sig_ready = sem("sig_ready")
        act_ready = sem("act_ready")
        back_done = sem("back_done")
        back_ready = sem("back_ready")
        y_ready = sem("y_ready")
        given_done = sem("given_done")
        given_added = sem("given_added")
        out_ready = sem("out_ready")
        sum_ready = sem("sum_ready")
        act_own, dve_own = sem("act_own"), sem("dve_own")

        def group_slots(group):
            s = (2 * group + 4) % 8
            return s, s + 1

        def group_chunk(group, h):
            return gu_ring[:, group_slots(group)[h], :].rearrange("p (k n) -> p k n", n=CW)

        def wait_group(eng, group, h, loops=0):
            chunk = 2 * group + h
            eng.wait_ge(slot_in[group_slots(group)[h]], (loops + chunk // 8 + 1) * 16)

        USES = [8] * 4 + [9] * 4 + [0] * 8

        block = ctx.enter_context(nc.Block())

        @block.sync
        def _(sp):
            def load_group(w, col, group, wait=None, loops=0):
                if wait is not None:
                    sp.wait_ge(groups_used, wait)
                for h in range(2):
                    src = w[0, h * 512:(h + 1) * 512, bass.ds(col, CW)].rearrange("(k p) n -> p k n", p=P)
                    sp.dma_start(group_chunk(group, h), src).then_inc(slot_in[group_slots(group)[h]], 16)

            for g in range(GROUPS_ADA1):
                load_group(w_ada, g * CW, g)
            with sp.Fori(0, 2) as it:
                for g in range(8):
                    col = it * 3072 + g * CW if g < 6 else it * 1024 + 6144 + (g - 6) * CW
                    load_group(w_in, col, GROUPS_ADA1 + g, wait=it * 8 + (g + 1))
            g0 = GROUPS_ADA1 + GROUPS_IN
            for g in range(GROUPS_ADA2):
                load_group(w_ada, (GROUPS_ADA1 + g) * CW, g0 + g, wait=g0 + g - 3)
            g0 += GROUPS_ADA2
            for n, (w, half) in enumerate([(w_pa, 0), (w_pb, 0), (w_pa, 1), (w_pb, 1), (w_o, 0), (w_o, 1)]):
                load_group(w, half * CW, g0 + n, wait=g0 + n - 3)

            def load_gu(expert, half, kt):
                sp.dma_start(gu_ring[:, 8 * half + kt, :],
                             w_gu[0, bass.ds(expert, 1), kt * P:(kt + 1) * P, :].rearrange("a p n -> p (a n)")
                             ).then_inc(slot_in[8 * half + kt], 16)

            def load_down(expert, j):
                sp.dma_start(down_ring[:, j, :].rearrange("p (k n) -> p k n", k=2),
                             w_down[0, bass.ds(expert, 1), j * 2 * P:(j + 1) * 2 * P, :]
                             .rearrange("a (k p) n -> p (a k) n", p=P)).then_inc(down_in[j], 16)

            for kt in range(KT):
                if kt % 2 == 0:
                    sp.wait_ge(groups_used, 31 + kt // 2)
                load_gu(0, 0, kt)
            sp.wait_ge(sbpv_done, SBH)
            for half in range(2):
                sp.dma_start(y_sb[64 * half:64 * half + NE, :], b_down[0, :, half * 512:(half + 1) * 512]
                             ).then_inc(bdown_in, 16)
            for j in range(4):
                load_down(0, j)
            for kt in range(KT):
                if kt == 2:
                    sp.wait_ge(x1_ready, 4)
                    sp.wait_ge(g2b_done, 1)
                load_gu(1, 1, kt)
            for j in range(4):
                sp.wait_ge(down_used, j + 1)
                load_down(1, j)

            def load_item(item, expert, half):
                for kt in range(KT):
                    sp.wait_ge(gu_used, item * 8 + (kt - 15))
                    load_gu(expert, half, kt)
                for j in range(4):
                    sp.wait_ge(down_used, item * 4 + (j - 3))
                    load_down(expert, j)

            with sp.Fori(1, PAIRS) as n:
                for half in range(2):
                    load_item(n * 2 + half, n * 2 + half, half)
            sp.wait_ge(items_ready, 1)
            extra = sp.value_load(ids[0:1, EXTRA:EXTRA + 1], min_val=0, max_val=EXTRA)
            with sp.Fori(0, EXTRA // 2) as n:
                for half in range(2):
                    with sp.If(extra > n * 2 + half):
                        expert = sp.value_load(ids[0:1, bass.ds(n * 2 + half, 1)], min_val=0, max_val=NE - 1)
                        load_item(n * 2 + (NE + half), expert, half)
            sp.wait_ge(taken_done, extra + (NE + 1))
            sp.dma_start(fgb, final_g.partition_broadcast(P)).then_inc(fg_in, 16)
            for tt in range(TT):
                sp.wait_ge(out_ready, tt + 1)
                sp.dma_start(out[0, tt * P:(tt + 1) * P, :], xres[:, tt, :]).then_inc(out_done, 16)
            sp.wait_ge(out_done, 16 * TT)

        @block.gpsimd
        def _(pool):
            own = Order(pool, pool_own)

            def tri(m, fill, keep_when, base, step, channel):
                return nc.gpsimd.affine_select(out=m, in_=m, compare_op=keep_when, fill=fill, base=base,
                                               pattern=[[step, P]], channel_multiplier=channel)

            nc.gpsimd.memset(ones[:], 1.0).then_inc(consts, 1)
            own.then(nc.gpsimd.memset(ident[:], 0.0))
            tri(ident[:], 1.0, ALU.not_equal, 0, -1, 1).then_inc(consts, 1)
            nc.gpsimd.iota(dist[:, 0:128], pattern=[[-1, 128]], base=0, channel_multiplier=1,
                           allow_small_or_imprecise_dtypes=True).then_inc(consts, 1)
            nc.gpsimd.iota(dist[:, 128:384], pattern=[[-1, 256]], base=P, channel_multiplier=1,
                           allow_small_or_imprecise_dtypes=True).then_inc(consts, 1)
            nc.gpsimd.iota(iota[:], pattern=[[1, CAP]], base=1, channel_multiplier=0,
                           allow_small_or_imprecise_dtypes=True).then_inc(consts, 1)
            nc.gpsimd.iota(number[:], pattern=[[0, 1]], base=0, channel_multiplier=1,
                           allow_small_or_imprecise_dtypes=True).then_inc(consts, 1)
            nc.gpsimd.memset(neg_ones[:], -1.0).then_inc(consts, 1)
            own.then(nc.gpsimd.memset(neg_tri[:], -1.0))
            tri(neg_tri[:], 0.0, ALU.is_ge, 0, -1, 1).then_inc(consts, 1)
            own.then(nc.gpsimd.memset(before[:], 1.0))
            tri(before[:], 0.0, ALU.is_gt, 0, 1, -1).then_inc(consts, 1)

            def causal(m):
                v = m.rearrange("p (a n) -> p a n", a=3)[:, 0:3:2, :]
                return nc.gpsimd.affine_select(out=v, in_=v, compare_op=ALU.is_gt, fill=0.0, base=0,
                                               pattern=[[0, 2], [1, P]], channel_multiplier=-1)

            for s in range(SBH + 2):
                if s < SBH:
                    pool.wait_ge(splus_ready, s + 1)
                    causal(sb_l[:, s % 3, :]).then_inc(splus_masked, 1)
                if s >= 2:
                    pool.wait_ge(sbw_ready, s - 1)
                    causal(sb_a[:, (s - 2) % 3, :]).then_inc(sbw_masked, 1)

        @block.scalar
        def _(act):
            own = Order(act, act_own)
            A = nc.scalar.activation
            for rows, src in ((slice(R_C, R_N1), c[0, :].rearrange("(r f) -> r f", f=P)),
                              (slice(R_N1, R_N2), norm1_g[0, :].rearrange("(r f) -> r f", f=P)),
                              (slice(R_N2, R_ADA), norm2_g[0, :].rearrange("(r f) -> r f", f=P)),
                              (slice(R_ADA, R_SUB), b_ada[0, :].rearrange("(r f) -> r f", f=P)),
                              (slice(R_SUB, R_LQ), subln_g[0:1, :])):
                act.dma_start(xn[rows, 0, 0:P], src).then_inc(small_in, 16)
            for row, a, b in ((R_LQ, lam_q1, lam_q2), (R_LK, lam_k1, lam_k2)):
                act.dma_start(xn[row:row + 1, 0, 0:DH], a[0:1, :]).then_inc(small_in, 16)
                act.dma_start(xn[row:row + 1, 0, DH:P], b[0:1, :]).then_inc(small_in, 16)
            act.dma_start(xres[:, :, :], x[0, :, :].rearrange("(t p) n -> p t n", p=P)).then_inc(x_in, 16)
            act.dma_start(bgu_rows, b_gu[0, :, :].rearrange("e (r f) -> (e r) f", f=P)
                          .rearrange("(a p) f -> p a f", p=P)).then_inc(bgu_in, 16)
            act.dma_start(rw_sb[:], router_w[0, :, :].rearrange("(k p) e -> p k e", p=P)).then_inc(router_in, 16)
            act.dma_start(rb_sb[:], router_b[0:1, :]).then_inc(router_in, 16)

            act.wait_ge(x_in, 16)
            for tt in range(TT):
                A(hT[:, 4 * tt:4 * tt + 4, :], xres[:, tt, :].rearrange("p (k t) -> p k t", k=4), ACT.Square,
                  accum_out=stat[:, tt:tt + 1]).then_inc(sq_done, 1)
            act.wait_ge(ms_ready, 1)
            A(stat[:, 4:6], stat[:, 2:4], ACT.Sqrt).then_inc(root_ready, 1)
            act.wait_ge(lam_done, 1)
            for n in range(2):
                A(lam[:, n:n + 1], bank[(7, 4)[n]][:, 256:257], ACT.Exp).then_inc(lam_exp, 1)
            act.wait_ge(xT_done, 4)
            act.wait_ge(mod_ready, 1)
            for kt in range(KT):
                A(hT[:, kt, :], bank[kt // 2][:, (kt % 2) * T:(kt % 2 + 1) * T], ACT.Identity,
                  scale=a1[:, kt:kt + 1], bias=mod[:, M_SH1 + kt:M_SH1 + kt + 1]).then_inc(emptied, 1)
            with act.Fori(0, 2) as it:
                for g in range(8):
                    for h in range(2):
                        if h == 0:
                            act.wait_ge(proj_done, it * 8 + (g + 1))
                        else:
                            act.wait_ge(groups_used, it * 8 + (GROUPS_ADA1 + g + 1))
                        src = bank[2 * (g % 2) + h][:, :]
                        if g < 4:
                            dst = qkT[:, bass.ds(it, 1), 4 * g + 2 * h:4 * g + 2 * h + 2, :]
                            A(dst.rearrange("p i b t -> p (i b t)"), src, ACT.Copy,
                              scale=DH ** -0.5 if g < 2 else 1.0).then_inc(emptied, 1)
                        elif g < 6:
                            dst = v_sb[:, bass.ds(it, 1), h, (g - 4) * CW:(g - 3) * CW]
                            A(dst.rearrange("p i n -> p (i n)"), src, ACT.Copy).then_inc(emptied, 1)
                        else:
                            b = 4 * (g - 6) + 2 * h
                            dst = gateT[:, bass.ds(it, 1), b:b + 2, :]
                            A(dst.rearrange("p i k t -> p (i k t)"), src, ACT.Sigmoid).then_inc(emptied, 1)

            for s in range(DAH + 1):
                if s < DAH:
                    for m in range(2):
                        for t in range(TT):
                            act.wait_ge(max_ready, 4 * s + 2 * m + t + 1)
                            span = slice(0, 128) if t == 0 else slice(128, 384)
                            A(da_s[:, s % 2, m, span], da_s[:, s % 2, m, span], ACT.Exp,
                              bias=smax[:, s % 2, 2 * m + t:2 * m + t + 1],
                              accum_out=ssum[:, s % 2, 2 * m + t:2 * m + t + 1]).then_inc(exp_ready, 1)
                if s >= 1:
                    act.wait_ge(wT_done, s)
                    if s >= 3:
                        act.wait_ge(pv_done, s - 2)
                    A(da_wT[:, (s - 1) % 2, :], bank[4][:, 0:384], ACT.Copy).then_inc(wT_ready, 1)
            act.wait_ge(ms_ready, 2)
            A(osq[:], osq[:], ACT.Sqrt).then_inc(root_ready, 1)

            for s in range(SBH + 2):
                if s < SBH:
                    act.wait_ge(absz_ready, s + 1)
                    own.then(A(sb_t[:, s % 2, :], sb_t[:, s % 2, :], ACT.Exp))
                    A(sb_t[:, s % 2, :], sb_t[:, s % 2, :], ACT.Ln, bias=1.0).then_inc(ln_ready, 1)
                if s >= 2:
                    h = s - 2
                    act.wait_ge(logw_done, h + 1)
                    if h >= 3:
                        act.wait_ge(sbpv_done, h - 2)
                    A(sb_a[:, h % 3, :], bank[(0, 1, 2, 5)[h % 4]][:, 0:384], ACT.Exp).then_inc(sbw_ready, 1)
                if 4 <= s < 8:
                    n = s - 4
                    act.wait_ge(oaT_done, n + 1)
                    A(oaT[:, 2 * n:2 * n + 2, :].rearrange("p k t -> p (k t)"), bank[3 + n % 2][:, :], ACT.Copy,
                      scale=nsub[:, 0:1]).then_inc(oaT_ready, 1)
                if s in (8, 9):
                    n = s - 8
                    act.wait_ge(g1b_done, n + 1)
                    A(g1b[:, n * 512:(n + 1) * 512], bank[3 + n][:, :], ACT.Copy).then_inc(g1b_ready, 1)

            act.wait_ge(g2b_done, 1)
            A(g2b, bank[4][:, :], ACT.Copy).then_inc(g2b_ready, 1)
            for tt in range(TT):
                act.wait_ge(x1_ready, tt + 3)
                A(xn[:, tt, :], xres[:, tt, :], ACT.Square, accum_out=stat[:, tt:tt + 1]).then_inc(sq_done, 1)
            act.wait_ge(ms_ready, 3)
            A(stat[:, 4:6], stat[:, 2:4], ACT.Sqrt).then_inc(root_ready, 1)
            for kt in range(0, KT, 2):
                act.wait_ge(xT_done, 5 + kt // 2)
                A(h2T[:, kt, :], bank[4 + kt // 2][:, 0:T], ACT.Identity,
                  scale=a2[:, kt:kt + 1], bias=mod[:, M_SH2 + kt:M_SH2 + kt + 1]).then_inc(h2T_even, 1)
            act.wait_ge(top_ready, 1)
            for tt in range(TT):
                A(r_b[:, tt, :], lg[:, tt, :], ACT.Exp, bias=small[:, tt:tt + 1]).then_inc(gexp_ready, 1)
            def copy_back(item):
                act.wait_ge(back_done, item + 2)
                A(back[:], bank[5][:, 0:T], ACT.Copy).then_inc(back_ready, 1)

            def copy_taken(item):
                act.wait_ge(taken_done, item + 1)
                A(x_raw, bank[4][:, :], ACT.Copy).then_inc(xraw_ready, 1)

            def expert(item):
                act.wait_ge(g_done, item + 1)
                A(g_raw, bank[0][:, :], ACT.Copy).then_inc(raw_ready, 1)
                act.wait_ge(gu_used, item * 8 + 8)
                A(u_raw, bank[1][:, :], ACT.Copy).then_inc(raw_ready, 1)
                copy_taken(item + 1)
                copy_back(item)
                act.wait_ge(gmin_ready, item + 1)
                A(sig, g_sb, ACT.Sigmoid, scale=ALPHA).then_inc(sig_ready, 1)

            copy_taken(0)
            copy_back(-1)
            act.wait_ge(tablesT_done, 1)
            A(tables.rearrange("p a t -> p (a t)"), bank[2][0:NE, :], ACT.Copy).then_inc(tables_ready, 1)
            act.wait_ge(items_done, 1)
            with act.Fori(0, PAIRS) as n:
                for half in range(2):
                    expert(n * 2 + half)
            act.wait_ge(items_ready, 1)
            extra = act.value_load(ids[0:1, EXTRA:EXTRA + 1], min_val=0, max_val=EXTRA)
            with act.Fori(0, EXTRA // 2) as n:
                for half in range(2):
                    with act.If(extra > n * 2 + half):
                        expert(n * 2 + (NE + half))

            act.wait_ge(sum_ready, 1)
            for tt in range(TT):
                A(xn[:, 1, :] if tt else scratch[:, 0:D], xres[:, tt, :], ACT.Square, accum_out=stat[:, tt:tt + 1]).then_inc(sq_done, 1)
            act.wait_ge(ms_ready, 4)
            A(stat[:, 4:6], stat[:, 2:4], ACT.Sqrt).then_inc(root_ready, 1)

        @block.vector
        def _(dve):
            own = Order(dve, dve_own)
            V = nc.vector

            def root_mean(n, tiles_done):
                dve.wait_ge(sq_done, 2 * tiles_done)
                V.tensor_scalar(stat[:, 2:4], stat[:, 0:2], 1.0 / D, EPS, ALU.mult, ALU.add).then_inc(ms_ready, 1)
                dve.wait_ge(root_ready, n)
                own.then(V.reciprocal(stat[:, 6:8], stat[:, 4:6]))

            dve.wait_ge(vecT_done, 1)
            V.tensor_copy(vec[:], bank[7][:, 0:R_END]).then_inc(vec_ready, 1)
            dve.wait_ge(vec_ready, 1)
            V.tensor_tensor(lam[:, 3:4], vec[:, R_LQ:R_LQ + 1], vec[:, R_LK:R_LK + 1], ALU.mult).then_inc(vec_ready, 1)
            V.tensor_scalar(nsub[:], vec[:, R_SUB:R_SUB + 1], 1.0 - LAM_INIT, None, ALU.mult).then_inc(vec_ready, 1)
            dve.wait_ge(bgu_done, 1)
            V.tensor_copy(bgu[:].rearrange("p e r -> p (e r)"), bank[6][:, :]).then_inc(vec_ready, 1)
            root_mean(1, 1)
            dve.wait_ge(bgu_done, 1)
            for tt in range(TT):
                V.tensor_scalar(xn[:, tt, :], xres[:, tt, :], stat[:, 6 + tt:7 + tt], None, ALU.mult
                                ).then_inc(xn_ready, 1)
            dve.wait_ge(lam_exp, 2)
            own.then(V.tensor_tensor(lam[:, 2:3], lam[:, 1:2], lam[:, 0:1], ALU.subtract))
            own.then(V.tensor_scalar(lam[:, 2:3], lam[:, 2:3], -LAM_INIT, None, ALU.add))
            dve.wait_ge(consts, 4)
            own.then(V.scalar_tensor_tensor(dist[:], dist[:], -1.0, dist[:], op0=ALU.mult, op1=ALU.max))
            V.memset(dist[0:64, 64:128], FAR)
            own.then(V.memset(dist[0:64, 128 + 192:384], FAR))
            dve.wait_ge(groups_used, GROUPS_ADA1)
            own.then(V.tensor_tensor(mod[:, 0:16], bank[5][:, 0:16], vec[:, R_ADA:R_ADA + 16], ALU.add))
            V.scalar_tensor_tensor(a1[:], mod[:, M_SC1:M_SC1 + 8], 1.0, vec[:, R_N1:R_N1 + 8],
                                   op0=ALU.add, op1=ALU.mult).then_inc(mod_ready, 1)

            SPAN = [slice(0, 128), slice(128, 384)]
            for s in range(DAH + 2):
                if s < DAH:
                    b = s % 2
                    for m in range(2):
                        dve.wait_ge(scores_done, 2 * s + m + 1)
                        if s >= 2 and m == 0:
                            dve.wait_ge(w_ready, s - 1)
                        V.scalar_tensor_tensor(da_s[:, b, m, :], dist[:], -(2.0 ** (-8.0 * (s + 1) / DAH)),
                                               bank[2 * b + m][:, 0:384], op0=ALU.mult, op1=ALU.add
                                               ).then_inc(scores_ready, 1)
                        dve.wait_ge(scores_ready, 2 * s + m + 1)
                        for t in range(TT):
                            V.tensor_reduce(smax[:, b, 2 * m + t:2 * m + t + 1], da_s[:, b, m, SPAN[t]], AX.X,
                                            ALU.max, negate=True).then_inc(max_ready, 1)
                if 1 <= s <= DAH:
                    h, b = s - 1, (s - 1) % 2
                    dve.wait_ge(exp_ready, 4 * h + 4)
                    own.then(V.reciprocal(srec[:, b, :], ssum[:, b, :]))
                    own.then(V.tensor_scalar(srec[:, b, 2:4], srec[:, b, 2:4], lam[:, 2:3], None, ALU.mult))
                    for t in range(TT):
                        V.tensor_scalar(da_s[:, b, 0, SPAN[t]], da_s[:, b, 0, SPAN[t]], srec[:, b, t:t + 1], None,
                                        ALU.mult).then_inc(dve_own, 1)
                        own.steps += 1
                    dve.wait_ge(dve_own, own.base + own.steps)
                    if h >= 2:
                        dve.wait_ge(wT_done, h - 1)
                    for t in range(TT):
                        last = V.scalar_tensor_tensor(da_w[:, b, SPAN[t]], da_s[:, b, 1, SPAN[t]],
                                                      srec[:, b, 2 + t:3 + t], da_s[:, b, 0, SPAN[t]],
                                                      op0=ALU.mult, op1=ALU.add)
                        if t == 0:
                            last.then_inc(dve_own, 1)
                            own.steps += 1
                    last.then_inc(w_ready, 1)
                if s >= 2:
                    h = s - 2
                    dve.wait_ge(pv_done, h + 1)
                    V.tensor_copy(oa[:, :, h * P:(h + 1) * P],
                                  bank[6 + h % 2][:, 0:256].rearrange("p (t n) -> p t n", t=TT)).then_inc(pv_read, 1)
            dve.wait_ge(pv_read, DAH)
            oav = oa.rearrange("p t (h n) -> p (t h) n", n=P)
            sqv = xn[:, :, :].rearrange("p t (h n) -> p (t h) n", n=P)
            dve.wait_ge(xT_done, 4)
            own.then(V.tensor_tensor(sqv, oav, oav, ALU.mult))
            own.then(V.tensor_reduce(osq[:], sqv, AX.X, ALU.add))
            V.tensor_scalar(osq[:], osq[:], 1.0 / (2 * DH), EPS, ALU.mult, ALU.add).then_inc(ms_ready, 1)

            def minus_abs(h):
                z, l = bank[(0, 1, 2, 5)[h % 4]][:, 0:384], sb_l[:, h % 3, :]
                dve.wait_ge(z_done, h + 1)
                if h >= 3:
                    dve.wait_ge(logw_done, h - 2)
                own.then(V.tensor_scalar(l, z, 0.0, None, ALU.max))
                V.scalar_tensor_tensor(sb_t[:, h % 2, :], l, -2.0, z, op0=ALU.mult, op1=ALU.add
                                       ).then_inc(absz_ready, 1)

            def softplus(h):
                dve.wait_ge(ln_ready, h + 1)
                V.tensor_tensor(sb_l[:, h % 3, :], sb_l[:, h % 3, :], sb_t[:, h % 2, :], ALU.add
                                ).then_inc(splus_ready, 1)

            dve.wait_ge(groups_used, GROUPS_ADA1 + GROUPS_IN + GROUPS_ADA2)
            own.then(V.tensor_tensor(mod[:, 16:48], bank[5][:, 16:48], vec[:, R_ADA + 16:R_ADA + 48], ALU.add))
            V.scalar_tensor_tensor(a2[:], mod[:, M_SC2:M_SC2 + 8], 1.0, vec[:, R_N2:R_N2 + 8],
                                   op0=ALU.add, op1=ALU.mult).then_inc(mod_ready, 1)
            minus_abs(0)
            dve.wait_ge(root_ready, 2)
            own.then(V.reciprocal(osq[:], osq[:]))
            V.tensor_tensor(oav, oav, osq[:].unsqueeze(2).to_broadcast([P, 16, P]), ALU.mult).then_inc(oa_ready, 1)
            for kt in range(KT):
                V.tensor_scalar(g1diag[:, kt, :], ident[:], mod[:, M_G1 + kt:M_G1 + kt + 1], None, ALU.mult
                                ).then_inc(diag_ready, 1)
            for s in range(1, SBH + 5):
                if s < SBH:
                    if s >= 2:
                        dve.wait_ge(splus_ready, s - 1)
                    minus_abs(s)
                if s - 1 < SBH:
                    softplus(s - 1)
                if s >= 5 and (s - 5) % 2 == 0 and (s - 5) // 2 < SBH // 2:
                    pair = (s - 5) // 2
                    dve.wait_ge(sbpv_done, 2 * pair + 2)
                    V.tensor_copy(obT[:, pair, :], bank[6 + pair % 2][:, 0:T]).then_inc(obT_ready, 1)

            def wait_bank(first_done, firsts, second, groups):
                if second:
                    dve.wait_ge(groups_used, groups)
                else:
                    dve.wait_ge(first_done, firsts)

            dve.wait_ge(g1b_done, 2)
            for kt in range(KT):
                V.tensor_scalar(g1diag[:, kt, :], ident[:], mod[:, M_G2 + kt:M_G2 + kt + 1], None, ALU.mult
                                ).then_inc(diag_ready, 1)
            for part_ in (slice(32, 64), slice(96, 128)):
                V.memset(y_sb[part_, :], 0.0)
            for half in range(2):
                for n in range(2):
                    blk = slice(4 * half + 2 * n, 4 * half + 2 * n + 2)
                    dst = mergedT[:, blk, :].rearrange("p k t -> p (k t)")
                    wait_bank(branch_done, 2 * half + 1, n, G_BRANCH + 2 * half + 1)
                    own.then(V.tensor_tensor(dst, bank[4 * half + n][:, :],
                                             gateT[:, 0, blk, :].rearrange("p k t -> p (k t)"), ALU.mult))
                for n in range(2):
                    blk = slice(4 * half + 2 * n, 4 * half + 2 * n + 2)
                    dst = mergedT[:, blk, :].rearrange("p k t -> p (k t)")
                    wait_bank(branch_done, 2 * half + 2, n, G_BRANCH + 2 * half + 2)
                    own.then(V.tensor_tensor(tmp[:, n, :], bank[4 * half + 2 + n][:, :],
                                             gateT[:, 1, blk, :].rearrange("p k t -> p (k t)"), ALU.mult))
                    V.tensor_tensor(dst, dst, tmp[:, n, :], ALU.add).then_inc(merged_ready, 1)
            dve.wait_ge(g1b_ready, 2)
            dve.wait_ge(merged_ready, 4)
            for half in range(2):
                for tt in range(TT):
                    n = 2 * half + tt
                    cols = slice(half * 512, (half + 1) * 512)
                    wait_bank(mixed_done, half + 1, tt, G_BRANCH + 4 + half + 1)
                    if n >= 2:
                        dve.wait_ge(x1_ready, n - 1)
                    own.then(V.tensor_tensor(tmp[:, n % 2, :], bank[n][:, :], g1b[:, cols], ALU.mult))
                    V.tensor_tensor(xres[:, tt, cols], xres[:, tt, cols], tmp[:, n % 2, :], ALU.add
                                    ).then_inc(x1_ready, 1)
            dve.wait_ge(sq_done, 4)
            V.tensor_scalar(stat[:, 2:4], stat[:, 0:2], 1.0 / D, EPS, ALU.mult, ALU.add).then_inc(ms_ready, 1)
            dve.wait_ge(root_ready, 3)
            own.then(V.reciprocal(stat[:, 6:8], stat[:, 4:6]))
            for tt in range(TT):
                V.tensor_scalar(xn[:, tt, :], xres[:, tt, :], stat[:, 6 + tt:7 + tt], None, ALU.mult
                                ).then_inc(xn_ready, 1)
            for kt in range(1, KT, 2):
                dve.wait_ge(xT_done, 5 + kt // 2)
                dve.wait_ge(h2T_even, kt // 2 + 1)
                V.tensor_scalar(h2T[:, kt, :], bank[4 + kt // 2][:, T:2 * T], a2[:, kt:kt + 1],
                                mod[:, M_SH2 + kt:M_SH2 + kt + 1], ALU.mult, ALU.add).then_inc(h2T_odd, 1)

            dve.wait_ge(logits_done, 1)
            own.then(V.tensor_copy(lg[:], bank[0][:, 0:TT * NE].rearrange("p (t e) -> p t e", t=TT)))
            for tt in range(TT):
                own.then(V.max(top8[:, tt, :], lg[:, tt, :]))
            V.tensor_scalar(small[:, 0:2], top8[:, :, 0], -1.0, None, ALU.mult).then_inc(top_ready, 1)
            for tt in range(TT):
                fourth = top8[:, tt, TOPK - 1:TOPK]
                own.then(V.tensor_scalar(sel[:, tt, :], lg[:, tt, :], fourth, None, ALU.is_gt))
                own.then(V.tensor_reduce(small[:, 2 + tt:3 + tt], sel[:, tt, :], AX.X, ALU.add))
                own.then(V.tensor_scalar(r_a[:, tt, :], lg[:, tt, :], fourth, None, ALU.is_equal))
                own.then(V.tensor_tensor_scan(r1[:, tt, 0:NE], r_a[:, tt, :], ones[:, 0:NE],
                                              small[:, 2 + tt:3 + tt], op0=ALU.add, op1=ALU.mult))
                own.then(V.scalar_tensor_tensor(r_a[:, tt, :], r1[:, tt, 0:NE], TOPK + 0.5, r_a[:, tt, :],
                                                op0=ALU.is_lt, op1=ALU.mult))
                V.tensor_tensor(sel[:, tt, :], sel[:, tt, :], r_a[:, tt, :], ALU.add).then_inc(sel_ready, 1)
            dve.wait_ge(sel_ready, 2)
            dve.wait_ge(gexp_ready, 2)
            own.then(V.tensor_tensor(r_b[:], r_b[:], sel[:], ALU.mult))
            own.then(V.tensor_reduce(small[:, 4:6], r_b[:], AX.X, ALU.add))
            own.then(V.reciprocal(small[:, 6:8], small[:, 4:6]))
            V.tensor_tensor(gates[:, :, 0:NE], r_b[:], small[:, 6:8].unsqueeze(2).to_broadcast([P, TT, NE]), ALU.mult
                            ).then_inc(gates_ready, 1)
            dve.wait_ge(rank_done, 1)
            own.then(V.memset(r1[:], 0.0))
            own.then(V.scalar_tensor_tensor(r1[:, :, 0:NE], bank[1][:, 0:TT * NE].rearrange("p (t e) -> p t e", t=TT),
                                            1.0, sel[:], op0=ALU.add, op1=ALU.mult))
            dve.wait_ge(gates_ready, 1)

            def pick(item):
                for tt in range(TT):
                    last = V.tensor_scalar(onehot[:, tt, :], iota[:], r1[:, tt, bass.ds(item, 1)], None, ALU.is_equal)
                    if tt == 0:
                        own.then(last)
                last.then_inc(onehot_ready, 1)

            pick(0)
            own.then(V.memset(gated[:], 0.0))
            own.then(V.tensor_copy(gated[:, :, 0, 0:NE], gates[:, :, 0:NE]))
            V.tensor_copy(gated[:, :, 1, 0:NE], gates[:, :, 0:NE]).then_inc(gated_ready, 1)

            def take(item):
                dve.wait_ge(takenT_done, item + 1)
                own.then(V.tensor_tensor(xT, blocks(6), wide(a2[:, :]), ALU.mult))
                V.tensor_tensor(xT, xT, wide(mod[:, M_SH2:M_SH2 + 8]), ALU.add).then_inc(xTe_ready, 1)

            def blocks(b):
                return bank[b][:, :].rearrange("p (j a s) -> p j a s", j=4, a=2)

            def wide(t):
                return t.rearrange("p (a j) -> p j a", a=2).unsqueeze(3).to_broadcast([P, 4, 2, CAP])

            take(0)
            dve.wait_ge(counts_done, 1)
            for k in range(BLOCKS - 1):
                own.then(V.tensor_scalar(over[:, k:k + 1], bank[1][0:NE, 96:97], float(CAP * (k + 1)), None, ALU.is_gt))
            V.tensor_reduce(over[:, 3:4], over[:, 0:3], AX.X, ALU.add).then_inc(over_ready, 1)
            dve.wait_ge(place_done, 1)
            for k in range(BLOCKS - 1):
                own.then(V.tensor_scalar(place[:, k:k + 1], bank[3][0:NE, 0:1], k + 1.0, None, ALU.add))
                own.then(V.tensor_scalar(item_of[:, k, :], iota[0:NE, 0:EXTRA], place[:, k:k + 1], over[:, k:k + 1],
                                         ALU.is_equal, ALU.mult))
            own.then(V.tensor_tensor(item_of[:, 3, :], item_of[:, 0, :], item_of[:, 1, :], ALU.add))
            own.then(V.tensor_tensor(item_of[:, 3, :], item_of[:, 3, :], item_of[:, 2, :], ALU.add))
            own.then(V.scalar_tensor_tensor(item_of[:, 4, :], item_of[:, 1, :], 2.0, item_of[:, 0, :],
                                            op0=ALU.mult, op1=ALU.add))
            own.then(V.scalar_tensor_tensor(item_of[:, 4, :], item_of[:, 2, :], 3.0, item_of[:, 4, :],
                                            op0=ALU.mult, op1=ALU.add))
            V.tensor_scalar(item_of[:, 4, :], item_of[:, 4, :], -float(CAP), None, ALU.mult).then_inc(itemsel_ready, 1)
            dve.wait_ge(items_done, 1)
            own.then(V.tensor_copy(r1[:, :, NE:ITEMS], bank[3][:, 16:48].rearrange("p (t i) -> p t i", t=TT)))
            own.then(V.tensor_copy(gates[:, :, NE:ITEMS], bank[3][:, 48:80].rearrange("p (t i) -> p t i", t=TT)))
            own.then(V.tensor_copy(ids_f[:], bank[3][0:1, 80:81 + EXTRA]))
            V.tensor_copy(ids[:], ids_f[:]).then_inc(items_ready, 1)
            dve.wait_ge(bdown_in, 32)
            dve.wait_ge(g2b_ready, 1)
            V.tensor_tensor(y_sb, y_sb, g2b, ALU.mult).then_inc(y_ready, 1)

            def add_given(item):
                for n in range(4):
                    tt, half = n // 2, n % 2
                    cols = slice(half * 512, (half + 1) * 512)
                    dve.wait_ge(given_done, item * 4 + (n + 5))
                    V.tensor_tensor(xres[:, tt, cols], xres[:, tt, cols], bank[4 + n][:, :], ALU.add
                                    ).then_inc(given_added, 1)

            def expert(item, number_of):
                bias = bgu[:, bass.ds(number_of, 1), :].rearrange("p e r -> p (e r)")
                dve.wait_ge(back_ready, item + 1)
                for tt in range(TT):
                    for a in range(2):
                        last = V.tensor_scalar(gated[:, tt, a, :], iota[:], r1[:, tt, bass.ds(item, 1)],
                                               gates[:, tt, bass.ds(item, 1)], ALU.is_equal, ALU.mult)
                        if 2 * tt + a < 3:
                            own.then(last)
                last.then_inc(gated_ready, 1)
                pick(item + 1)
                add_given(item - 1)
                dve.wait_ge(gT_done, item + 1)
                own.then(V.tensor_tensor(g_sb, blocks(2), wide(bias[:, 0:8]), ALU.add))
                V.tensor_scalar(g_sb, g_sb, LIMIT, None, ALU.min).then_inc(gmin_ready, 1)
                dve.wait_ge(uT_done, item + 1)
                own.then(V.tensor_tensor(u_sb, blocks(3), wide(bias[:, 8:16]), ALU.add))
                own.then(V.tensor_scalar(u_sb, u_sb, LIMIT, -LIMIT, ALU.min, ALU.max))
                dve.wait_ge(gmin_ready, item + 1)
                own.then(V.scalar_tensor_tensor(u_sb, u_sb, 1.0, g_sb, op0=ALU.add, op1=ALU.mult))
                dve.wait_ge(sig_ready, item + 1)
                V.tensor_tensor(act_sb, u_sb, sig, ALU.mult).then_inc(act_ready, 1)
                take(item + 1)
                dve.wait_ge(down_used, item * 4 + 4)
                V.tensor_tensor(y_sb, bank[7][:, :], g2b, ALU.mult).then_inc(y_ready, 1)

            PER = 3 + 1 + 1 + 2 + 1 + 1
            start = own.steps
            with dve.Fori(0, PAIRS) as n:
                for half in range(2):
                    own.start_at(n * (2 * PER) + (start + PER * half))
                    expert(n * 2 + half, n * 2 + half)
                    assert own.steps == PER
            dve.wait_ge(items_ready, 1)
            extra = dve.value_load(ids[0:1, EXTRA:EXTRA + 1], min_val=0, max_val=EXTRA)
            start += NE * PER
            with dve.Fori(0, EXTRA // 2) as n:
                for half in range(2):
                    with dve.If(extra > n * 2 + half):
                        number_of = dve.value_load(ids[0:1, bass.ds(n * 2 + half, 1)], min_val=0, max_val=NE - 1)
                        own.start_at(n * (2 * PER) + (start + PER * half))
                        expert(n * 2 + (NE + half), number_of)
            add_given(extra + (NE - 1))

            dve.drain().then_inc(sum_ready, 1)
            dve.wait_ge(sq_done, 6)
            V.tensor_scalar(stat[:, 2:4], stat[:, 0:2], 1.0 / D, EPS, ALU.mult, ALU.add).then_inc(ms_ready, 1)
            dve.wait_ge(root_ready, 4)
            V.reciprocal(stat[:, 6:8], stat[:, 4:6]).then_inc(ms_ready, 1)
            dve.wait_ge(ms_ready, 5)
            dve.wait_ge(fg_in, 16)
            for tt in range(TT):
                V.scalar_tensor_tensor(xres[:, tt, :], xres[:, tt, :], stat[:, 6 + tt:7 + tt], fgb,
                                       op0=ALU.mult, op1=ALU.mult).then_inc(out_ready, 1)

        @block.tensor
        def _(pe):
            M = nc.tensor.matmul

            pe.wait_ge(consts, 2)
            pe.wait_ge(small_in, 9 * 16)
            nc.tensor.transpose(bank[7][:, 0:R_END], vt, ident[0:R_END, 0:R_END]).then_inc(vecT_done, 1)
            pe.wait_ge(bgu_in, 16)
            for a in range(4):
                last = nc.tensor.transpose(bank[6][:, a * P:(a + 1) * P], bgu_rows[:, a, :], ident[:])
            last.then_inc(bgu_done, 1)
            pe.wait_ge(vec_ready, 2)
            for n in range(2):
                last = M(bank[(7, 4)[n]][:, 256:257], ones[64 * n:64 * n + 64, :], lam[64 * n:64 * n + 64, 3:4],
                         start=True, stop=True)
            last.then_inc(lam_done, 1)

            def transpose_rows(b0):
                for kt in range(KT):
                    for tt in range(TT):
                        last = nc.tensor.transpose(bank[b0 + kt // 2][:, (kt % 2) * T + tt * P:(kt % 2) * T + (tt + 1) * P],
                                                   xn[:, tt, kt * P:(kt + 1) * P], ident[:])
                    if kt % 2:
                        last.then_inc(xT_done, 1)

            pe.wait_ge(xn_ready, 2)
            transpose_rows(0)

            def ada_group(g, group):
                for h in range(2):
                    wait_group(pe, group, h)
                for blk in range(4):
                    for kt in range(KT):
                        last = M(bank[5][:, 4 * g + blk:4 * g + blk + 1],
                                 group_chunk(group, kt // 4)[:, kt % 4, blk * P:(blk + 1) * P],
                                 vec[:, R_C + kt:R_C + kt + 1], start=kt == 0, stop=kt == KT - 1)
                last.then_inc(groups_used, 1)
                return last

            for g in range(GROUPS_ADA1):
                ada_group(g, g)

            with pe.Fori(0, 2) as it:
                for g in range(8):
                    group = GROUPS_ADA1 + g
                    for h in range(2):
                        wait_group(pe, group, h, loops=it * 2)
                    for h in range(2):
                        pe.wait_ge(emptied, it * 16 + (2 * g + h + 5))
                        if g == 0 and h == 0:
                            pe.wait_ge(emptied, 8)
                        dst = bank[2 * (g % 2) + h]
                        if g in (4, 5):
                            for kt in range(KT):
                                last = M(dst[:, :], hT[:, kt, h * P:(h + 1) * P], group_chunk(group, kt // 4)[:, kt % 4, :],
                                         start=kt == 0, stop=kt == KT - 1)
                        else:
                            for b in range(2):
                                cols = slice((2 * h + b) * P, (2 * h + b + 1) * P)
                                for kt in range(KT):
                                    last = M(dst[:, b * T:(b + 1) * T], group_chunk(group, kt // 4)[:, kt % 4, cols],
                                             hT[:, kt, :], start=kt == 0, stop=kt == KT - 1)
                        last.then_inc(groups_used if h else proj_done, 1)

            pe.wait_ge(emptied, 8 + 32)
            for s in range(DAH + 2):
                if s < DAH:
                    part, blk = slice(64 * (s % 2), 64 * (s % 2) + 64), s // 2
                    if s >= 2:
                        pe.wait_ge(scores_ready, 2 * (s - 1))
                    for m in range(2):
                        q = qkT[part, 0, 4 * m + blk, :]
                        k = qkT[part, 0, 8 + 4 * m + blk, :]
                        dst = bank[2 * (s % 2) + m]
                        M(dst[:, 0:128], q[:, 0:P], k[:, 0:P], start=True, stop=True)
                        M(dst[:, 128:384], q[:, P:T], k, start=True, stop=True).then_inc(scores_done, 1)
                    ada_group(GROUPS_ADA1 + s, GROUPS_ADA1 + GROUPS_IN + s)
                if 1 <= s <= DAH:
                    h = s - 1
                    pe.wait_ge(w_ready, h + 1)
                    if h >= 1:
                        pe.wait_ge(wT_ready, h)
                    for n in range(3):
                        last = nc.tensor.transpose(bank[4][:, n * P:(n + 1) * P], da_w[:, h % 2, n * P:(n + 1) * P], ident[:])
                    last.then_inc(wT_done, 1)
                if s >= 2:
                    h = s - 2
                    pe.wait_ge(wT_ready, h + 1)
                    if h >= 2:
                        pe.wait_ge(pv_read, h - 1)
                    dst, wt = bank[6 + h % 2], da_wT[:, h % 2, :]
                    cols = slice(h * P, (h + 1) * P)
                    M(dst[:, 0:128], wt[:, 0:P], v_sb[:, 0, 0, cols], start=True, stop=True)
                    M(dst[:, 128:256], wt[:, P:2 * P], v_sb[:, 0, 0, cols], start=True, stop=False)
                    M(dst[:, 128:256], wt[:, 2 * P:3 * P], v_sb[:, 0, 1, cols], start=False, stop=True).then_inc(pv_done, 1)

            pe.wait_ge(scores_ready, 2 * DAH)
            pe.wait_ge(pv_read, DAH)
            for s in range(SBH + 4):
                if s < SBH:
                    part, blk = slice(64 * (s % 2), 64 * (s % 2) + 64), s // 2
                    if s == 3:
                        pe.wait_ge(mod_ready, 2)
                    if s >= 4:
                        pe.wait_ge(sbw_ready, s - 3)
                    q, k = qkT[part, 1, blk, :], qkT[part, 1, 8 + blk, :]
                    z = bank[(0, 1, 2, 5)[s % 4]]
                    M(z[:, 0:256], k[:, 0:P], q, start=True, stop=False, skip_group_check=True)
                    M(z[:, 256:384], k[:, P:T], q[:, P:T], start=False, stop=False, skip_group_check=True
                      ).then_inc(z_done, 1)
                if 2 <= s < SBH + 2:
                    h = s - 2
                    z, l = bank[(0, 1, 2, 5)[h % 4]], sb_l[:, h % 3, :]
                    pe.wait_ge(splus_masked, h + 1)
                    M(z[:, 0:256], neg_tri[:], l[:, 0:256], start=False, stop=False, skip_group_check=True)
                    M(z[:, 128:256], neg_ones[:], l[:, 256:384], start=False, stop=False, skip_group_check=True)
                    M(z[:, 256:384], neg_tri[:], l[:, 256:384], start=False, stop=True, skip_group_check=True
                      ).then_inc(logw_done, 1)
                if 4 <= s:
                    h = s - 4
                    pe.wait_ge(sbw_masked, h + 1)
                    if h >= 4 and h % 2 == 0:
                        pe.wait_ge(obT_ready, h // 2 - 1)
                    dst = bank[6 + (h // 2) % 2][64 * (h % 2):64 * (h % 2) + 64, :]
                    a, cols = sb_a[:, h % 3, :], slice(h * DH, (h + 1) * DH)
                    M(dst[:, 0:256], v_sb[:, 1, 0, cols], a[:, 0:256], start=True, stop=False, skip_group_check=True)
                    M(dst[:, 128:256], v_sb[:, 1, 1, cols], a[:, 256:384], start=False, stop=True, skip_group_check=True
                      ).then_inc(sbpv_done, 1)
                if 3 <= s < 7:
                    n = s - 3
                    if n == 0:
                        pe.wait_ge(oa_ready, 1)
                        pe.wait_ge(wT_ready, DAH)
                    if n >= 2:
                        pe.wait_ge(oaT_ready, n - 1)
                    for j in range(4):
                        kt, tt = 2 * n + j // 2, j % 2
                        last = nc.tensor.transpose(bank[3 + n % 2][:, j * P:(j + 1) * P], oa[:, tt, kt * P:(kt + 1) * P], ident[:])
                    last.then_inc(oaT_done, 1)
                if s in (7, 8):
                    n = s - 7
                    pe.wait_ge(oaT_ready, 3 + n)
                    pe.wait_ge(diag_ready, 4 * n + 4)
                    for j in range(4):
                        last = M(bank[3 + n][:, j * P:(j + 1) * P], ones[:], g1diag[:, 4 * n + j, :], start=True, stop=True)
                    last.then_inc(g1b_done, 1)

            g0 = GROUPS_ADA1 + GROUPS_IN + GROUPS_ADA2
            pe.wait_ge(sbw_ready, SBH)
            pe.wait_ge(g1b_ready, 2)
            for n in range(4):
                src = oaT if n % 2 == 0 else obT
                if n == 1:
                    pe.wait_ge(obT_ready, SBH // 2)
                for h in range(2):
                    wait_group(pe, g0 + n, h)
                for blk in range(4):
                    for kt in range(KT):
                        last = M(bank[2 * n + blk // 2][:, (blk % 2) * T:(blk % 2 + 1) * T],
                                 group_chunk(g0 + n, kt // 4)[:, kt % 4, blk * P:(blk + 1) * P], src[:, kt, :],
                                 start=kt == 0, stop=kt == KT - 1)
                    if blk % 2 == 1:
                        last.then_inc(groups_used if blk == 3 else branch_done, 1)
            pe.wait_ge(merged_ready, 4)
            for half in range(2):
                for h in range(2):
                    wait_group(pe, g0 + 4 + half, h)
                for tt in range(TT):
                    for kt in range(KT):
                        last = M(bank[2 * half + tt][:, :], mergedT[:, kt, tt * P:(tt + 1) * P],
                                 group_chunk(g0 + 4 + half, kt // 4)[:, kt % 4, :], start=kt == 0, stop=kt == KT - 1)
                    last.then_inc(groups_used if tt else mixed_done, 1)

            pe.wait_ge(diag_ready, 2 * KT)
            for a in range(2):
                last = M(bank[4][64 * a:64 * a + 64, :], ones[:, 0:64],
                         g1diag[:, 4 * a:4 * a + 4, :].rearrange("p k n -> p (k n)"), start=True, stop=True)
            last.then_inc(g2b_done, 1)
            pe.wait_ge(g2b_ready, 1)
            pe.wait_ge(xn_ready, 4)
            transpose_rows(4)
            pe.wait_ge(h2T_even, KT // 2)
            pe.wait_ge(h2T_odd, KT // 2)
            pe.wait_ge(router_in, 32)
            pe.wait_ge(x1_ready, 4)
            for tt in range(TT):
                dst = bank[0][:, tt * NE:(tt + 1) * NE]
                for kt in range(KT):
                    M(dst, h2T[:, kt, tt * P:(tt + 1) * P], rw_sb[:, kt, :], start=kt == 0, stop=False)
                last = M(dst, ones[0:1, :], rb_sb[:], start=False, stop=True)
            last.then_inc(logits_done, 1)
            pe.wait_ge(sel_ready, 2)
            M(bank[1][:, 0:NE], before[:], sel[:, 0, :], start=True, stop=True)
            M(bank[1][:, NE:2 * NE], ones[:], sel[:, 0, :], start=True, stop=False)
            M(bank[1][:, NE:2 * NE], before[:], sel[:, 1, :], start=False, stop=True).then_inc(rank_done, 1)

            def take(item):
                pe.wait_ge(onehot_ready, item + 1)
                for tt in range(TT):
                    for a in range(2):
                        last = M(bank[4][64 * a:64 * a + 64, :], onehot[:, tt, :], xn[:, tt, a * 512:(a + 1) * 512],
                                 start=tt == 0, stop=tt == TT - 1, skip_group_check=True)
                last.then_inc(taken_done, 1)

            def transposes(b, src):
                for j in range(4):
                    last = nc.tensor.transpose(bank[b][:, j * P:(j + 1) * P], src[:, j * P:(j + 1) * P], ident[:])
                return last

            def take_transposed(item):
                pe.wait_ge(xraw_ready, item + 1)
                transposes(6, x_raw).then_inc(takenT_done, 1)

            def way_back(item):
                pe.wait_ge(gated_ready, item + 2)
                for tt in range(TT):
                    last = nc.tensor.transpose(bank[5][:, tt * P:(tt + 1) * P],
                                               gated[:, tt, :, :].rearrange("p a s -> p (a s)"), ident[:])
                last.then_inc(back_done, 1)

            def give(item):
                pe.wait_ge(y_ready, item + 2)
                pe.wait_ge(back_ready, item + 2)
                for n in range(4):
                    tt, a = n // 2, n % 2
                    rows = slice(64 * a, 64 * a + 64)
                    M(bank[4 + n][:, :], back[rows, tt * P:(tt + 1) * P], y_sb[rows, :], start=True, stop=True
                      ).then_inc(given_done, 1)

            def expert(item, half, fills):
                pe.wait_ge(xTe_ready, item + 1)
                for kt in range(KT):
                    pe.wait_ge(slot_in[8 * half + kt], fills * 16 + 16 * USES[8 * half + kt])
                    for f in range(4):
                        a = f % 2
                        last = M(bank[f // 2][64 * a:64 * a + 64, :], xT[:, kt % 4, kt // 4, :],
                                 gu_ring[:, 8 * half + kt, f * 512:(f + 1) * 512],
                                 start=kt == 0, stop=kt == KT - 1, skip_group_check=True)
                        if kt == KT - 1 and f == 1:
                            last.then_inc(g_done, 1)
                    last.then_inc(gu_used, 1)
                    if kt == 1:
                        give(item - 1)
                pe.wait_ge(given_added, item * 4 + 4)
                take(item + 1)
                way_back(item)
                pe.wait_ge(raw_ready, item * 2 + 1)
                transposes(2, g_raw).then_inc(gT_done, 1)
                pe.wait_ge(raw_ready, item * 2 + 2)
                transposes(3, u_raw).then_inc(uT_done, 1)
                take_transposed(item + 1)
                pe.wait_ge(act_ready, item + 1)
                for kt in range(KT):
                    if kt % 2 == 0:
                        pe.wait_ge(down_in[kt // 2], item * 16 + 16)
                    for a in range(2):
                        last = M(bank[7][64 * a:64 * a + 64, :], act_sb[:, kt % 4, kt // 4, :],
                                 down_ring[:, kt // 2, (kt % 2) * D + a * 512:(kt % 2) * D + (a + 1) * 512],
                                 start=kt == 0, stop=kt == KT - 1, skip_group_check=True)
                    if kt % 2 == 1:
                        last.then_inc(down_used, 1)

            take(0)
            for tt in range(TT):
                last = M(bank[1][0:NE, 96:97], sel[:, tt, :], ones[:, 0:1], start=tt == 0, stop=tt == TT - 1)
            last.then_inc(counts_done, 1)
            way_back(-1)
            take_transposed(0)
            for n, table in enumerate((r1, gates)):
                for tt in range(TT):
                    last = nc.tensor.transpose(bank[2][0:NE, n * T + tt * P:n * T + (tt + 1) * P], table[:, tt, 0:NE], ident[:])
            last.then_inc(tablesT_done, 1)
            pe.wait_ge(over_ready, 1)
            M(bank[3][0:NE, 0:1], before[0:NE, 0:NE], over[:, 3:4], start=True, stop=True).then_inc(place_done, 1)
            pe.wait_ge(tables_ready, 1)
            pe.wait_ge(itemsel_ready, 1)
            for tt in range(TT):
                dst = bank[3][:, 16 + tt * EXTRA:16 + (tt + 1) * EXTRA]
                M(dst, tables[:, 0, tt * P:(tt + 1) * P], item_of[:, 3, :], start=True, stop=False)
                M(dst, ones[0:NE, :], item_of[:, 4, :], start=False, stop=True)
                M(bank[3][:, 48 + tt * EXTRA:48 + (tt + 1) * EXTRA], tables[:, 1, tt * P:(tt + 1) * P], item_of[:, 3, :],
                  start=True, stop=True)
            M(bank[3][0:1, 80:80 + EXTRA], number[0:NE, :], item_of[:, 3, :], start=True, stop=True)
            M(bank[3][0:1, 80 + EXTRA:81 + EXTRA], over[:, 3:4], ones[0:NE, 0:1], start=True, stop=True
              ).then_inc(items_done, 1)
            pe.wait_ge(items_ready, 1)

            with pe.Fori(0, PAIRS) as n:
                for half in range(2):
                    expert(n * 2 + half, half, n + 1)
            extra = pe.value_load(ids[0:1, EXTRA:EXTRA + 1], min_val=0, max_val=EXTRA)
            with pe.Fori(0, EXTRA // 2) as n:
                for half in range(2):
                    with pe.If(extra > n * 2 + half):
                        expert(n * 2 + (NE + half), half, n + (PAIRS + 1))
            give(extra + (NE - 1))


_INS = ["x", "c", "w_ada", "b_ada", "norm1_g", "w_in", "lam_q1", "lam_k1", "lam_q2", "lam_k2", "subln_g", "w_pa", "w_pb",
        "w_o", "norm2_g", "router_w", "router_b", "w_gu", "b_gu", "w_down", "b_down", "final_g"]


def kernel(**inputs):
    import concourse.bacc as bacc
    from concourse.bass_utils import run_bass_kernel_spmd

    nc = bacc.Bacc("TRN2", target_bir_lowering=False, num_devices=1)
    arrays, args = {}, []
    for name in _INS:
        a = np.ascontiguousarray(inputs[name])
        arrays[f"in_{name}"] = a
        args.append(nc.dram_tensor(f"in_{name}", a.shape, mybir.dt.from_np(a.dtype), kind="ExternalInput").ap())
    args.append(nc.dram_tensor("out", (1, T, D), F32, kind="ExternalOutput").ap())
    build(nc, *args)
    return run_bass_kernel_spmd(nc, [arrays], core_ids=[0]).results[0]["out"]
```

```python
import math
from contextlib import ExitStack

import concourse.bass as bass
import numpy as np
from concourse import mybir

F32 = mybir.dt.float32
I32 = mybir.dt.int32
ALU = mybir.AluOpType
ACT = mybir.ActivationFunctionType
AX = mybir.AxisListType

P = 128
D = 1024
T = 256
KT = D // P
TT = T // P
DH = 64
DAH, SBH = 8, 16
CHUNKMASK = 64
NE, TOPK = 32, 4
EPS = 1e-6
LAM_INIT = 0.8 - 0.6 * math.exp(-0.3 * 0)
FAR = 1e30
LIMIT, ALPHA = 7.0, 1.702

CW = 512
ADA_1, ADA = 4, 12
GROUPS = ([("ada", g) for g in range(ADA_1)] + [("in", g) for g in range(4)]
          + [(w, g) for g in range(4, 12) for w in ("in", "ada")] + [("in", g) for g in range(12, 16)]
          + [(w, half) for w in ("pa", "pb", "o") for half in range(2)])
POS = {group: n for n, group in enumerate(GROUPS)}
VALUES = (4, 5, 10, 11)
CAP = 64
BLOCKS = T // CAP
PAIRS = NE // 2
TOGETHER = NE // 2

R_C, R_N1, R_N2, R_ADA, R_SUB, R_LQ, R_LK, R_END = 0, 8, 16, 24, 72, 73, 74, 75
M_SH1, M_SC1, M_G1, M_SH2, M_SC2, M_G2 = (8 * n for n in range(6))


class Order:

    def __init__(self, engine, sem):
        self.engine, self.sem, self.base, self.steps = engine, sem, 0, 0

    def then(self, instruction):
        instruction.then_inc(self.sem, 1)
        self.steps += 1
        self.engine.wait_ge(self.sem, self.base + self.steps)

    def start_at(self, base):
        self.base, self.steps = base, 0


def build(nc, x, c, w_ada, b_ada, norm1_g, w_in, lam_q1, lam_k1, lam_q2, lam_k2, subln_g, w_pa, w_pb, w_o,
          norm2_g, router_w, router_b, w_gu, b_gu, w_down, b_down, final_g, out):
    ctx = ExitStack()
    with ctx:
        def sb(name, shape, dt=F32):
            return ctx.enter_context(nc.sbuf_tensor(name, shape, dt))

        def sem(name):
            return ctx.enter_context(nc.semaphore(name))

        gu_ring = sb("gu_ring", [P, 16, 2048])
        down_ring = sb("down_ring", [P, 4, 2048])
        qkT = down_ring[:, :, :].rearrange("p s n -> p (s n)").rearrange("p (i b t) -> p i b t", i=2, b=16)
        v_sb = gu_ring[:, 8:10, :].rearrange("p i (t n) -> p i t n", t=TT)
        hT = gu_ring[:, 10, :].rearrange("p (k t) -> p k t", k=KT)
        g1b = gu_ring[:, 10, 0:D]
        g1diag = gu_ring[:, 10, D:2 * D].rearrange("p (k n) -> p k n", k=KT)
        gateT = gu_ring[:, 11:13, :].rearrange("p i (k t) -> p i k t", k=KT)
        oaT = gu_ring[:, 13, :].rearrange("p (k t) -> p k t", k=KT)
        obT = gu_ring[:, 14, :].rearrange("p (k t) -> p k t", k=KT)
        da_w = gu_ring[:, 14, 0:768].rearrange("p (b n) -> p b n", b=2)
        da_wT = gu_ring[:, 14, 768:1536].rearrange("p (b n) -> p b n", b=2)
        mergedT = gu_ring[:, 15, :].rearrange("p (k t) -> p k t", k=KT)
        oa = gu_ring[:, 15, :].rearrange("p (t n) -> p t n", t=TT)

        xres = sb("xres", [P, TT, D])
        xn = sb("xn", [P, TT, D])
        scratch = sb("scratch", [P, 5120])
        at = [0]

        def part(n):
            at[0] += n
            assert at[0] <= 5120
            return scratch[:, at[0] - n:at[0]]

        da_s = part(4 * 384).rearrange("p (b m n) -> p b m n", b=2, m=2)
        sb_t = part(2 * 384).rearrange("p (b n) -> p b n", b=2)
        rows = scratch[:, at[0]:at[0] + CW]
        sb_l = part(3 * 384).rearrange("p (b n) -> p b n", b=3)
        sb_a = part(3 * 384).rearrange("p (b n) -> p b n", b=3)
        dist = part(384)
        c_cols = sb_t[:, 0, 0:256].rearrange("p (k m) -> p k m", k=KT)
        x1T = scratch[:, 0:2048].rearrange("p (k t) -> p k t", k=KT)
        shifted = scratch[:, 0:KT * NE].rearrange("p (k e) -> p k e", k=KT)
        tmp = scratch[:, 2048:3072].rearrange("p (b n) -> p b n", b=2)
        at[0] = 0
        xT = part(512).rearrange("p (j a s) -> p j a s", j=4, a=2)
        g_sb = part(512).rearrange("p (j a s) -> p j a s", j=4, a=2)
        sig = part(512).rearrange("p (j a s) -> p j a s", j=4, a=2)
        u_sb = part(512).rearrange("p (j a s) -> p j a s", j=4, a=2)
        act_sb = part(512).rearrange("p (j a s) -> p j a s", j=4, a=2)
        x_raw, g_raw, u_raw, y_sb, g2b = part(512), part(512), part(512), part(512), part(512)
        lg, r_a, r_b = (scratch[:, 3072 + 64 * n:3136 + 64 * n].rearrange("p (t e) -> p t e", t=TT)
                        for n in range(3))
        f_xT, f_y = u_sb, g_raw
        f_back = u_raw.rearrange("p (a t) -> p a t", a=2)


        ident = sb("ident", [P, P])
        ones = sb("ones", [P, P])
        before = sb("before", [P, P])
        iota = sb("iota", [P, CAP])
        onehot = sb("onehot", [P, TT, CAP])
        gated = sb("gated", [P, TT, 2, CAP])
        back = sb("back", [P, 2, T])
        neg_ones, neg_tri = back[:, 0, 0:P], back[:, 0, P:2 * P]
        vec = sb("vec", [P, R_END])
        bgu = sb("bgu", [P, NE, 16])
        mod = sb("mod", [P, 48])
        a1 = sb("a1", [P, KT])
        a2 = sb("a2", [P, KT])
        lam = sb("lam", [P, 4])
        nsub = sb("nsub", [P, 1])
        stat = sb("stat", [P, 8])
        smax = sb("smax", [P, 2, 4])
        ssum = sb("ssum", [P, 2, 4])
        srec = sb("srec", [P, 2, 4])
        osq = sb("osq", [P, 16])
        rw_sb = sb("rw_sb", [P, KT, NE])
        rb_sb = sb("rb_sb", [1, NE])
        shift = sb("shift", [P, NE])
        top8 = sb("top8", [P, TT, 8])
        r1 = sb("r1", [P, TT, NE + 1])
        sel = sb("sel", [P, TT, NE])
        gates = sb("gates", [P, TT, NE])
        over = sb("over", [NE, 4])
        passes_f = sb("passes_f", [1, 2, NE])
        passes = sb("passes", [1, 2, NE], I32)
        small = sb("small", [P, 8])
        first_of = sb("first_of", [P, 1])
        vt = xn[0:R_END, 0, 0:P]
        fgb = xn[:, 0, :]
        bgu_rows = gu_ring[:, 15, 0:512].rearrange("p (a f) -> p a f", a=4)

        bank = [ctx.enter_context(nc.psum_tensor(f"bank{n}", [P, 512], F32)) for n in range(8)]

        slot_in = [sem(f"slot_in{n}") for n in range(16)]
        down_in = [sem(f"down_in{n}") for n in range(4)]
        small_in = sem("small_in")
        bgu_in = sem("bgu_in")
        x_in = sem("x_in")
        router_in = sem("router_in")
        bdown_in = sem("bdown_in")
        fg_in = sem("fg_in")
        out_done = sem("out_done")
        filled = sem("filled")
        rows_ready = sem("rows_ready")
        cols_done = sem("cols_done")
        sigmoid_ready = sem("sigmoid_ready")
        gu_used = sem("gu_used")
        down_used = sem("down_used")
        consts = sem("consts")
        pool_own = sem("pool_own")
        vecT_done = sem("vecT_done")
        vec_ready = sem("vec_ready")
        lam_done = sem("lam_done")
        lam_exp = sem("lam_exp")
        sq_done = sem("sq_done")
        ms_ready = sem("ms_ready")
        root_ready = sem("root_ready")
        xn_ready = sem("xn_ready")
        xT_done = sem("xT_done")
        mod_ready = sem("mod_ready")
        emptied = sem("emptied")
        scores_done = sem("scores_done")
        scores_ready = sem("scores_ready")
        max_ready = sem("max_ready")
        exp_ready = sem("exp_ready")
        w_ready = sem("w_ready")
        wT_done = sem("wT_done")
        wT_ready = sem("wT_ready")
        pv_done = sem("pv_done")
        pv_read = sem("pv_read")
        oa_ready = sem("oa_ready")
        oaT_done = sem("oaT_done")
        diag_ready = sem("diag_ready")
        g1b_done = sem("g1b_done")
        z_done = sem("z_done")
        absz_ready = sem("absz_ready")
        ln_ready = sem("ln_ready")
        splus_ready = sem("splus_ready")
        splus_masked = sem("splus_masked")
        logw_done = sem("logw_done")
        sbw_ready = sem("sbw_ready")
        sbw_masked = sem("sbw_masked")
        sbpv_done = sem("sbpv_done")
        obT_ready = sem("obT_ready")
        merged_ready = sem("merged_ready")
        mixed_done = sem("mixed_done")
        x1_ready = sem("x1_ready")
        rw_ready = sem("rw_ready")
        shift_done = sem("shift_done")
        shift_ready = sem("shift_ready")
        x1T_low = sem("x1T_low")
        x1T_high = sem("x1T_high")
        logits_done = sem("logits_done")
        top_ready = sem("top_ready")
        gexp_ready = sem("gexp_ready")
        sel_ready = sem("sel_ready")
        rank_done = sem("rank_done")
        counts_done = sem("counts_done")
        over_ready = sem("over_ready")
        passes_done = sem("passes_done")
        passes_ready = sem("passes_ready")
        gates_ready = sem("gates_ready")
        g2b_done = sem("g2b_done")
        bgu_done = sem("bgu_done")
        onehot_ready = sem("onehot_ready")
        gated_ready = sem("gated_ready")
        taken_done = sem("taken_done")
        xraw_ready = sem("xraw_ready")
        takenT_done = sem("takenT_done")
        xTe_ready = sem("xTe_ready")
        g_done = sem("g_done")
        raw_ready = sem("raw_ready")
        gT_done = sem("gT_done")
        uT_done = sem("uT_done")
        gmin_ready = sem("gmin_ready")
        sig_ready = sem("sig_ready")
        act_ready = sem("act_ready")
        back_done = sem("back_done")
        back_ready = sem("back_ready")
        y_ready = sem("y_ready")
        given_done = sem("given_done")
        given_added = sem("given_added")
        f_onehot = sem("f_onehot")
        f_gated = sem("f_gated")
        f_taken = sem("f_taken")
        f_xraw = sem("f_xraw")
        f_takenT = sem("f_takenT")
        f_xT_ready = sem("f_xT_ready")
        f_gu_done = sem("f_gu_done")
        f_raw = sem("f_raw")
        f_guT_done = sem("f_guT_done")
        f_back_done = sem("f_back_done")
        f_back_ready = sem("f_back_ready")
        f_gmin = sem("f_gmin")
        f_sig = sem("f_sig")
        f_act = sem("f_act")
        f_down_done = sem("f_down_done")
        f_y_ready = sem("f_y_ready")
        f_given = sem("f_given")
        f_added = sem("f_added")
        f_own = sem("f_own")
        f_mark = sem("f_mark")
        out_ready = sem("out_ready")
        rec_ready = sem("rec_ready")
        act_own, dve_own = sem("act_own"), sem("dve_own")

        def group_slots(group):
            s = (2 * group + 4) % 8
            return s, s + 1

        def group_chunk(group, h):
            return gu_ring[:, group_slots(group)[h], :].rearrange("p (k n) -> p k n", n=CW)

        def wait_group(eng, group, h):
            chunk = 2 * group + h
            eng.wait_ge(slot_in[group_slots(group)[h]], (chunk // 8 + 1) * 16)

        USES = [8] * 4 + [9] * 4 + [0] * 8

        def further_passes(eng, expert, one_pass):
            count = eng.value_load(passes[0:1, 0, bass.ds(expert, 1)], min_val=0, max_val=BLOCKS - 1)
            with eng.If(count > 0):
                before_it = eng.value_load(passes[0:1, 1, bass.ds(expert, 1)], min_val=0, max_val=T * TOPK // CAP)
                for b in range(1, BLOCKS):
                    with eng.If(count > b - 1):
                        one_pass(b, before_it + (b - 1))

        def turn_gate(half):
            return 24 + half + max(0, half - 3)

        def turn_oaT(n):
            return 28 + 2 * n

        def turn_pa(half):
            return 36 + half + (2 if half >= 2 else 0)

        def turn_g1b(n):
            return 38 + n

        TURN_G2B = 42
        EMPTIED_HT = KT

        block = ctx.enter_context(nc.Block())

        @block.sync
        def _(sp):
            for rows_, src in ((slice(R_C, R_N1), c[0, :].rearrange("(r f) -> r f", f=P)),
                               (slice(R_N1, R_N2), norm1_g[0, :].rearrange("(r f) -> r f", f=P)),
                               (slice(R_N2, R_ADA), norm2_g[0, :].rearrange("(r f) -> r f", f=P)),
                               (slice(R_ADA, R_SUB), b_ada[0, :].rearrange("(r f) -> r f", f=P)),
                               (slice(R_SUB, R_LQ), subln_g[0:1, :])):
                sp.dma_start(xn[rows_, 0, 0:P], src).then_inc(small_in, 16)

            def load_gu(expert, half, kt):
                sp.dma_start(gu_ring[:, 8 * half + kt, :],
                             w_gu[0, bass.ds(expert, 1), kt * P:(kt + 1) * P, :].rearrange("a p n -> p (a n)")
                             ).then_inc(slot_in[8 * half + kt], 16)

            def load_down(expert, j):
                sp.dma_start(down_ring[:, j, :].rearrange("p (k n) -> p k n", k=2),
                             w_down[0, bass.ds(expert, 1), j * 2 * P:(j + 1) * 2 * P, :]
                             .rearrange("a (k p) n -> p (a k) n", p=P)).then_inc(down_in[j], 16)

            weights = {"ada": w_ada, "in": w_in, "pa": w_pa, "pb": w_pb, "o": w_o}
            for n, (w, g) in enumerate(GROUPS):
                if n == 5:
                    sp.dma_start(bgu_rows, b_gu[0, :, :].rearrange("e (r f) -> (e r) f", f=P)
                                  .rearrange("(a p) f -> p a f", p=P)).then_inc(bgu_in, 16)
                    sp.dma_start(rw_sb[:], router_w[0, :, :].rearrange("(k p) e -> p k e", p=P)).then_inc(router_in, 16)
                    sp.dma_start(rb_sb[:], router_b[0:1, :]).then_inc(router_in, 16)
                if n == len(GROUPS) - 1:
                    sp.wait_ge(sbpv_done, SBH)
                    for half in range(2):
                        sp.dma_start(y_sb[64 * half:64 * half + NE, :], b_down[0, :, half * 512:(half + 1) * 512]
                                     ).then_inc(bdown_in, 16)
                    for j in range(4):
                        load_down(0, j)
                    for kt in range(2):
                        load_gu(1, 1, kt)
                if n >= 4:
                    sp.wait_ge(filled, 2 * (n - 3))
                for h in range(2):
                    sp.dma_start(group_chunk(n, h), weights[w][0, h * 512:(h + 1) * 512, g * CW:(g + 1) * CW]
                                 .rearrange("(k p) n -> p k n", p=P)).then_inc(slot_in[group_slots(n)[h]], 16)

            for kt in range(KT):
                if kt == 4:
                    sp.wait_ge(merged_ready, 4)
                    for k in range(3, 7):
                        load_gu(1, 1, k)
                if kt % 2 == 0:
                    if kt < 6:
                        sp.wait_ge(filled, 2 * (len(GROUPS) - 3 + kt // 2))
                    else:
                        sp.wait_ge(mixed_done, 4)
                load_gu(0, 0, kt)
            sp.wait_ge(x1_ready, 4)
            sp.wait_ge(g2b_done, 1)
            for kt in (2, 7):
                load_gu(1, 1, kt)

            def load_item_gu(item, half):
                for kt in range(KT):
                    sp.wait_ge(gu_used, item * 8 + (kt - 15))
                    load_gu(item, half, kt)

            def load_item_down(item):
                for j in range(4):
                    sp.wait_ge(down_used, item * 4 + (j - 3))
                    load_down(item, j)

            load_item_gu(2, 0)
            load_item_down(1)
            with sp.Fori(1, TOGETHER // 2) as n:
                load_item_gu(n * 2 + 1, 1)
                load_item_down(n * 2)
                load_item_gu(n * 2 + 2, 0)
                load_item_down(n * 2 + 1)
            load_item_down(TOGETHER)
            load_item_gu(TOGETHER + 1, 1)
            load_item_down(TOGETHER + 1)
            with sp.Fori(TOGETHER // 2 + 1, PAIRS) as n:
                for half in range(2):
                    load_item_gu(n * 2 + half, half)
                    load_item_down(n * 2 + half)
            sp.wait_ge(taken_done, NE + 1)
            sp.dma_start(fgb, final_g.partition_broadcast(P)).then_inc(fg_in, 16)
            for tt in range(TT):
                sp.wait_ge(out_ready, tt + 1)
                sp.dma_start(out[0, tt * P:(tt + 1) * P, :], xres[:, tt, :]).then_inc(out_done, 16)
            sp.wait_ge(out_done, 16 * TT)

        @block.gpsimd
        def _(pool):
            own = Order(pool, pool_own)

            def tri(m, fill, keep_when, base, step, channel):
                return nc.gpsimd.affine_select(out=m, in_=m, compare_op=keep_when, fill=fill, base=base,
                                               pattern=[[step, P]], channel_multiplier=channel)

            nc.gpsimd.memset(ones[:], 1.0).then_inc(consts, 1)
            own.then(nc.gpsimd.memset(ident[:], 0.0))
            tri(ident[:], 1.0, ALU.not_equal, 0, -1, 1).then_inc(consts, 1)
            nc.gpsimd.iota(dist[:, 0:128], pattern=[[-1, 128]], base=0, channel_multiplier=1,
                           allow_small_or_imprecise_dtypes=True).then_inc(consts, 1)
            nc.gpsimd.iota(dist[:, 128:384], pattern=[[-1, 256]], base=P, channel_multiplier=1,
                           allow_small_or_imprecise_dtypes=True).then_inc(consts, 1)
            nc.gpsimd.iota(iota[:], pattern=[[1, CAP]], base=1, channel_multiplier=0,
                           allow_small_or_imprecise_dtypes=True).then_inc(consts, 1)
            nc.gpsimd.memset(neg_ones, -1.0).then_inc(consts, 1)
            own.then(nc.gpsimd.memset(neg_tri, -1.0))
            tri(neg_tri, 0.0, ALU.is_ge, 0, -1, 1).then_inc(consts, 1)
            own.then(nc.gpsimd.memset(before[:], 1.0))
            tri(before[:], 0.0, ALU.is_gt, 0, 1, -1).then_inc(consts, 1)

            def causal(m):
                v = m.rearrange("p (a n) -> p a n", a=3)[:, 0:3:2, :]
                return nc.gpsimd.affine_select(out=v, in_=v, compare_op=ALU.is_gt, fill=0.0, base=0,
                                               pattern=[[0, 2], [1, P]], channel_multiplier=-1)

            for s in range(SBH + 2):
                if s < SBH:
                    pool.wait_ge(splus_ready, s + 1)
                    causal(sb_l[:, s % 3, :]).then_inc(splus_masked, 1)
                if s >= 2:
                    pool.wait_ge(sbw_ready, s - 1)
                    causal(sb_a[:, (s - 2) % 3, :]).then_inc(sbw_masked, 1)

        @block.scalar
        def _(act):
            own = Order(act, act_own)
            A = nc.scalar.activation
            for row, a, b in ((R_LQ, lam_q1, lam_q2), (R_LK, lam_k1, lam_k2)):
                act.dma_start(xn[row:row + 1, 0, 0:DH], a[0:1, :]).then_inc(small_in, 16)
                act.dma_start(xn[row:row + 1, 0, DH:P], b[0:1, :]).then_inc(small_in, 16)
            act.dma_start(xres[:, :, :], x[0, :, :].rearrange("(t p) n -> p t n", p=P)).then_inc(x_in, 16)

            act.wait_ge(x_in, 16)
            for tt in range(TT):
                A(hT[:, 4 * tt:4 * tt + 4, :], xres[:, tt, :].rearrange("p (k t) -> p k t", k=4), ACT.Square,
                  accum_out=stat[:, tt:tt + 1]).then_inc(sq_done, 1)
            act.wait_ge(ms_ready, 1)
            A(stat[:, 4:6], stat[:, 2:4], ACT.Sqrt).then_inc(root_ready, 1)
            act.wait_ge(lam_done, 1)
            for n in range(2):
                A(lam[:, n:n + 1], bank[(7, 4)[n]][:, 256:257], ACT.Exp).then_inc(lam_exp, 1)
            def copy_rows(g):
                act.wait_ge(filled, 2 * (POS["ada", g] + 1))
                if g:
                    act.wait_ge(cols_done, g)
                A(rows, bank[5][:, :], ACT.Copy).then_inc(rows_ready, 1)

            for g in range(ADA_1):
                copy_rows(g)
            act.wait_ge(xT_done, 4)
            act.wait_ge(mod_ready, 1)
            for kt in range(KT):
                A(hT[:, kt, :], bank[kt // 2][:, (kt % 2) * T:(kt % 2 + 1) * T], ACT.Identity,
                  scale=a1[:, kt:kt + 1], bias=mod[:, M_SH1 + kt:M_SH1 + kt + 1]).then_inc(emptied, 1)

            def empty(g, h, turn):
                act.wait_ge(filled, 2 * POS["in", g] + h + 1)
                branch, n = g // 6, g % 6
                src, scale = bank[turn % 2][:, :], 1.0
                if g >= 12:
                    b = 4 * (g % 2) + 2 * h
                    dst = gateT[:, (g - 12) // 2, b:b + 2, :].rearrange("p k t -> p (k t)")
                elif g in VALUES:
                    dst = v_sb[:, branch, h, (n - 4) * CW:(n - 3) * CW]
                else:
                    dst = qkT[:, branch, 4 * n + 2 * h:4 * n + 2 * h + 2, :].rearrange("p b t -> p (b t)")
                    scale = DH ** -0.5 if n < 2 else 1.0
                A(dst, src, ACT.Copy, scale=scale).then_inc(emptied, 1)

            def differential(s):
                if s < DAH:
                    for m in range(2):
                        for t in range(TT):
                            act.wait_ge(max_ready, 4 * s + 2 * m + t + 1)
                            span = slice(0, 128) if t == 0 else slice(128, 384)
                            A(da_s[:, s % 2, m, span], da_s[:, s % 2, m, span], ACT.Exp,
                              bias=smax[:, s % 2, 2 * m + t:2 * m + t + 1],
                              accum_out=ssum[:, s % 2, 2 * m + t:2 * m + t + 1]).then_inc(exp_ready, 1)
                if s >= 2:
                    h = s - 2
                    act.wait_ge(wT_done, h + 1)
                    if h >= 2:
                        act.wait_ge(pv_done, h - 1)
                    A(da_wT[:, h % 2, :], bank[6][:, 0:384], ACT.Copy).then_inc(wT_ready, 1)

            for g in range(12):
                for h in range(2):
                    empty(g, h, 2 * g + h)
                    s = 2 * (g - 6) + h
                    if 0 <= s < DAH + 2:
                        differential(s)
                if g >= ADA_1:
                    copy_rows(g)
            act.wait_ge(ms_ready, 2)
            A(osq[:], osq[:], ACT.Sqrt).then_inc(root_ready, 1)

            for s in range(24):
                if s % 2 == 1 and s < 16:
                    empty(12 + s // 4, (s // 2) % 2, turn_gate(s // 2))
                elif s % 2 == 1:
                    half, h = (s - 16) // 4, (s // 2) % 2
                    act.wait_ge(filled, 2 * POS["pa", half] + h + 1)
                    b = 4 * half + 2 * h
                    A(mergedT[:, b:b + 2, :].rearrange("p k t -> p (k t)"), bank[turn_pa(s // 2 - 8) % 2][:, :], ACT.Copy
                      ).then_inc(emptied, 1)
                if s in (7, 9, 11, 13):
                    n = (s - 7) // 2
                    act.wait_ge(oaT_done, n + 1)
                    A(oaT[:, 2 * n:2 * n + 2, :].rearrange("p k t -> p (k t)"), bank[turn_oaT(n) % 2][:, :], ACT.Copy,
                      scale=nsub[:, 0:1]).then_inc(emptied, 1)
                if s == 19:
                    for n in range(2):
                        act.wait_ge(g1b_done, n + 1)
                        A(g1b[:, n * 512:(n + 1) * 512], bank[turn_g1b(n) % 2][:, :], ACT.Copy).then_inc(emptied, 1)
                if s < SBH:
                    act.wait_ge(absz_ready, s + 1)
                    own.then(A(sb_t[:, s % 2, :], sb_t[:, s % 2, :], ACT.Exp))
                    A(sb_t[:, s % 2, :], sb_t[:, s % 2, :], ACT.Ln, bias=1.0).then_inc(ln_ready, 1)
                if 2 <= s < SBH + 2:
                    h = s - 2
                    act.wait_ge(logw_done, h + 1)
                    if h >= 3:
                        act.wait_ge(sbpv_done, h - 2)
                    A(sb_a[:, h % 3, :], bank[2 + h % 4][:, 0:384], ACT.Exp).then_inc(sbw_ready, 1)
                if s == SBH + 2:
                    act.wait_ge(emptied, EMPTIED_HT + turn_gate(7) + 1)
                    for i in range(2):
                        A(gateT[:, i, :, :], gateT[:, i, :, :], ACT.Sigmoid).then_inc(sigmoid_ready, 1)
            act.wait_ge(g2b_done, 1)
            A(g2b, bank[TURN_G2B % 2][:, :], ACT.Copy).then_inc(emptied, 1)
            for tt in range(TT):
                act.wait_ge(xT_done, 5 + 2 * tt)
                A(x1T[:, 0:4, tt * P:(tt + 1) * P], bank[(2, 0)[tt]][:, :].rearrange("p (k t) -> p k t", k=4), ACT.Copy
                  ).then_inc(x1T_low, 1)
                act.wait_ge(x1_ready, 2 * tt + 2)
                A(xn[:, tt, :], xres[:, tt, :], ACT.Square, accum_out=stat[:, tt:tt + 1]).then_inc(sq_done, 1)
                act.wait_ge(ms_ready, 3 + tt)
                A(stat[:, 4 + tt:5 + tt], stat[:, 2 + tt:3 + tt], ACT.Sqrt).then_inc(root_ready, 1)
            for tt in range(TT):
                act.wait_ge(top_ready, tt + 1)
                A(r_b[:, tt, :], lg[:, tt, :], ACT.Exp, bias=small[:, tt:tt + 1]).then_inc(gexp_ready, 1)
            def copy_back(item):
                act.wait_ge(back_done, item + 2)
                A(back[0:64, 0, :], bank[5][0:64, 0:T], ACT.Copy)
                A(back[64:128, 1, :], bank[5][64:128, 0:T], ACT.Copy).then_inc(back_ready, 1)

            def copy_taken(item):
                act.wait_ge(taken_done, item + 1)
                A(x_raw, bank[4][:, :], ACT.Copy).then_inc(xraw_ready, 1)

            def expert(item):
                act.wait_ge(g_done, item + 1)
                A(g_raw, bank[0][:, :], ACT.Copy).then_inc(raw_ready, 1)
                act.wait_ge(gu_used, item * 8 + 8)
                A(u_raw, bank[1][:, :], ACT.Copy).then_inc(raw_ready, 1)
                act.wait_ge(gmin_ready, item + 1)
                A(sig, g_sb, ACT.Sigmoid, scale=ALPHA).then_inc(sig_ready, 1)
                copy_back(item)
                copy_taken(item + 1)

            def further(b, k):
                act.wait_ge(f_taken, k + 1)
                A(x_raw, bank[4][:, :], ACT.Copy).then_inc(f_xraw, 1)
                act.wait_ge(f_gu_done, k + 1)
                A(g_raw, bank[0][:, :], ACT.Copy)
                A(u_raw, bank[1][:, :], ACT.Copy).then_inc(f_raw, 1)
                act.wait_ge(f_gmin, k + 1)
                A(sig, g_sb, ACT.Sigmoid, scale=ALPHA).then_inc(f_sig, 1)
                act.wait_ge(f_back_done, k + 1)
                act.wait_ge(f_act, k + 1)
                A(f_back[0:64, 0, :], bank[5][0:64, 0:T], ACT.Copy)
                A(f_back[64:128, 1, :], bank[5][64:128, 0:T], ACT.Copy).then_inc(f_back_ready, 1)

            copy_taken(0)
            copy_back(-1)
            act.wait_ge(passes_ready, 1)
            with act.Fori(0, PAIRS) as n:
                for half in range(2):
                    further_passes(act, n * 2 + half, further)
                    expert(n * 2 + half)

            A(small[:, 0:1], stat[:, 4:5], ACT.Sqrt)
            for tt in range(TT):
                act.wait_ge(given_added, NE * 4 + 2 * tt + 2)
                A(xn[:, 1, :] if tt else scratch[:, 0:D], xres[:, tt, :], ACT.Square, accum_out=stat[:, tt:tt + 1]
                  ).then_inc(sq_done, 1)
                act.wait_ge(ms_ready, 5 + tt)
                A(stat[:, 4 + tt:5 + tt], stat[:, 2 + tt:3 + tt], ACT.Sqrt).then_inc(root_ready, 1)

        @block.vector
        def _(dve):
            own = Order(dve, dve_own)
            V = nc.vector

            def root_mean(n, tiles_done):
                dve.wait_ge(sq_done, 2 * tiles_done)
                V.tensor_scalar(stat[:, 2:4], stat[:, 0:2], 1.0 / D, EPS, ALU.mult, ALU.add).then_inc(ms_ready, 1)
                dve.wait_ge(root_ready, n)
                own.then(V.reciprocal(stat[:, 6:8], stat[:, 4:6]))

            dve.wait_ge(vecT_done, 1)
            V.tensor_copy(vec[:], bank[7][:, 0:R_END]).then_inc(vec_ready, 1)
            dve.wait_ge(vec_ready, 1)
            V.tensor_tensor(lam[:, 3:4], vec[:, R_LQ:R_LQ + 1], vec[:, R_LK:R_LK + 1], ALU.mult).then_inc(vec_ready, 1)
            V.tensor_scalar(nsub[:], vec[:, R_SUB:R_SUB + 1], 1.0 - LAM_INIT, None, ALU.mult).then_inc(vec_ready, 1)
            V.tensor_copy(c_cols, vec[:, R_C:R_C + KT].unsqueeze(2).to_broadcast([P, KT, 32])).then_inc(vec_ready, 1)
            dve.wait_ge(consts, 2)
            V.tensor_reduce(first_of[:], ident[:, 0:P:32], AX.X, ALU.add).then_inc(vec_ready, 1)
            root_mean(1, 1)
            dve.wait_ge(vecT_done, 1)
            for tt in range(TT):
                V.tensor_scalar(xn[:, tt, :], xres[:, tt, :], stat[:, 6 + tt:7 + tt], None, ALU.mult
                                ).then_inc(xn_ready, 1)
            dve.wait_ge(lam_exp, 2)
            own.then(V.tensor_tensor(lam[:, 2:3], lam[:, 1:2], lam[:, 0:1], ALU.subtract))
            own.then(V.tensor_scalar(lam[:, 2:3], lam[:, 2:3], -LAM_INIT, None, ALU.add))
            dve.wait_ge(consts, 4)
            own.then(V.scalar_tensor_tensor(dist[:], dist[:], -1.0, dist[:], op0=ALU.mult, op1=ALU.max))
            V.memset(dist[0:64, 64:128], FAR)
            own.then(V.memset(dist[0:64, 128 + 192:384], FAR))
            dve.wait_ge(cols_done, ADA_1)
            own.then(V.tensor_tensor(mod[:, 0:16], bank[7][:, 0:16], vec[:, R_ADA:R_ADA + 16], ALU.add))
            V.scalar_tensor_tensor(a1[:], mod[:, M_SC1:M_SC1 + 8], 1.0, vec[:, R_N1:R_N1 + 8],
                                   op0=ALU.add, op1=ALU.mult).then_inc(mod_ready, 1)
            dve.wait_ge(bgu_done, 1)
            V.tensor_copy(bgu[:].rearrange("p e r -> p (e r)"), bank[6][:, :]).then_inc(vec_ready, 1)

            SPAN = [slice(0, 128), slice(128, 384)]
            for s in range(DAH + 3):
                if s < DAH:
                    b = s % 2
                    for m in range(2):
                        dve.wait_ge(scores_done, 2 * s + m + 1)
                        if s >= 2 and m == 0:
                            dve.wait_ge(w_ready, s - 1)
                        V.scalar_tensor_tensor(da_s[:, b, m, :], dist[:], -(2.0 ** (-8.0 * (s + 1) / DAH)),
                                               bank[2 + m][:, 0:384], op0=ALU.mult, op1=ALU.add
                                               ).then_inc(scores_ready, 1)
                        dve.wait_ge(scores_ready, 2 * s + m + 1)
                        for t in range(TT):
                            V.tensor_reduce(smax[:, b, 2 * m + t:2 * m + t + 1], da_s[:, b, m, SPAN[t]], AX.X,
                                            ALU.max, negate=True).then_inc(max_ready, 1)
                if 1 <= s <= DAH:
                    h, b = s - 1, (s - 1) % 2
                    dve.wait_ge(exp_ready, 4 * h + 4)
                    own.then(V.reciprocal(srec[:, b, :], ssum[:, b, :]))
                    own.then(V.tensor_scalar(srec[:, b, 2:4], srec[:, b, 2:4], lam[:, 2:3], None, ALU.mult))
                    for t in range(TT):
                        V.tensor_scalar(da_s[:, b, 0, SPAN[t]], da_s[:, b, 0, SPAN[t]], srec[:, b, t:t + 1], None,
                                        ALU.mult).then_inc(dve_own, 1)
                        own.steps += 1
                    dve.wait_ge(dve_own, own.base + own.steps)
                    if h >= 2:
                        dve.wait_ge(wT_done, h - 1)
                    for t in range(TT):
                        last = V.scalar_tensor_tensor(da_w[:, b, SPAN[t]], da_s[:, b, 1, SPAN[t]],
                                                      srec[:, b, 2 + t:3 + t], da_s[:, b, 0, SPAN[t]],
                                                      op0=ALU.mult, op1=ALU.add)
                        if t == 0:
                            last.then_inc(dve_own, 1)
                            own.steps += 1
                    last.then_inc(w_ready, 1)
                if s >= 3:
                    h = s - 3
                    dve.wait_ge(pv_done, h + 1)
                    V.tensor_copy(oa[:, :, h * P:(h + 1) * P],
                                  bank[4][:, 0:256].rearrange("p (t n) -> p t n", t=TT)).then_inc(pv_read, 1)
            dve.wait_ge(pv_read, DAH)
            oav = oa.rearrange("p t (h n) -> p (t h) n", n=P)
            sqv = xn[:, :, :].rearrange("p t (h n) -> p (t h) n", n=P)
            dve.wait_ge(xT_done, 4)
            own.then(V.tensor_tensor(sqv, oav, oav, ALU.mult))
            own.then(V.tensor_reduce(osq[:], sqv, AX.X, ALU.add))
            V.tensor_scalar(osq[:], osq[:], 1.0 / (2 * DH), EPS, ALU.mult, ALU.add).then_inc(ms_ready, 1)

            def minus_abs(h):
                z, l = bank[2 + h % 4][:, 0:384], sb_l[:, h % 3, :]
                dve.wait_ge(z_done, h + 1)
                if h >= 3:
                    dve.wait_ge(logw_done, h - 2)
                own.then(V.tensor_scalar(l, z, 0.0, None, ALU.max))
                V.scalar_tensor_tensor(sb_t[:, h % 2, :], l, -2.0, z, op0=ALU.mult, op1=ALU.add
                                       ).then_inc(absz_ready, 1)

            def softplus(h):
                dve.wait_ge(ln_ready, h + 1)
                V.tensor_tensor(sb_l[:, h % 3, :], sb_l[:, h % 3, :], sb_t[:, h % 2, :], ALU.add
                                ).then_inc(splus_ready, 1)

            dve.wait_ge(cols_done, ADA)
            own.then(V.tensor_tensor(mod[:, 16:48], bank[7][:, 16:48], vec[:, R_ADA + 16:R_ADA + 48], ALU.add))
            V.scalar_tensor_tensor(a2[:], mod[:, M_SC2:M_SC2 + 8], 1.0, vec[:, R_N2:R_N2 + 8],
                                   op0=ALU.add, op1=ALU.mult).then_inc(mod_ready, 1)
            minus_abs(0)
            dve.wait_ge(root_ready, 2)
            own.then(V.reciprocal(osq[:], osq[:]))
            V.tensor_tensor(oav, oav, osq[:].unsqueeze(2).to_broadcast([P, 16, P]), ALU.mult).then_inc(oa_ready, 1)
            for s in range(1, SBH + 5):
                if s == SBH + 1:
                    dve.wait_ge(filled, 2 * POS["in", 15] + 2)
                    for kt in range(KT):
                        V.tensor_scalar(g1diag[:, kt, :], ident[:], mod[:, M_G1 + kt:M_G1 + kt + 1], None, ALU.mult
                                        ).then_inc(diag_ready, 1)
                if s < SBH:
                    if s >= 2:
                        dve.wait_ge(splus_ready, s - 1)
                    minus_abs(s)
                if s - 1 < SBH:
                    softplus(s - 1)
                if s >= 5 and (s - 5) % 2 == 0 and (s - 5) // 2 < SBH // 2:
                    pair = (s - 5) // 2
                    dve.wait_ge(sbpv_done, 2 * pair + 2)
                    V.tensor_copy(obT[:, pair, :], bank[6 + pair % 2][:, 0:T]).then_inc(obT_ready, 1)

            dve.wait_ge(g1b_done, 2)
            for kt in range(KT):
                V.tensor_scalar(g1diag[:, kt, :], ident[:], mod[:, M_G2 + kt:M_G2 + kt + 1], None, ALU.mult
                                ).then_inc(diag_ready, 1)
            dve.wait_ge(router_in, 32)
            def over_experts(columns):
                return columns.unsqueeze(2).to_broadcast([P, KT, NE])
            own.then(V.tensor_tensor(shifted, rw_sb[:], over_experts(mod[:, M_SH2:M_SH2 + KT]), ALU.mult))
            V.tensor_tensor(rw_sb[:], rw_sb[:], over_experts(a2[:, :]), ALU.mult).then_inc(rw_ready, 1)
            for part_ in (slice(32, 64), slice(96, 128)):
                V.memset(y_sb[part_, :], 0.0)
            V.memset(back[64:128, 0, :], 0.0)
            V.memset(back[0:64, 1, :], 0.0)
            dve.wait_ge(sigmoid_ready, 2)
            for half in range(2):
                dve.wait_ge(emptied, EMPTIED_HT + turn_pa(2 * half + 1) + 1)
                own.then(V.tensor_tensor(mergedT[:, 4 * half:4 * half + 4, :], mergedT[:, 4 * half:4 * half + 4, :],
                                         gateT[:, 0, 4 * half:4 * half + 4, :], ALU.mult))
            for n in range(4):
                blk = slice(2 * n, 2 * n + 2)
                dst = mergedT[:, blk, :].rearrange("p k t -> p (k t)")
                dve.wait_ge(filled, 2 * POS["pb", 0] + n + 1)
                own.then(V.tensor_tensor(tmp[:, n % 2, :], bank[2 + n][:, :],
                                         gateT[:, 1, blk, :].rearrange("p k t -> p (k t)"), ALU.mult))
                V.tensor_tensor(dst, dst, tmp[:, n % 2, :], ALU.add).then_inc(merged_ready, 1)
            dve.wait_ge(merged_ready, 4)
            dve.wait_ge(shift_done, 1)
            own.then(V.tensor_reduce(shift[:], bank[1][:, 0:KT * NE].rearrange("p (k e) -> p e k", k=KT), AX.X, ALU.add))
            V.tensor_tensor(shift[:], shift[:], bank[1][:, KT * NE:(KT + 1) * NE], ALU.add).then_inc(shift_ready, 1)
            dve.wait_ge(shift_ready, 1)

            def route(tt):
                dve.wait_ge(logits_done, tt + 1)
                own.then(V.scalar_tensor_tensor(lg[:, tt, :], bank[4 + tt][:, 0:NE], stat[:, 6 + tt:7 + tt], shift[:],
                                                op0=ALU.mult, op1=ALU.add))
                own.then(V.max(top8[:, tt, :], lg[:, tt, :]))
                V.tensor_scalar(small[:, tt:tt + 1], top8[:, tt, 0:1], -1.0, None, ALU.mult).then_inc(top_ready, 1)
                fourth = top8[:, tt, TOPK - 1:TOPK]
                own.then(V.tensor_scalar(sel[:, tt, :], lg[:, tt, :], fourth, None, ALU.is_gt))
                own.then(V.tensor_reduce(small[:, 2 + tt:3 + tt], sel[:, tt, :], AX.X, ALU.add))
                own.then(V.tensor_scalar(r_a[:, tt, :], lg[:, tt, :], fourth, None, ALU.is_equal))
                own.then(V.tensor_tensor_scan(r1[:, tt, 0:NE], r_a[:, tt, :], ones[:, 0:NE],
                                              small[:, 2 + tt:3 + tt], op0=ALU.add, op1=ALU.mult))
                own.then(V.scalar_tensor_tensor(r_a[:, tt, :], r1[:, tt, 0:NE], TOPK + 0.5, r_a[:, tt, :],
                                                op0=ALU.is_lt, op1=ALU.mult))
                V.tensor_tensor(sel[:, tt, :], sel[:, tt, :], r_a[:, tt, :], ALU.add).then_inc(sel_ready, 1)
                dve.wait_ge(sel_ready, tt + 1)

            def add_mixed(n):
                tt, cols = n // 2, slice((n % 2) * 512, (n % 2 + 1) * 512)
                dve.wait_ge(mixed_done, n + 1)
                if n >= 2:
                    dve.wait_ge(x1_ready, n - 1)
                own.then(V.tensor_tensor(tmp[:, n % 2, :], bank[(0, 1, 6, 7)[n]][:, :], g1b[:, cols], ALU.mult))
                V.tensor_tensor(xres[:, tt, cols], xres[:, tt, cols], tmp[:, n % 2, :], ALU.add).then_inc(x1_ready, 1)

            add_mixed(0)
            add_mixed(1)
            for tt in range(TT):
                dve.wait_ge(xT_done, 6 + 2 * tt)
                V.tensor_copy(x1T[:, 4:8, tt * P:(tt + 1) * P], bank[(3, 1)[tt]][:, :].rearrange("p (k t) -> p k t", k=4)
                              ).then_inc(x1T_high, 1)
                dve.wait_ge(sq_done, 3 + tt)
                V.tensor_scalar(stat[:, 2 + tt:3 + tt], stat[:, tt:tt + 1], 1.0 / D, EPS, ALU.mult, ALU.add
                                ).then_inc(ms_ready, 1)
                dve.wait_ge(root_ready, 3 + tt)
                own.then(V.reciprocal(stat[:, 6 + tt:7 + tt], stat[:, 4 + tt:5 + tt]))
                V.tensor_scalar(xn[:, tt, :], xres[:, tt, :], stat[:, 6 + tt:7 + tt], None, ALU.mult
                                ).then_inc(xn_ready, 1)
                if tt == 0:
                    add_mixed(2)
                route(tt)
                if tt == 0:
                    add_mixed(3)
            dve.wait_ge(gexp_ready, 2)
            own.then(V.tensor_tensor(r_b[:], r_b[:], sel[:], ALU.mult))
            own.then(V.tensor_reduce(small[:, 4:6], r_b[:], AX.X, ALU.add))
            own.then(V.reciprocal(small[:, 6:8], small[:, 4:6]))
            V.tensor_tensor(gates[:, :, 0:NE], r_b[:], small[:, 6:8].unsqueeze(2).to_broadcast([P, TT, NE]), ALU.mult
                            ).then_inc(gates_ready, 1)
            dve.wait_ge(rank_done, 1)
            own.then(V.memset(r1[:], 0.0))
            own.then(V.scalar_tensor_tensor(r1[:, :, 0:NE], bank[1][:, 0:TT * NE].rearrange("p (t e) -> p t e", t=TT),
                                            1.0, sel[:], op0=ALU.add, op1=ALU.mult))
            dve.wait_ge(gates_ready, 1)

            def pick(item):
                for tt in range(TT):
                    last = V.tensor_scalar(onehot[:, tt, :], iota[:], r1[:, tt, bass.ds(item, 1)], None, ALU.is_equal)
                    if tt == 0:
                        own.then(last)
                last.then_inc(onehot_ready, 1)

            pick(0)
            own.then(V.memset(gated[:], 0.0))
            own.then(V.tensor_copy(gated[:, :, 0, 0:NE], gates[:, :, 0:NE]))
            V.tensor_copy(gated[:, :, 1, 0:NE], gates[:, :, 0:NE]).then_inc(gated_ready, 1)

            dve.wait_ge(counts_done, 1)
            for k in range(BLOCKS - 1):
                own.then(V.tensor_scalar(over[:, k:k + 1], bank[2][0:NE, 0:1], float(CAP * (k + 1)), None, ALU.is_gt))
            V.tensor_reduce(over[:, 3:4], over[:, 0:3], AX.X, ALU.add).then_inc(over_ready, 1)

            def take(item):
                dve.wait_ge(takenT_done, item + 1)
                own.then(V.tensor_tensor(xT, blocks(6), wide(a2[:, :]), ALU.mult))
                V.tensor_tensor(xT, xT, wide(mod[:, M_SH2:M_SH2 + 8]), ALU.add).then_inc(xTe_ready, 1)

            def blocks(b):
                return bank[b][:, :].rearrange("p (j a s) -> p j a s", j=4, a=2)

            def wide(t):
                return t.rearrange("p (a j) -> p j a", a=2).unsqueeze(3).to_broadcast([P, 4, 2, CAP])

            dve.wait_ge(passes_done, 1)
            own.then(V.tensor_copy(passes_f[:].rearrange("p a e -> p (a e)"), bank[3][0:1, 0:2 * NE]))
            V.tensor_copy(passes[:], passes_f[:]).then_inc(passes_ready, 1)
            take(0)
            dve.wait_ge(bdown_in, 32)
            dve.wait_ge(emptied, EMPTIED_HT + TURN_G2B + 1)
            V.tensor_tensor(y_sb, y_sb, g2b, ALU.mult).then_inc(y_ready, 1)

            def add_given(item):
                for n in range(4):
                    tt, half = n // 2, n % 2
                    cols = slice(half * 512, (half + 1) * 512)
                    dve.wait_ge(given_done, item * 4 + (n + 5))
                    V.tensor_tensor(xres[:, tt, cols], xres[:, tt, cols], bank[4 + n][:, :], ALU.add
                                    ).then_inc(given_added, 1)

            def expert(item):
                bias = bgu[:, bass.ds(item, 1), :].rearrange("p e r -> p (e r)")
                dve.wait_ge(back_ready, item + 1)
                for tt in range(TT):
                    for a in range(2):
                        last = V.tensor_scalar(gated[:, tt, a, :], iota[:], r1[:, tt, bass.ds(item, 1)],
                                               gates[:, tt, bass.ds(item, 1)], ALU.is_equal, ALU.mult)
                        if 2 * tt + a < 3:
                            own.then(last)
                last.then_inc(gated_ready, 1)
                pick(item + 1)
                add_given(item - 1)
                dve.wait_ge(gT_done, item + 1)
                own.then(V.tensor_tensor(g_sb, blocks(2), wide(bias[:, 0:8]), ALU.add))
                V.tensor_scalar(g_sb, g_sb, LIMIT, None, ALU.min).then_inc(gmin_ready, 1)
                dve.wait_ge(gmin_ready, item + 1)
                dve.wait_ge(sig_ready, item + 1)
                own.then(V.tensor_tensor(sig, sig, g_sb, ALU.mult))
                dve.wait_ge(uT_done, item + 1)
                own.then(V.tensor_tensor(u_sb, blocks(3), wide(bias[:, 8:16]), ALU.add))
                own.then(V.tensor_scalar(u_sb, u_sb, LIMIT, -LIMIT, ALU.min, ALU.max))
                V.scalar_tensor_tensor(act_sb, u_sb, 1.0, sig, op0=ALU.add, op1=ALU.mult).then_inc(act_ready, 1)
                take(item + 1)
                dve.wait_ge(down_used, item * 4 + 4)
                V.tensor_tensor(y_sb, bank[7][:, :], g2b, ALU.mult).then_inc(y_ready, 1)

            further_own = Order(dve, f_own)
            FURTHER = 1 + 3 + 1 + 1 + 1 + 1 + 1

            def further(expert, b, k):
                f = further_own
                dve.wait_ge(f_mark, k + 1)
                f.start_at(k * FURTHER)
                bias = bgu[:, bass.ds(expert, 1), :].rearrange("p e r -> p (e r)")
                for tt in range(TT):
                    last = V.tensor_scalar(onehot[:, tt, :], iota[:], float(CAP * b), r1[:, tt, bass.ds(expert, 1)],
                                           ALU.add, ALU.is_equal)
                    if tt == 0:
                        f.then(last)
                last.then_inc(f_onehot, 1)
                dve.wait_ge(f_onehot, k + 1)
                dve.wait_ge(back_ready, expert + 1)
                for tt in range(TT):
                    for a in range(2):
                        last = V.tensor_scalar(gated[:, tt, a, :], onehot[:, tt, :], gates[:, tt, bass.ds(expert, 1)],
                                               None, ALU.mult)
                        if 2 * tt + a < 3:
                            f.then(last)
                last.then_inc(f_gated, 1)
                dve.wait_ge(f_takenT, k + 1)
                f.then(V.tensor_tensor(f_xT, blocks(6), wide(a2[:, :]), ALU.mult))
                V.tensor_tensor(f_xT, f_xT, wide(mod[:, M_SH2:M_SH2 + 8]), ALU.add).then_inc(f_xT_ready, 1)
                dve.wait_ge(f_guT_done, k + 1)
                f.then(V.tensor_tensor(g_sb, blocks(2), wide(bias[:, 0:8]), ALU.add))
                V.tensor_scalar(g_sb, g_sb, LIMIT, None, ALU.min).then_inc(f_gmin, 1)
                V.memset(f_back[64:128, 0, :], 0.0)
                V.memset(f_back[0:64, 1, :], 0.0)
                f.then(V.tensor_tensor(u_sb, blocks(3), wide(bias[:, 8:16]), ALU.add))
                f.then(V.tensor_scalar(u_sb, u_sb, LIMIT, -LIMIT, ALU.min, ALU.max))
                dve.wait_ge(f_gmin, k + 1)
                dve.wait_ge(f_sig, k + 1)
                f.then(V.tensor_tensor(sig, sig, g_sb, ALU.mult))
                V.scalar_tensor_tensor(act_sb, u_sb, 1.0, sig, op0=ALU.add, op1=ALU.mult).then_inc(f_act, 1)
                assert f.steps == FURTHER
                dve.wait_ge(f_down_done, k + 1)
                V.tensor_tensor(f_y, bank[7][:, :], g2b, ALU.mult).then_inc(f_y_ready, 1)
                for n in range(4):
                    tt, half = n // 2, n % 2
                    cols = slice(half * 512, (half + 1) * 512)
                    dve.wait_ge(f_given, k * 4 + (n + 1))
                    V.tensor_tensor(xres[:, tt, cols], xres[:, tt, cols], bank[4 + n][:, :], ALU.add).then_inc(f_added, 1)
                dve.wait_ge(f_added, k * 4 + 4)
                V.memset(small[:, 7:8], 0.0).then_inc(f_mark, 1)

            PER = 3 + 1 + 1 + 2 + 1 + 1
            start = own.steps
            dve.wait_ge(passes_ready, 1)
            V.memset(small[:, 7:8], 0.0).then_inc(f_mark, 1)
            with dve.Fori(0, PAIRS) as n:
                for half in range(2):
                    own.start_at(n * (2 * PER) + (start + PER * half))
                    further_passes(dve, n * 2 + half, lambda b, k: further(n * 2 + half, b, k))
                    expert(n * 2 + half)
                    assert own.steps == PER
            add_given(NE - 1)

            dve.wait_ge(fg_in, 16)
            for tt in range(TT):
                dve.wait_ge(sq_done, 5 + tt)
                V.tensor_scalar(stat[:, 2 + tt:3 + tt], stat[:, tt:tt + 1], 1.0 / D, EPS, ALU.mult, ALU.add
                                ).then_inc(ms_ready, 1)
                dve.wait_ge(root_ready, 5 + tt)
                V.reciprocal(stat[:, 6 + tt:7 + tt], stat[:, 4 + tt:5 + tt]).then_inc(rec_ready, 1)
                dve.wait_ge(rec_ready, tt + 1)
                V.scalar_tensor_tensor(xres[:, tt, :], xres[:, tt, :], stat[:, 6 + tt:7 + tt], fgb,
                                       op0=ALU.mult, op1=ALU.mult).then_inc(out_ready, 1)

        @block.tensor
        def _(pe):
            M = nc.tensor.matmul

            pe.wait_ge(consts, 2)
            pe.wait_ge(small_in, 9 * 16)
            nc.tensor.transpose(bank[7][:, 0:R_END], vt, ident[0:R_END, 0:R_END]).then_inc(vecT_done, 1)
            pe.wait_ge(vec_ready, 2)
            for n in range(2):
                last = M(bank[(7, 4)[n]][:, 256:257], ones[64 * n:64 * n + 64, :], lam[64 * n:64 * n + 64, 3:4],
                         start=True, stop=True)
            last.then_inc(lam_done, 1)

            pe.wait_ge(xn_ready, 2)
            for kt in range(KT):
                for tt in range(TT):
                    last = nc.tensor.transpose(bank[kt // 2][:, (kt % 2) * T + tt * P:(kt % 2) * T + (tt + 1) * P],
                                               xn[:, tt, kt * P:(kt + 1) * P], ident[:])
                if kt % 2:
                    last.then_inc(xT_done, 1)

            def ada_rows(g):
                for h in range(2):
                    wait_group(pe, POS["ada", g], h)
                if g:
                    pe.wait_ge(rows_ready, g)
                for kt in range(KT):
                    q = kt % 4
                    last = M(bank[5][32 * q:32 * q + 32, :], c_cols[:, kt, :],
                             group_chunk(POS["ada", g], kt // 4)[:, q, :], start=kt < 4, stop=kt >= 4,
                             skip_group_check=True)
                last.then_inc(filled, 2)

            def ada_columns(g):
                pe.wait_ge(rows_ready, g + 1)
                for blk in range(4):
                    last = M(bank[7][:, 4 * g + blk:4 * g + blk + 1], rows[:, blk * P:(blk + 1) * P], first_of[:],
                             start=True, stop=True)
                last.then_inc(cols_done, 1)

            pe.wait_ge(vec_ready, 5)
            pe.wait_ge(lam_exp, 2)
            for g in range(ADA_1):
                ada_rows(g)
                ada_columns(g)

            def take_turn(turn):
                pe.wait_ge(emptied, EMPTIED_HT + max(0, turn - 1))
                return bank[turn % 2]

            def project(g, h, b, turn):
                group = POS["in", g]
                dst = bank[turn % 2]
                if b == 0:
                    if turn:
                        take_turn(turn)
                    for n in range(2):
                        wait_group(pe, group, n)
                if g in VALUES:
                    for kt in range(KT) if b == 0 else ():
                        last = M(dst[:, :], hT[:, kt, h * P:(h + 1) * P], group_chunk(group, kt // 4)[:, kt % 4, :],
                                 start=kt == 0, stop=kt == KT - 1)
                        if kt == KT - 1:
                            last.then_inc(filled, 1)
                    return
                cols = slice((2 * h + b) * P, (2 * h + b + 1) * P)
                for kt in range(KT):
                    if turn == 0 and b == 0:
                        pe.wait_ge(emptied, max(2, kt + 1))
                    last = M(dst[:, b * T:(b + 1) * T], group_chunk(group, kt // 4)[:, kt % 4, cols],
                             hT[:, kt, :], start=kt == 0, stop=kt == KT - 1)
                if b:
                    last.then_inc(filled, 1)

            def differential(s):
                if s < DAH:
                    part, blk = slice(64 * (s % 2), 64 * (s % 2) + 64), s // 2
                    if s >= 1:
                        pe.wait_ge(scores_ready, 2 * s)
                    for m in range(2):
                        q = qkT[part, 0, 4 * m + blk, :]
                        k = qkT[part, 0, 8 + 4 * m + blk, :]
                        dst = bank[2 + m]
                        M(dst[:, 0:128], q[:, 0:P], k[:, 0:P], start=True, stop=True)
                        M(dst[:, 128:384], q[:, P:T], k, start=True, stop=True).then_inc(scores_done, 1)
                if 2 <= s < DAH + 2:
                    h = s - 2
                    pe.wait_ge(w_ready, h + 1)
                    if h >= 1:
                        pe.wait_ge(wT_ready, h)
                    for n in range(3):
                        last = nc.tensor.transpose(bank[6][:, n * P:(n + 1) * P], da_w[:, h % 2, n * P:(n + 1) * P], ident[:])
                    last.then_inc(wT_done, 1)
                if s >= 3:
                    h = s - 3
                    pe.wait_ge(wT_ready, h + 1)
                    if h >= 1:
                        pe.wait_ge(pv_read, h)
                    dst, wt = bank[4], da_wT[:, h % 2, :]
                    cols = slice(h * P, (h + 1) * P)
                    M(dst[:, 0:128], wt[:, 0:P], v_sb[:, 0, 0, cols], start=True, stop=True)
                    M(dst[:, 128:256], wt[:, P:2 * P], v_sb[:, 0, 0, cols], start=True, stop=False)
                    M(dst[:, 128:256], wt[:, 2 * P:3 * P], v_sb[:, 0, 1, cols], start=False, stop=True).then_inc(pv_done, 1)

            for g in range(12):
                for h in range(2):
                    for b in range(2):
                        project(g, h, b, 2 * g + h)
                    s = 2 * (g - 6) + h
                    if 0 <= s < DAH + 3:
                        differential(s)
                    if h == 0 and g > ADA_1:
                        ada_columns(g - 1)
                if g >= ADA_1:
                    ada_rows(g)
                if g == 1:
                    pe.wait_ge(bgu_in, 16)
                    for a in range(4):
                        last = nc.tensor.transpose(bank[6][:, a * P:(a + 1) * P], bgu_rows[:, a, :], ident[:])
                    last.then_inc(bgu_done, 1)

            def stick_breaking(s):
                if s < SBH:
                    part, blk = slice(64 * (s % 2), 64 * (s % 2) + 64), s // 2
                    if s == 0:
                        pe.wait_ge(scores_ready, 2 * DAH)
                    if s == 2:
                        pe.wait_ge(pv_read, DAH)
                    if s == 3:
                        pe.wait_ge(rows_ready, ADA)
                    if s >= 4:
                        pe.wait_ge(sbw_ready, s - 3)
                    q, k = qkT[part, 1, blk, :], qkT[part, 1, 8 + blk, :]
                    z = bank[2 + s % 4]
                    M(z[:, 0:256], k[:, 0:P], q, start=True, stop=False, skip_group_check=True)
                    M(z[:, 256:384], k[:, P:T], q[:, P:T], start=False, stop=False, skip_group_check=True
                      ).then_inc(z_done, 1)
                if 2 <= s < SBH + 2:
                    h = s - 2
                    z, l = bank[2 + h % 4], sb_l[:, h % 3, :]
                    pe.wait_ge(splus_masked, h + 1)
                    M(z[:, 0:256], neg_tri, l[:, 0:256], start=False, stop=False, skip_group_check=True)
                    M(z[:, 128:256], neg_ones, l[:, 256:384], start=False, stop=False, skip_group_check=True)
                    M(z[:, 256:384], neg_tri, l[:, 256:384], start=False, stop=True, skip_group_check=True
                      ).then_inc(logw_done, 1)
                if 4 <= s:
                    h = s - 4
                    pe.wait_ge(sbw_masked, h + 1)
                    if h == 0:
                        pe.wait_ge(wT_ready, DAH)
                    if h == 2:
                        pe.wait_ge(mod_ready, 2)
                    if h >= 4 and h % 2 == 0:
                        pe.wait_ge(obT_ready, h // 2 - 1)
                    dst = bank[6 + (h // 2) % 2][64 * (h % 2):64 * (h % 2) + 64, :]
                    a, cols = sb_a[:, h % 3, :], slice(h * DH, (h + 1) * DH)
                    M(dst[:, 0:256], v_sb[:, 1, 0, cols], a[:, 0:256], start=True, stop=False, skip_group_check=True)
                    M(dst[:, 128:256], v_sb[:, 1, 1, cols], a[:, 256:384], start=False, stop=True, skip_group_check=True
                      ).then_inc(sbpv_done, 1)

            def branch_block(group, h, b, src, dst):
                for kt in range(KT):
                    last = M(dst[:, b * T:(b + 1) * T], group_chunk(group, kt // 4)[:, kt % 4, (2 * h + b) * P:(2 * h + b + 1) * P],
                             src[:, kt, :], start=kt == 0, stop=kt == KT - 1)
                if b:
                    last.then_inc(filled, 1)

            for s in range(24):
                half, b = s // 2, s % 2
                if s in (8, 10, 12, 14):
                    n = (s - 8) // 2
                    pe.wait_ge(oa_ready, 1)
                    dst = take_turn(turn_oaT(n))
                    for j in range(4):
                        kt, tt = 2 * n + j // 2, j % 2
                        last = nc.tensor.transpose(dst[:, j * P:(j + 1) * P], oa[:, tt, kt * P:(kt + 1) * P], ident[:])
                    last.then_inc(oaT_done, 1)
                if s == 20:
                    for n in range(2):
                        pe.wait_ge(diag_ready, 4 * n + 4)
                        M(take_turn(turn_g1b(n))[:, :], ones[:], g1diag[:, 4 * n:4 * n + 4, :].rearrange("p k n -> p (k n)"),
                          start=True, stop=True).then_inc(g1b_done, 1)
                if half < 8:
                    project(12 + half // 2, half % 2, b, turn_gate(half))
                else:
                    group, turn = POS["pa", (half - 8) // 2], turn_pa(half - 8)
                    if b == 0:
                        take_turn(turn)
                        for h in range(2):
                            wait_group(pe, group, h)
                    branch_block(group, half % 2, b, oaT, bank[turn % 2])
                if s == 0:
                    ada_columns(ADA - 1)
                if s < SBH + 4:
                    stick_breaking(s)

            pe.wait_ge(obT_ready, SBH // 2)
            for half in range(2):
                group = POS["pb", half]
                for h in range(2):
                    wait_group(pe, group, h)
                for n in range(4):
                    branch_block(group, n // 2, n % 2, obT, bank[2 + 2 * half + n // 2])
                if half == 0:
                    pe.wait_ge(diag_ready, 2 * KT)
                    dst = take_turn(TURN_G2B)
                    for a in range(2):
                        last = M(dst[64 * a:64 * a + 64, :], ones[:, 0:64],
                                 g1diag[:, 4 * a:4 * a + 4, :].rearrange("p k n -> p (k n)"), start=True, stop=True)
                    last.then_inc(g2b_done, 1)
                    pe.wait_ge(rw_ready, 1)
                    dst = take_turn(TURN_G2B + 1)
                    M(dst[:, 0:KT * NE], ones[:], shifted.rearrange("p k e -> p (k e)"), start=True, stop=True)
                    M(dst[:, KT * NE:(KT + 1) * NE], ones[0:1, :], rb_sb[:], start=True, stop=True).then_inc(shift_done, 1)

            def mix(tt, half, kts):
                dst = bank[(0, 1, 6, 7)[2 * tt + half]]
                for kt in kts:
                    last = M(dst[:, :], mergedT[:, kt, tt * P:(tt + 1) * P],
                             group_chunk(POS["o", half], kt // 4)[:, kt % 4, :], start=kt == 0, stop=kt == KT - 1,
                             skip_group_check=True)
                return last

            def transpose_x1(tt, half, b):
                pe.wait_ge(x1_ready, 2 * tt + half + 1)
                for n in range(4):
                    last = nc.tensor.transpose(bank[b + half][:, n * P:(n + 1) * P],
                                               xres[:, tt, (4 * half + n) * P:(4 * half + n + 1) * P], ident[:])
                last.then_inc(xT_done, 1)

            def logits(tt):
                pe.wait_ge(x1T_low, tt + 1)
                pe.wait_ge(x1T_high, tt + 1)
                for kt in range(KT):
                    last = M(bank[4 + tt][:, 0:NE], x1T[:, kt, tt * P:(tt + 1) * P], rw_sb[:, kt, :], start=kt == 0,
                             stop=kt == KT - 1, skip_group_check=True)
                last.then_inc(logits_done, 1)

            take_turn(TURN_G2B + 2)
            for half in range(2):
                for h in range(2):
                    wait_group(pe, POS["o", half], h)
            for n in range(4):
                pe.wait_ge(merged_ready, n + 1)
                last = mix(0, 0, (2 * n, 2 * n + 1))
            last.then_inc(mixed_done, 1)
            pe.wait_ge(shift_ready, 1)
            mix(0, 1, range(KT)).then_inc(mixed_done, 1)
            mix(1, 0, range(KT)).then_inc(mixed_done, 1)
            for half in range(2):
                transpose_x1(0, half, 2)
            mix(1, 1, range(4)).then_inc(filled, 2)
            logits(0)
            transpose_x1(1, 0, 0)
            mix(1, 1, range(4, KT)).then_inc(mixed_done, 1)
            transpose_x1(1, 1, 0)
            logits(1)
            pe.wait_ge(sel_ready, 2)
            M(bank[1][:, 0:NE], before[:], sel[:, 0, :], start=True, stop=True)
            M(bank[1][:, NE:2 * NE], ones[:], sel[:, 0, :], start=True, stop=False)
            M(bank[1][:, NE:2 * NE], before[:], sel[:, 1, :], start=False, stop=True).then_inc(rank_done, 1)

            def take(item, tiles=range(TT)):
                pe.wait_ge(onehot_ready, item + 1)
                for tt in tiles:
                    for a in range(2):
                        last = M(bank[4][64 * a:64 * a + 64, :], onehot[:, tt, :], xn[:, tt, a * 512:(a + 1) * 512],
                                 start=tt == 0, stop=tt == TT - 1, skip_group_check=True)
                if tiles[-1] == TT - 1:
                    last.then_inc(taken_done, 1)

            def transposes(b, src):
                for j in range(4):
                    last = nc.tensor.transpose(bank[b][:, j * P:(j + 1) * P], src[:, j * P:(j + 1) * P], ident[:])
                return last

            def take_transposed(item):
                pe.wait_ge(xraw_ready, item + 1)
                transposes(6, x_raw).then_inc(takenT_done, 1)

            def way_back(item):
                pe.wait_ge(gated_ready, item + 2)
                for tt in range(TT):
                    last = nc.tensor.transpose(bank[5][:, tt * P:(tt + 1) * P],
                                               gated[:, tt, :, :].rearrange("p a s -> p (a s)"), ident[:])
                last.then_inc(back_done, 1)

            def give(item):
                pe.wait_ge(y_ready, item + 2)
                pe.wait_ge(back_ready, item + 2)
                for n in range(4):
                    tt, a = n // 2, n % 2
                    M(bank[4 + n][:, :], back[:, a, tt * P:(tt + 1) * P], y_sb, start=True, stop=True
                      ).then_inc(given_done, 1)

            def expert(item, half, fills):
                pe.wait_ge(xTe_ready, item + 1)

                def gate_up(kt, parts):
                    for f in parts:
                        a = f % 2
                        last = M(bank[f // 2][64 * a:64 * a + 64, :], xT[:, kt % 4, kt // 4, :],
                                 gu_ring[:, 8 * half + kt, f * 512:(f + 1) * 512],
                                 start=kt == 0, stop=kt == KT - 1, skip_group_check=True)
                    if f == 3:
                        last.then_inc(gu_used, 1)
                    elif kt == KT - 1:
                        last.then_inc(g_done, 1)

                for kt in range(KT):
                    pe.wait_ge(slot_in[8 * half + kt], fills * 16 + 16 * USES[8 * half + kt])
                    if kt < KT - 2:
                        gate_up(kt, range(4))
                    else:
                        gate_up(kt, (0, 1))
                    if kt == 1:
                        give(item - 1)
                gate_up(KT - 2, (2, 3))
                pe.wait_ge(raw_ready, item * 2 + 1)
                transposes(2, g_raw).then_inc(gT_done, 1)
                gate_up(KT - 1, (2, 3))
                pe.wait_ge(given_added, item * 4 + 4)
                way_back(item)
                take(item + 1, (0,))
                pe.wait_ge(raw_ready, item * 2 + 2)
                transposes(3, u_raw).then_inc(uT_done, 1)
                take(item + 1, (1,))
                take_transposed(item + 1)
                pe.wait_ge(act_ready, item + 1)
                for kt in range(KT):
                    if kt % 2 == 0:
                        pe.wait_ge(down_in[kt // 2], item * 16 + 16)
                    for a in range(2):
                        last = M(bank[7][64 * a:64 * a + 64, :], act_sb[:, kt % 4, kt // 4, :],
                                 down_ring[:, kt // 2, (kt % 2) * D + a * 512:(kt % 2) * D + (a + 1) * 512],
                                 start=kt == 0, stop=kt == KT - 1, skip_group_check=True)
                    if kt % 2 == 1:
                        last.then_inc(down_used, 1)

            def further(expert, half, fills, k):
                pe.wait_ge(xTe_ready, expert + 1)
                pe.wait_ge(y_ready, expert + 1)
                pe.wait_ge(back_ready, expert + 1)
                pe.wait_ge(f_onehot, k + 1)
                for tt in range(TT):
                    for a in range(2):
                        last = M(bank[4][64 * a:64 * a + 64, :], onehot[:, tt, :], xn[:, tt, a * 512:(a + 1) * 512],
                                 start=tt == 0, stop=tt == TT - 1, skip_group_check=True)
                last.then_inc(f_taken, 1)
                pe.wait_ge(f_xraw, k + 1)
                transposes(6, x_raw).then_inc(f_takenT, 1)
                pe.wait_ge(f_xT_ready, k + 1)
                for kt in range(KT):
                    pe.wait_ge(slot_in[8 * half + kt], fills * 16 + 16 * USES[8 * half + kt])
                    for f in range(4):
                        a = f % 2
                        last = M(bank[f // 2][64 * a:64 * a + 64, :], f_xT[:, kt % 4, kt // 4, :],
                                 gu_ring[:, 8 * half + kt, f * 512:(f + 1) * 512],
                                 start=kt == 0, stop=kt == KT - 1, skip_group_check=True)
                last.then_inc(f_gu_done, 1)
                pe.wait_ge(f_raw, k + 1)
                transposes(2, g_raw)
                transposes(3, u_raw).then_inc(f_guT_done, 1)
                pe.wait_ge(f_gated, k + 1)
                for tt in range(TT):
                    last = nc.tensor.transpose(bank[5][:, tt * P:(tt + 1) * P],
                                               gated[:, tt, :, :].rearrange("p a s -> p (a s)"), ident[:])
                last.then_inc(f_back_done, 1)
                pe.wait_ge(f_act, k + 1)
                for kt in range(KT):
                    if kt % 2 == 0:
                        pe.wait_ge(down_in[kt // 2], expert * 16 + 16)
                    for a in range(2):
                        last = M(bank[7][64 * a:64 * a + 64, :], act_sb[:, kt % 4, kt // 4, :],
                                 down_ring[:, kt // 2, (kt % 2) * D + a * 512:(kt % 2) * D + (a + 1) * 512],
                                 start=kt == 0, stop=kt == KT - 1, skip_group_check=True)
                last.then_inc(f_down_done, 1)
                pe.wait_ge(f_back_ready, k + 1)
                pe.wait_ge(f_y_ready, k + 1)
                for n in range(4):
                    tt, a = n // 2, n % 2
                    M(bank[4 + n][:, :], f_back[:, a, tt * P:(tt + 1) * P], f_y, start=True, stop=True).then_inc(f_given, 1)
                pe.wait_ge(f_added, k * 4 + 4)
                nc.tensor.transpose(bank[2][:, 0:P], ident[:], ident[:])

            for tt in range(TT):
                last = M(bank[2][0:NE, 0:1], sel[:, tt, :], ones[:, 0:1], start=tt == 0, stop=tt == TT - 1)
            last.then_inc(counts_done, 1)
            take(0)
            pe.wait_ge(over_ready, 1)
            M(bank[3][0:1, 0:NE], over[:, 3:4], ident[0:NE, 0:NE], start=True, stop=True)
            M(bank[3][0:1, NE:2 * NE], over[:, 3:4], before[0:NE, 0:NE], start=True, stop=True).then_inc(passes_done, 1)
            take_transposed(0)
            way_back(-1)
            pe.wait_ge(passes_ready, 1)
            with pe.Fori(0, PAIRS) as n:
                for half in range(2):
                    further_passes(pe, n * 2 + half, lambda b, k: further(n * 2 + half, half, n + 1, k))
                    expert(n * 2 + half, half, n + 1)
            give(NE - 1)


_INS = ["x", "c", "w_ada", "b_ada", "norm1_g", "w_in", "lam_q1", "lam_k1", "lam_q2", "lam_k2", "subln_g", "w_pa", "w_pb",
        "w_o", "norm2_g", "router_w", "router_b", "w_gu", "b_gu", "w_down", "b_down", "final_g"]


def kernel(**inputs):
    import concourse.bacc as bacc
    from concourse.bass_utils import run_bass_kernel_spmd

    nc = bacc.Bacc("TRN2", target_bir_lowering=False, num_devices=1)
    arrays, args = {}, []
    for name in _INS:
        a = np.ascontiguousarray(inputs[name])
        arrays[f"in_{name}"] = a
        args.append(nc.dram_tensor(f"in_{name}", a.shape, mybir.dt.from_np(a.dtype), kind="ExternalInput").ap())
    args.append(nc.dram_tensor("out", (1, T, D), F32, kind="ExternalOutput").ap())
    build(nc, *args)
    return run_bass_kernel_spmd(nc, [arrays], core_ids=[0]).results[0]["out"]
```
